# Optimizing a Trainium2 kernel written in Bass

```python
import functools
import jax, jax.numpy as jnp
from jax import lax
import numpy as np

D_MODEL = 1024
BATCH = 1
SEQ = 512
DEPTH = 1
DEC_BATCH = 8
DEC_SEQ = 4
PAST_LEN = 512
PAGE_SIZE = 128

MIX_WIDTH = D_MODEL
HG_HEADS = 4
HG_DIM = (MIX_WIDTH // 2) // HG_HEADS
HG_WIDTH = HG_HEADS * HG_DIM
HG_CHUNK = 32
MB_HEADS = 8
MB_DIM = (MIX_WIDTH - HG_WIDTH) // MB_HEADS
MB_WIDTH = MB_HEADS * MB_DIM
MB_BLOCK = 256
MB_TOPK = 3
MB_QBLK = 64
IN_WIDTHS = (HG_WIDTH, HG_WIDTH, HG_WIDTH, HG_WIDTH, MB_WIDTH, MB_WIDTH, MB_WIDTH)
IN_PROJ = sum(IN_WIDTHS)
MEM_LEN = 256
XA_HEADS = 4
XA_DIM = D_MODEL // XA_HEADS
N_GROUPS = 4
EXP_PER_GROUP = 8
N_EXPERTS = N_GROUPS * EXP_PER_GROUP
EXP_TOPK = 2
D_EXPERT = D_MODEL
MOE_BLK = 128
RMS_EPS = 1e-6

kernel_name = 'hymba_hgrn2_moba_hmoe_step'

def _rmsnorm(x, g):
    xf = x.astype(jnp.float32)
    y = xf * lax.rsqrt(jnp.mean(xf * xf, axis=-1, keepdims=True) + RMS_EPS)
    return (y * g.astype(jnp.float32)).astype(x.dtype)

def _alibi_slopes(n):
    return np.power(2.0, -8.0 * np.arange(1, n + 1) / n).astype(np.float32)

def _hgrn2_chunked(q, k, logf, v, s0):
    B, T, H, K = q.shape
    c = min(HG_CHUNK, T)
    n = -(-T // c)
    pad = n * c - T

    def prep(a):
        a = jnp.pad(a.astype(jnp.float32), ((0, 0), (0, pad), (0, 0), (0, 0)))
        return jnp.moveaxis(a.reshape(B, n, c, H, a.shape[-1]), 1, 0)

    tri = jnp.tril(jnp.ones((c, c), bool))[None, :, :, None, None]

    def step(S, blk):
        qc, kc, lc, vc = blk
        b = jnp.cumsum(lc, axis=1)
        decay = jnp.exp(jnp.where(tri, b[:, :, None] - b[:, None, :], -jnp.inf))
        att = jnp.einsum('bthk,bshk,btshk->bhts', qc, kc, decay)
        o = (jnp.einsum('bhts,bshv->bthv', att, vc)
             + jnp.einsum('bthk,bhkv->bthv', qc * jnp.exp(b), S))
        bl = b[:, -1]
        S = (jnp.exp(bl)[..., None] * S
             + jnp.einsum('bshk,bshv->bhkv', kc * jnp.exp(bl[:, None] - b), vc))
        return S, o

    S, o = lax.scan(step, s0.astype(jnp.float32), (prep(q), prep(k), prep(logf), prep(v)))
    o = jnp.moveaxis(o, 0, 1).reshape(B, n * c, H, v.shape[-1])[:, :T]
    return o, S

def _moba_seq(q, k, v, p0):
    T = q.shape[0]
    L = k.shape[0]
    nb = -(-L // MB_BLOCK)
    padk = nb * MB_BLOCK - L
    kb = jnp.pad(k, ((0, padk), (0, 0), (0, 0))).astype(jnp.float32).reshape(nb, MB_BLOCK, MB_HEADS, MB_DIM)
    vb = jnp.pad(v, ((0, padk), (0, 0), (0, 0))).astype(jnp.float32).reshape(nb, MB_BLOCK, MB_HEADS, MB_DIM)
    kb_h = jnp.moveaxis(kb, 2, 0)
    vb_h = jnp.moveaxis(vb, 2, 0)
    kmean = jnp.mean(kb, axis=1)
    kk = max(1, min(MB_TOPK, nb - 1))
    qb = min(MB_QBLK, T)
    nq = -(-T // qb)
    padq = nq * qb - T
    qp = jnp.pad(q.astype(jnp.float32), ((0, padq), (0, 0), (0, 0))).reshape(nq, qb, MB_HEADS, MB_DIM)
    pos = (p0 + jnp.minimum(jnp.arange(nq * qb), T - 1)).reshape(nq, qb)
    slopes = jnp.asarray(_alibi_slopes(MB_HEADS))
    heads = jnp.arange(MB_HEADS)[:, None, None]
    offs = jnp.arange(MB_BLOCK)
    blk_ids = jnp.arange(nb)
    scale = MB_DIM ** -0.5

    def qstep(args):
        qq, pp = args
        blk = pp // MB_BLOCK
        gate = jnp.einsum('qhd,nhd->hqn', qq, kmean)
        gate = jnp.where(blk_ids[None, None, :] < blk[None, :, None], gate, -jnp.inf)
        _, sel = lax.top_k(gate, kk)
        valid = sel < blk[None, :, None]
        ksel = kb_h[heads, sel]
        vsel = vb_h[heads, sel]
        dist_sel = (pp[None, :, None, None] - (sel[..., None] * MB_BLOCK + offs)).astype(jnp.float32)
        s_sel = jnp.einsum('qhd,hqjsd->hqjs', qq, ksel) * scale - slopes[:, None, None, None] * dist_sel
        s_sel = jnp.where(valid[..., None], s_sel, -jnp.inf).reshape(MB_HEADS, qb, kk * MB_BLOCK)
        kown = kb[blk]
        vown = vb[blk]
        kpos = blk[:, None] * MB_BLOCK + offs
        dist_own = (pp[:, None] - kpos).astype(jnp.float32)
        s_own = jnp.einsum('qhd,qshd->hqs', qq, kown) * scale - slopes[:, None, None] * dist_own[None]
        s_own = jnp.where((kpos <= pp[:, None])[None], s_own, -jnp.inf)
        p = jax.nn.softmax(jnp.concatenate([s_sel, s_own], axis=-1), axis=-1)
        o = (jnp.einsum('hqs,hqsd->qhd', p[..., :kk * MB_BLOCK],
                        vsel.reshape(MB_HEADS, qb, kk * MB_BLOCK, MB_DIM))
             + jnp.einsum('hqs,qshd->qhd', p[..., kk * MB_BLOCK:], vown))
        return o

    o = lax.map(qstep, (qp, pos))
    return o.reshape(nq * qb, MB_HEADS, MB_DIM)[:T].astype(q.dtype)

def _moba_prompt(q, k, v):
    return lax.map(lambda a: _moba_seq(a[0], a[1], a[2], 0), (q, k, v))

def _moba_sample(q, k, v, pool_k, pool_v, page_table):
    def one(a):
        qb, kn, vn, pt = a
        kp = pool_k[pt].reshape(-1, MB_HEADS, MB_DIM)
        vp = pool_v[pt].reshape(-1, MB_HEADS, MB_DIM)
        kf = jnp.concatenate([kp, kn.astype(kp.dtype)], axis=0)
        vf = jnp.concatenate([vp, vn.astype(vp.dtype)], axis=0)
        return _moba_seq(qb, kf, vf, kp.shape[0])
    return lax.map(one, (q, k, v, page_table))

def _mem_kv(mem, g_mem, w_xk, w_xv):
    B, M, _ = mem.shape
    m = _rmsnorm(mem, g_mem)
    return ((m @ w_xk).reshape(B, M, XA_HEADS, XA_DIM), (m @ w_xv).reshape(B, M, XA_HEADS, XA_DIM))

def _cross_attn(h, mk, mv, w_xq, w_xo):
    B, T, _ = h.shape
    q = (h @ w_xq).reshape(B, T, XA_HEADS, XA_DIM)
    s = jnp.einsum('bthd,bmhd->bhtm', q.astype(jnp.float32), mk.astype(jnp.float32)) * XA_DIM ** -0.5
    p = jax.nn.softmax(s, axis=-1)
    o = jnp.einsum('bhtm,bmhd->bthd', p, mv.astype(jnp.float32)).astype(h.dtype)
    return o.reshape(B, T, D_MODEL) @ w_xo

def _grouped_experts(x, eid, gates, w1, w3, w2):
    n, d = x.shape
    a = n * EXP_TOPK
    flat_e = eid.reshape(-1)
    flat_t = jnp.arange(a) // EXP_TOPK
    flat_g = gates.reshape(-1).astype(jnp.float32)
    order = jnp.argsort(flat_e)
    se = flat_e[order]
    counts = jnp.bincount(flat_e, length=N_EXPERTS)
    padc = ((counts + MOE_BLK - 1) // MOE_BLK) * MOE_BLK
    start = jnp.cumsum(counts) - counts
    pend = jnp.cumsum(padc)
    pstart = pend - padc
    dest = pstart[se] + jnp.arange(a) - start[se]
    rows = -(-(a + N_EXPERTS * (MOE_BLK - 1)) // MOE_BLK) * MOE_BLK
    nblk = rows // MOE_BLK
    row_tok = jnp.full((rows,), n, jnp.int32).at[dest].set(flat_t[order].astype(jnp.int32))
    row_g = jnp.zeros((rows,), jnp.float32).at[dest].set(flat_g[order])
    blk_e = jnp.minimum(jnp.searchsorted(pend, jnp.arange(nblk) * MOE_BLK, side='right'), N_EXPERTS - 1)
    xs = jnp.concatenate([x, jnp.zeros((1, d), x.dtype)], axis=0)[row_tok].reshape(nblk, MOE_BLK, d)

    def expert(args):
        xb, e = args
        hmid = jax.nn.silu(xb @ w1[e]) * (xb @ w3[e])
        return hmid @ w2[e]

    outs = lax.map(expert, (xs, blk_e)).reshape(rows, d).astype(jnp.float32)
    y = jnp.zeros((n + 1, d), jnp.float32).at[row_tok].add(outs * row_g[:, None])[:n]
    return y.astype(x.dtype)

def _hmoe(h, w_grp, b_grp, w_exp, b_exp, w1, w3, w2):
    B, T, D = h.shape
    x = h.reshape(B * T, D)
    n = x.shape[0]
    glog = (x @ w_grp).astype(jnp.float32) + b_grp.astype(jnp.float32)
    gw, gsel = lax.top_k(jax.nn.softmax(glog, axis=-1), 1)
    gw, gsel = gw[:, 0], gsel[:, 0]
    elog = ((x @ w_exp).astype(jnp.float32) + b_exp.astype(jnp.float32)).reshape(n, N_GROUPS, EXP_PER_GROUP)
    eprob = jax.nn.softmax(elog[jnp.arange(n), gsel], axis=-1)
    ew, esel = lax.top_k(eprob, EXP_TOPK)
    gates = gw[:, None] * ew / jnp.sum(ew, axis=-1, keepdims=True)
    eid = gsel[:, None] * EXP_PER_GROUP + esel
    return _grouped_experts(x, eid, gates, w1, w3, w2).reshape(B, T, D)

def _layer(x, s0, moba_fn, mem_k, mem_v, g_mix, w_in, lb, hg_norm, w_out, g_cross, w_xq, w_xo,
           g_ffn, w_grp, b_grp, w_exp, b_exp, w1, w3, w2):
    B, T, _ = x.shape
    h = _rmsnorm(x, g_mix)
    proj = h @ w_in
    offs = np.cumsum((0,) + IN_WIDTHS)
    hq, hf, hi, hg, mq, mk, mv = [proj[..., int(offs[j]):int(offs[j + 1])] for j in range(len(IN_WIDTHS))]
    q = jax.nn.silu(hq).reshape(B, T, HG_HEADS, HG_DIM)
    f = lb + (1.0 - lb) * jax.nn.sigmoid(hf.astype(jnp.float32))
    logf = jnp.log(f).reshape(B, T, HG_HEADS, HG_DIM)
    kh = (1.0 - f).reshape(B, T, HG_HEADS, HG_DIM)
    o, s_new = _hgrn2_chunked(q, kh, logf, hi.reshape(B, T, HG_HEADS, HG_DIM), s0)
    o = _rmsnorm(o, hg_norm) * jax.nn.silu(hg.reshape(B, T, HG_HEADS, HG_DIM).astype(jnp.float32))
    mk4 = mk.reshape(B, T, MB_HEADS, MB_DIM)
    mv4 = mv.reshape(B, T, MB_HEADS, MB_DIM)
    att = moba_fn(mq.reshape(B, T, MB_HEADS, MB_DIM), mk4, mv4)
    mix = jnp.concatenate([o.reshape(B, T, HG_WIDTH).astype(x.dtype),
                           att.reshape(B, T, MB_WIDTH).astype(x.dtype)], axis=-1) @ w_out
    x = x + mix
    x = x + _cross_attn(_rmsnorm(x, g_cross), mem_k, mem_v, w_xq, w_xo)
    x = x + _hmoe(_rmsnorm(x, g_ffn), w_grp, b_grp, w_exp, b_exp, w1, w3, w2)
    return x, s_new, mk4, mv4

def setup_inputs(seed: int = 0) -> dict:
    key = jax.random.key(seed)
    ks = jax.random.split(key, 32)
    f32 = jnp.float32
    n_pages = PAST_LEN // PAGE_SIZE
    used = DEC_BATCH * n_pages
    n_phys = used + max(1, used // 4)

    def nrm(i, shape, scale=1.0):
        return jax.random.normal(ks[i], shape, f32) * scale

    def gain(i, shape):
        return 1.0 + 0.02 * jax.random.normal(ks[i], shape, f32)

    page_table = jax.random.permutation(ks[7], n_phys)[:used].reshape(DEC_BATCH, n_pages).astype(jnp.int32)
    return {
        'x_prompt': nrm(0, (BATCH, SEQ, D_MODEL)),
        'x_sample': nrm(1, (DEC_BATCH, DEC_SEQ, D_MODEL)),
        'state_hgrn': nrm(2, (DEPTH, DEC_BATCH, HG_HEADS, HG_DIM, HG_DIM), 0.5),
        'cache_moba_k': nrm(3, (DEPTH, n_phys, PAGE_SIZE, MB_HEADS, MB_DIM)),
        'cache_moba_v': nrm(4, (DEPTH, n_phys, PAGE_SIZE, MB_HEADS, MB_DIM)),
        'cache_mem_k': nrm(5, (DEPTH, DEC_BATCH, MEM_LEN, XA_HEADS, XA_DIM)),
        'cache_mem_v': nrm(6, (DEPTH, DEC_BATCH, MEM_LEN, XA_HEADS, XA_DIM)),
        'page_table': page_table,
        'mem_prompt': nrm(8, (BATCH, MEM_LEN, D_MODEL)),
        'g_mix': gain(9, (DEPTH, D_MODEL)),
        'w_in': nrm(10, (DEPTH, D_MODEL, IN_PROJ), D_MODEL ** -0.5),
        'hg_lb': nrm(11, (DEPTH + 1, HG_WIDTH), 0.5),
        'hg_norm': gain(12, (DEPTH, HG_DIM)),
        'w_out': nrm(13, (DEPTH, MIX_WIDTH, D_MODEL), MIX_WIDTH ** -0.5),
        'g_cross': gain(14, (DEPTH, D_MODEL)),
        'g_mem': gain(15, (DEPTH, D_MODEL)),
        'w_xq': nrm(16, (DEPTH, D_MODEL, D_MODEL), D_MODEL ** -0.5),
        'w_xk': nrm(17, (DEPTH, D_MODEL, D_MODEL), D_MODEL ** -0.5),
        'w_xv': nrm(18, (DEPTH, D_MODEL, D_MODEL), D_MODEL ** -0.5),
        'w_xo': nrm(19, (DEPTH, D_MODEL, D_MODEL), D_MODEL ** -0.5),
        'g_ffn': gain(20, (DEPTH, D_MODEL)),
        'w_grp': nrm(21, (DEPTH, D_MODEL, N_GROUPS), D_MODEL ** -0.5),
        'b_grp': nrm(22, (DEPTH, N_GROUPS), 0.01),
        'w_exp': nrm(23, (DEPTH, D_MODEL, N_EXPERTS), D_MODEL ** -0.5),
        'b_exp': nrm(24, (DEPTH, N_EXPERTS), 0.01),
        'w1': nrm(25, (DEPTH, N_EXPERTS, D_MODEL, D_EXPERT), D_MODEL ** -0.5),
        'w3': nrm(26, (DEPTH, N_EXPERTS, D_MODEL, D_EXPERT), D_MODEL ** -0.5),
        'w2': nrm(27, (DEPTH, N_EXPERTS, D_EXPERT, D_MODEL), D_EXPERT ** -0.5),
        'g_final': gain(28, (D_MODEL,)),
    }

def reference(x_prompt, x_sample, state_hgrn, cache_moba_k, cache_moba_v, cache_mem_k, cache_mem_v,
              page_table, mem_prompt, g_mix, w_in, hg_lb, hg_norm, w_out, g_cross, g_mem, w_xq, w_xk,
              w_xv, w_xo, g_ffn, w_grp, b_grp, w_exp, b_exp, w1, w3, w2, g_final):
    lbs = jnp.cumsum(jax.nn.softmax(hg_lb.astype(jnp.float32), axis=0), axis=0)
    xp, xs = x_prompt, x_sample
    sp_l, kp_l, vp_l, mk_l, mv_l, ss_l, ks_l, vs_l = [], [], [], [], [], [], [], []
    for l in range(DEPTH):
        lw = (g_mix[l], w_in[l], lbs[l], hg_norm[l], w_out[l], g_cross[l], w_xq[l], w_xo[l], g_ffn[l],
              w_grp[l], b_grp[l], w_exp[l], b_exp[l], w1[l], w3[l], w2[l])
        mkp, mvp = _mem_kv(mem_prompt, g_mem[l], w_xk[l], w_xv[l])
        s0 = jnp.zeros((xp.shape[0], HG_HEADS, HG_DIM, HG_DIM), jnp.float32)
        xp, sp, kp, vp = _layer(xp, s0, _moba_prompt, mkp, mvp, *lw)
        moba_s = functools.partial(_moba_sample, pool_k=cache_moba_k[l], pool_v=cache_moba_v[l],
                                   page_table=page_table)
        xs, ss, ks_, vs_ = _layer(xs, state_hgrn[l], moba_s, cache_mem_k[l], cache_mem_v[l], *lw)
        sp_l.append(sp); kp_l.append(kp); vp_l.append(vp); mk_l.append(mkp); mv_l.append(mvp)
        ss_l.append(ss); ks_l.append(ks_); vs_l.append(vs_)
    y_prompt = _rmsnorm(xp, g_final)
    y_sample = _rmsnorm(xs, g_final)
    return (y_prompt, y_sample,
            jnp.stack(sp_l).astype(x_prompt.dtype), jnp.stack(kp_l), jnp.stack(vp_l),
            jnp.stack(mk_l), jnp.stack(mv_l),
            jnp.stack(ss_l).astype(state_hgrn.dtype), jnp.stack(ks_l), jnp.stack(vs_l))


_drawn_inputs = setup_inputs


def setup_inputs(seed=0):
    import zlib

    import numpy as np

    out = dict(_drawn_inputs(seed))
    spreads = {}
    factors = {'g_cross': 8.0, 'g_mem': 2.854, 'b_grp': 15.006, 'b_exp': 9.492, 'g_final': 7.44}
    for name, (base, spread) in spreads.items():
        noise = np.random.default_rng([zlib.crc32(name.encode()), seed]).standard_normal(out[name].shape)
        drawn = base * np.exp(spread * noise) if base else spread * noise
        out[name] = __import__('jax').numpy.asarray(drawn.astype(out[name].dtype))
    for name, factor in factors.items():
        out[name] = (out[name] * factor).astype(out[name].dtype)
    return out
```

```python
from contextlib import ExitStack

import numpy as np

import concourse.bass as bass
from concourse import mybir

F32 = mybir.dt.float32
U32 = mybir.dt.uint32
I32 = mybir.dt.int32
ACT = mybir.ActivationFunctionType
ALU = mybir.AluOpType
AX = mybir.AxisListType.X

P = 128
D = 1024
KC = D // P
SEQ = 512
NT = SEQ // P
NB, NQ = 8, 4
NS = NB * NQ
TOK = SEQ + NS
TILES = [(i, P) for i in range(NT)] + [(NT, NS)]
HG, HD = 4, 128
CH, SUB = 32, 8
NCH = SEQ // CH
MB, MD = 8, 64
PAGE, NPG, NPHYS = 128, 4, 40
PAST = NPG * PAGE
XH, XD, MEM = 4, 256, 256
MT = MEM // P
NG, EPG = 4, 8
NE = NG * EPG
CAP = 64
XBLK = 16
NBLK = NE + XBLK
EPS = 1e-6
NEG = -1e30


def constants():
    p = np.arange(P)
    c = {}
    c["c_ident"] = np.eye(P)
    t = np.arange(SEQ)
    tt = t % P
    c["c_maskd"] = ((p[:, None] // SUB == tt[None] // SUB) & (p[:, None] <= tt[None]))
    off = np.zeros((P, 3, SEQ // CH, SUB))
    for j in range(1, CH // SUB):
        for ch in range(NCH):
            s0 = (ch % (P // CH)) * CH
            off[s0:s0 + j * SUB, j - 1, ch, :] = 1
    c["c_masko"] = off.reshape(P, 3 * SEQ // CH * SUB)
    r = np.arange(NS)
    ms = (r[:, None] // NQ == r[None] // NQ) & (r[:, None] <= r[None])
    c["c_masks"] = np.tile(ms, (1, HG))
    c["c_bsel"] = (r[:, None] // NQ == np.arange(NB)[None])
    scan = np.ones(TOK)
    scan[0:SEQ:CH] = 0
    scan[SEQ::NQ] = 0
    c["c_scan"] = np.broadcast_to(scan, (P, TOK))
    x = np.arange(SEQ + SEQ - P)[None] - p[:, None] - (SEQ - P)
    c["c_alibi"] = np.where(x <= 0, x, NEG)
    b, h, q = p // 32, (p % 32) // NQ, p % NQ
    slope = 2.0 ** (-(h + 1.0))
    sb = np.full((P, 2, PAST + NS), NEG)
    for g in range(2):
        sb[:, g, :PAST] = -slope[:, None] * (PAST + q[:, None] - np.arange(PAST)[None])
        for k in range(NS):
            ok = (k // NQ == 4 * g + b) & (k % NQ <= q)
            sb[:, g, PAST + k] = np.where(ok, -slope * (q - k % NQ), NEG)
    c["c_sbias"] = sb.reshape(P, -1)
    c["c_before"] = (p[:, None] < p[None])
    c["c_ones"] = np.ones((P, P))
    c["c_iota"] = np.broadcast_to(np.arange(P), (P, P))
    c["c_tokid"] = np.arange(5)[None] * P + p[:, None]
    c["c_steps"] = np.broadcast_to(CAP * np.arange(1, 9), (P, 8))
    return {k: np.ascontiguousarray(v, dtype=np.float32) for k, v in c.items()}


OUTS = [("y_prompt", (1, SEQ, D)), ("y_sample", (NB, NQ, D)), ("hg_prompt", (1, 1, HG, HD, HD)),
        ("mk_prompt", (1, 1, SEQ, MB, MD)), ("mv_prompt", (1, 1, SEQ, MB, MD)),
        ("xk_prompt", (1, 1, MEM, XH, XD)), ("xv_prompt", (1, 1, MEM, XH, XD)),
        ("hg_sample", (1, NB, HG, HD, HD)), ("mk_sample", (1, NB, NQ, MB, MD)),
        ("mv_sample", (1, NB, NQ, MB, MD))]

IN = {"hq": 0, "hf": 1, "hi": 2, "hg": 3, "mq": 4, "mk": 5, "mv": 6}
WBLOCKS = [("w_in", IN[n], n) for n in ("hf", "hq", "mk", "mq", "mv", "hi", "hg")] + \
          [("w_out", 0, "o0"), ("w_out", 1, "o1"), ("w_xk", 0, "xk0"), ("w_xk", 1, "xk1"),
           ("w_xv", 0, "xv0"), ("w_xv", 1, "xv1"), ("w_xq", 0, "xq0"), ("w_xq", 1, "xq1"),
           ("w_xo", 0, "xo0"), ("w_xo", 1, "xo1")]
WPOS = {n: i for i, (_, _, n) in enumerate(WBLOCKS)}


RING = 6


def plan_jobs():
    jobs = []

    def add(eng, *name):
        jobs.append((name, eng))

    def turned(what, tiles):
        for i, _ in tiles:
            add("A", what, i, 0)
            add("V", what, i, 1)

    turned("hT", TILES)
    for c in range(5):
        add("A", "hf", c)
    for c in range(5):
        add("V", "hq", c)
    for i, _ in TILES:
        add("A", "mk", i)
    for c in range(5):
        add("V", "mq", c)
    for c in range(5):
        add("A", "mkT", c)
    for i, _ in TILES:
        add("V", "mv", i)
    for i, _ in TILES:
        add("A", "hi", i)
    for i, _ in TILES:
        add("V", "hg", i)
    for h in range(HG):
        add("V", "attd", h)
        add("V", "atto", h)
        add("A", "kdn", h)
        add("A", "kds", h)
    for i in range(NT):
        for c in range(P // CH):
            add("V", "U", i * (P // CH) + c)
        add("V", "o", i)
        if i:
            add("A", "hgT", i - 1)
    add("V", "o", NT)
    add("A", "hgT", NT - 1)
    for b in range(NB):
        add("V", "Us", b)
    add("A", "hgT", NT)
    for h in range(MB + 1):
        if h < MB:
            for i in range(NT):
                add("V", "S", h, i)
        if h:
            for k in range(NT):
                add("A", "PT", h - 1, k)
            if h % 2 == 0:
                add("A", "OT", h // 2 - 1)
    for g in range(2):
        for b in range(4 * g, 4 * g + 4):
            for c in range(4):
                add("AV"[c % 2], "KT", b, c)
        add("V", "Sn", g)
        add("A", "Pt", g)
        add("V", "Ptn", g)
        add("A", "Os", g)
    for half in range(2):
        for i, _ in TILES:
            add("V", "x1", half, i)
    turned("memT", TILES[:MT])
    for n in range(4):
        for i in range(MT):
            add("AV"[i], "mem", n, i)
    for c in range(4):
        add("AV"[c % 2], "memKT", c)
    turned("h2T", TILES)
    for half in range(2):
        for c in range(5):
            add("AV"[c % 2], "xq", half, c)
    for h in range(XH + 1):
        if h < XH:
            for i in range(2):
                add("A", "XS", h, i)
        if h:
            for k in range(MT):
                add("V", "XPT", h - 1, k)
            for c in range(2):
                add("A", "XOT", h - 1, c)
    for g in range(2):
        for b in range(4 * g, 4 * g + 4):
            for c in range(4):
                add("AV"[c % 2], "XKT", b, c)
        add("A", "XPt", g)
        add("A", "XOs", g)
    for half in range(2):
        for i, _ in TILES:
            add("V", "x2", half, i)
    turned("h3T", TILES)
    for i, _ in TILES:
        add("V", "logit", i)
    add("V", "rank")
    add("V", "table")
    return jobs


class Banks:

    def __init__(self, nc, psum, sem):
        self.psum = psum
        self.jobs = plan_jobs()
        self.number, self.rank, seen = {}, {}, {"A": 0, "V": 0}
        for n, (name, eng) in enumerate(self.jobs):
            self.number[name] = n
            self.rank[name] = seen[eng]
            seen[eng] += 1
        assert len(self.number) == len(self.jobs)
        self.total = seen
        self.filled = sem("psum_filled")
        self.emptied = {"A": sem("act_emptied"), "V": sem("dve_emptied")}

    def bank(self, *name):
        return self.psum[self.number[name] % RING]

    def wait_filled(self, eng, *name):
        eng.wait_ge(self.filled, self.number[name] + 1)

    def wait_emptied(self, eng, *name):
        who = self.jobs[self.number[name]][1]
        eng.wait_ge(self.emptied[who], self.rank[name] + 1)

    def wait_free(self, pe, *name):
        n = self.number[name] - RING
        if n >= 0:
            self.wait_emptied(pe, *self.jobs[n][0])

    def fills(self, ins, *name):
        ins.then_inc(self.filled, 1)

    def empties(self, ins, *name):
        ins.then_inc(self.emptied[self.jobs[self.number[name]][1]], 1)


class Steps:

    def __init__(self, sem):
        self.sem, self.n = sem, 0

    def did(self, ins):
        ins.then_inc(self.sem, 1)
        self.n += 1
        return self.n

    def settle(self, eng):
        eng.wait_ge(self.sem, self.n)


def step_kernel(nc, a):
    with ExitStack() as ctx:
        def sb(name, shape, dt=F32):
            return ctx.enter_context(nc.sbuf_tensor(name, shape, dt))

        def sem(name):
            return ctx.enter_context(nc.semaphore(name))

        ring = sb("ring", [P, 12, 2, D])
        r_x = sb("r_x", [P, 5 * D])
        r_h = sb("r_h", [P, KC * TOK])
        r_mix = sb("r_mix", [P, KC * TOK])
        r_c = sb("r_c", [P, 16 * TOK])
        gain = sb("gain", [P, D])
        ident = sb("ident", [P, P])
        maskd = sb("maskd", [P, SEQ])
        masko = sb("masko", [P, 3 * P])
        masks = sb("masks", [NS, HG * NS])
        bsel = sb("bsel", [NS, NB])
        scan = sb("scan", [P, TOK])
        alibi = sb("alibi", [P, 2 * SEQ - P])
        sbias = sb("sbias", [P, 2, PAST + NS])
        before = sb("before", [P, P])
        ones = sb("ones", [P, P])
        iota = sb("iota", [P, P])
        tokid = sb("tokid", [P, 5])
        steps = sb("steps", [P, 8])
        lbl = sb("lbl", [P, 2, HG])
        lb = sb("lb", [P, HG])
        omlb = sb("omlb", [P, HG])
        ghn = sb("ghn", [P, HD])
        ss = sb("ss", [P, 22])
        y0 = sb("y0", [P, 22])
        nt = sb("nt", [P, 4, 22])
        hss = sb("hss", [P, 5, HG])
        hy0 = sb("hy0", [P, 5, HG])
        hnt = sb("hnt", [P, 3, HG])
        dl = sb("dl", [P, HG, NCH + NB])
        stat = sb("stat", [P, 4, 2 * NT])
        table = sb("table", [P, NBLK // 2], U32)
        zeros = sb("zeros", [P, 256])
        yidx = sb("yidx", [P, 2, 5], U32)
        ovi = sb("ovi", [1, 1 + XBLK], I32)
        gates = sb("gates", [P, 2, 5])
        psum_t = ctx.enter_context(nc.psum_tensor("psum", [P, 8, 512], F32))
        psum = [psum_t[:, n, :] for n in range(8)]
        tok_rows = nc.dram_tensor("tok_rows", [TOK, D], F32, kind="Internal").ap()
        out_rows = nc.dram_tensor("out_rows", [NBLK * CAP, D], F32, kind="Internal").ap()

        def part(buf, at, *shape):
            n = int(np.prod(shape))
            v = buf[:, at:at + n]
            if len(shape) == 1:
                return v
            names = "abcd"[:len(shape)]
            kw = {c: s for c, s in zip(names[1:], shape[1:])}
            return v.rearrange(f"p ({' '.join(names)}) -> p {' '.join(names)}", **kw)

        flat = ring[:, :, :, :].rearrange("p a b n -> p (a b n)")
        W0, KV, TAIL = 0, 8192, 16384
        wslot = [part(flat, W0 + 4096 * n, KC, 512) for n in range(2)]
        xr = part(r_x, 0, 5, D)
        hT = part(r_h, 0, KC, TOK)
        mixT = part(r_mix, 0, KC, TOK)
        hn = [part(r_c, D * n, D) for n in range(2)]
        qh = part(r_c, 0, HG, TOK)
        fk = part(r_c, 4 * TOK, HG, TOK)
        mqT = part(r_c, 8 * TOK, 4, TOK)
        mkT = part(r_c, 12 * TOK, 4, TOK)
        vh = part(flat, TAIL, 5, 512)
        gh = part(flat, TAIL + 2560, 5, 512)
        mv = part(flat, TAIL + 5120, 5, 512)
        qtmp = [part(flat, KV + 512 * n, 512) for n in range(2)]
        mkn = part(flat, KV + 1024, 5, 512)
        at = KV
        hgt = {}
        for name, n in (("lf", TOK), ("b", TOK), ("bc", TOK), ("ta", TOK), ("tb", TOK), ("qd", TOK), ("kd", TOK),
                        ("kdT", TOK), ("qo", 3 * P), ("k1", SEQ), ("k2", SEQ), ("k3", SEQ),
                        ("qx", HG * 288), ("kds", 512), ("atts", P)):
            hgt[name] = part(flat, at, n)
            at += n
        assert at <= TAIL
        kb = [hgt["k1"], hgt["k2"], hgt["k3"]]
        qx = part(flat, KV + 8 * TOK + 3 * P + 3 * SEQ, HG, 288)
        kds = hgt["kds"]
        atts = hgt["atts"]
        att = part(r_x, 0, HG, SEQ)
        state = part(r_x, 2048, 6, HG, HD)
        kdn = part(r_h, 0, NT, HG, HD)
        on = [part(gain, 512 * n, 512) for n in range(2)]
        s0 = part(r_h, 0, NB, HG, HD)
        kdx = part(r_x, 0, NB, 512)
        pb = [[part(flat, KV + 512 * (4 * n + i), SEQ) for i in range(NT)] for n in range(2)]
        pt = [part(flat, KV + 4096 + 2048 * n, NT, SEQ) for n in range(2)]
        kbuf = [part(r_x, 2048 * n, NPG, 512) for n in range(2)]
        vbuf = [part(flat, KV + 2048 * n, NPG, 512) for n in range(4)]
        kT = [part(r_h, 2048 * n, 4, PAST) for n in range(2)]
        sx = part(r_c, 0, PAST + NS)
        ptS = part(r_c, TOK, NPG, P)
        ptn = part(r_c, TOK + 512, P)
        qxm = part(r_c, 4 * TOK, 4, NB, 32)
        memx = part(flat, TAIL, MT, D)
        memT = part(flat, TAIL + 2048, KC, MEM)
        memk = part(flat, TAIL + 4096, MT, D)
        memv = part(flat, TAIL + 6144, MT, D)
        memkT = part(r_mix, 0, KC, MEM)
        qT = part(r_c, 0, KC, TOK)
        oT = part(r_c, 8 * TOK, KC, TOK)
        xp = [part(r_mix, 2048 + 1024 * n, NT, MEM) for n in range(2)]
        xpt = [part(flat, TAIL + 4096 + 1024 * n, MT, SEQ) for n in range(2)]
        xkbuf = [part(flat, TAIL + 2048 * n, MT, D) for n in range(2)]
        xvbuf = [part(flat, KV + 2048 * n, MT, D) for n in range(4)]
        xkT = [part(r_h, 2048 * n, KC, MEM) for n in range(2)]
        xsx = part(r_mix, 0, MEM)
        xptS = part(r_mix, MEM, MT, P)
        qxx = part(r_mix, 2048, KC, NB, 32)
        rt = {}
        at = 0
        for name, n in (("lg", 5 * 36), ("g8", 40), ("m8", 40), ("i8f", 5), ("ohg", 20), ("ge", 20), ("gw", 5),
                        ("pr", 5 * 32), ("se", 40), ("me", 40), ("ek", 10), ("ex", 5), ("eid", 10),
                        ("m", 2 * 5 * 32), ("ms", 5 * 32), ("cnt", 32), ("big", 32 * 8), ("ovn", 32),
                        ("ove", 32), ("ovs", 32), ("tmp", 5 * 32), ("rk", 10), ("qk", 10), ("rr", 10),
                        ("ovk", 10), ("sk", 10), ("t1", 10), ("t2", 10), ("ohs", 2 * 5 * NBLK),
                        ("ohr", 2 * 5 * CAP), ("cmp", XBLK * 32), ("exs", XBLK), ("bias", 36), ("wr", KC * 36)):
            rt[name] = part(r_mix, at, n)
            at += n
        assert at <= KC * TOK
        i8 = sb("i8", [P, 5, 8], U32)
        xg = part(r_c, 0, D)
        xT = part(r_c, 2048, KC, P)
        he = [part(r_c, 3072 + 512 * n, 512) for n in range(2)]
        h2 = [part(r_c, 4096 + 512 * n, 512) for n in range(2)]
        heT = [part(r_c, 5120 + 512 * n, 4, P) for n in range(2)]
        ys = [part(r_c, 6144 + 512 * n, 512) for n in range(2)]
        yg = [[part(r_c, D * (2 * n + k), D) for k in range(2)] for n in range(2)]
        fin = [part(r_c, D * (4 + n), D) for n in range(2)]

        J = Banks(nc, psum, sem)
        x_in = [sem(f"x{i}_in") for i in range(5)]
        gain0_in, gain_in = sem("gain0_in"), sem("gain_in")
        const_in = sem("const_in")
        page_in = sem("pages_in")
        w_in = [sem(f"wslot{n}_in") for n in range(2)]
        mem_in = sem("mem_in")
        s0_in = sem("s0_in")
        k_in = [sem(f"k{n}_in") for n in range(2)]
        v_in = sem("v_in")
        xk_in = [sem(f"xk{n}_in") for n in range(2)]
        xv_in = sem("xv_in")
        xr_in = sem("xr_in")
        rtw_in = sem("router_weights_in")
        rooted = sem("rooted")
        normed = sem("normed")
        exped = sem("exped")
        hgd, hga = sem("hg_exponents"), sem("hg_exps")
        zeroed = sem("zeroed")
        head_ready = sem("head_ready")
        o_root, o_normed = sem("o_root"), sem("o_normed")
        kdx_done = sem("kdx_done")
        s_max, s_exp, s_prob = sem("s_max"), sem("s_exp"), sem("s_prob")
        qx_done = sem("qx_done")
        sc_full, sc_free = sem("sample_scores_full"), sem("sample_scores_free")
        ss_max, ss_exp, ss_prob = sem("ss_max"), sem("ss_exp"), sem("ss_prob")
        xs_max, xs_exp, xs_prob = sem("xs_max"), sem("xs_exp"), sem("xs_prob")
        xr_new = sem("xr_new")
        r_exp_in, r_exp = sem("router_exp_in"), sem("router_exp")
        onehots, routed = sem("onehots"), sem("routed")
        rank_in = sem("rank_in")
        out_mk, out_mv, out_s, out_mem, out_s0 = (sem(f"out_{n}") for n in ("mk", "mv", "s", "mem", "s0"))
        rows_out = [sem(f"rows{n}_out") for n in range(2)]
        zeros_out = sem("zeros_out")
        a_step, v_step, p_step = sem("act_step"), sem("dve_step"), sem("pool_step")
        wm_in = [sem(f"moe_w{r}_in") for r in range(12)]
        w_used = sem("moe_w_used")
        xg_in = sem("xg_in")
        xt_full, xt_free = sem("xt_full"), sem("xt_free")
        up_exp, up_free = sem("up_exp"), sem("up_free")
        ht_full, ht_free = sem("ht_full"), sem("ht_free")
        y_free = sem("y_free")
        dve_moe = sem("dve_moe_steps")
        rows_in = [sem(f"out_rows{n}_in") for n in range(2)]
        moe_done, late_stored = sem("moe_done"), sem("late_stored")
        yg_in = [sem(f"yg{n}_in") for n in range(2)]
        fin_out = [sem(f"fin{n}_out") for n in range(2)]

        block = ctx.enter_context(nc.Block())
        CONSTS = [(ident, "c_ident"), (maskd, "c_maskd"), (masko, "c_masko"), (masks, "c_masks"),
                  (bsel, "c_bsel"), (scan, "c_scan"), (alibi, "c_alibi"), (sbias, "c_sbias"),
                  (before, "c_before"), (ones, "c_ones"), (iota, "c_iota"), (tokid, "c_tokid"),
                  (steps, "c_steps")]
        NCONST = 16 * (len(CONSTS) - 1 + 2)
        x_rows = a["x_prompt"].rearrange("b (i p) d -> p (b i) d", p=P)
        x_samp = a["x_sample"].rearrange("b t d -> (b t) d")
        y_rows = a["y_prompt"].rearrange("b (i p) d -> p (b i) d", p=P)
        y_samp = a["y_sample"].rearrange("b t d -> (b t) d")

        def rows(i):
            return P if i < NT else NS

        def tok(i):
            return slice(P * i, P * i + rows(i))

        last = {"hf": ("hf", 4), "hq": ("hq", 4), "mk": ("mk", 4), "mq": ("mq", 4), "mv": ("mv", 4),
                "hi": ("hi", 4), "hg": ("hg", 4)}
        for n in range(2):
            last[f"o{n}"] = ("x1", n, 4)
            last[f"xk{n}"] = ("mem", n, 1)
            last[f"xv{n}"] = ("mem", 2 + n, 1)
            last[f"xq{n}"] = ("xq", n, 4)
            last[f"xo{n}"] = ("x2", n, 4)

        w_moe = [a["w1"][0], a["w3"][0], a["w2"][0]]

        def moe_chunk(r, e):
            m, q = (r % 2, r // 2) if r < 8 else (2, r - 8)
            return w_moe[m][e][256 * q:256 * (q + 1), :].rearrange("(a p) n -> p a n", p=P)

        @block.sync
        def _(sp):
            for i in range(NT):
                sp.dma_start(xr[:, i, :], x_rows[:, i, :]).then_inc(x_in[i], 16)
                if i == 0:
                    sp.dma_start(gain[:, :], a["g_mix"].to_broadcast([P, D])).then_inc(gain0_in, 16)
            sp.dma_start(xr[0:NS, NT, :], x_samp).then_inc(x_in[NT], 16)
            for n, (name, col, tag) in enumerate(WBLOCKS):
                if n >= 2:
                    J.wait_filled(sp, *last[WBLOCKS[n - 2][2]])
                src = a[name][0].rearrange("(k p) n -> p k n", p=P)[:, :, 512 * col:512 * (col + 1)]
                sp.dma_start(wslot[n % 2], src).then_inc(w_in[n % 2], 16)
            J.wait_filled(sp, "x2", 1, NT)
            J.wait_filled(sp, "XOs", 1)
            for r in range(12):
                sp.dma_start(ring[:, r, :, :], moe_chunk(r, 0)).then_inc(wm_in[r], 16)
            with sp.Fori(1, NE) as e:
                for r in range(12):
                    sp.wait_ge(w_used, 12 * e + (r - 11))
                    sp.dma_start(ring[:, r, :, :], moe_chunk(r, e)).then_inc(wm_in[r], 16)
            sp.wait_ge(routed, 1)
            n_ov = sp.value_load(ovi[0:1, 0:1], min_val=0, max_val=XBLK)
            with sp.If(n_ov > 0):
                with sp.Fori(0, XBLK // 2) as j:
                    with sp.If(2 * j < n_ov):
                        for u in range(2):
                            ex = sp.value_load(ovi[0:1, bass.ds(2 * j + (u + 1), 1)], min_val=0, max_val=NE - 1)
                            for r in range(12):
                                sp.wait_ge(w_used, 24 * j + (12 * (NE + u) + r - 11))
                                sp.dma_start(ring[:, r, :, :], moe_chunk(r, ex)).then_inc(wm_in[r], 16)

        @block.gpsimd
        def _(pool):
            for buf, name in CONSTS[:8] + CONSTS[8:]:
                full = buf[:, :] if len(buf.shape) == 2 else buf[:, :, :].rearrange("p a b -> p (a b)")
                q = page_in if name == "c_ident" else const_in
                pool.dma_start(full, a[name]).then_inc(q, 16)
            pool.dma_start(lbl[:, :, :], a["hg_lb"].rearrange("l (h k) -> k l h", k=HD),
                           allow_slow_non_contiguous=True).then_inc(const_in, 16)
            pool.dma_start(ghn[:, :], a["hg_norm"].to_broadcast([P, HD])).then_inc(const_in, 16)
            pool.memset(zeros[:, :], 0.0).then_inc(p_step, 1)
            pool.wait_ge(p_step, 1)
            n = XBLK * CAP * D // P // 256
            pool.dma_start(out_rows[NE * CAP:, :].rearrange("(p r) (c d) -> p (r c) d", p=P, d=256),
                           zeros[:, :].unsqueeze(1).to_broadcast([P, n, 256])).then_inc(zeros_out, 16)
            pool.wait_ge(normed, 5)
            pool.memset(part(r_x, 0, 2048), 0.0).then_inc(zeroed, 1)
            pool.wait_ge(out_mk, 32)
            J.wait_filled(pool, "mkT", 4)
            J.wait_emptied(pool, "hq", 4)
            pool.memset(part(flat, KV + 8 * TOK + 3 * P, 3 * SEQ + HG * 288 + 512 + P), 0.0).then_inc(zeroed, 1)
            J.wait_filled(pool, "U", NCH - 1)
            pool.dma_start(s0, a["state_hgrn"][0].rearrange("b h k v -> k b h v")).then_inc(s0_in, 16)
            J.wait_emptied(pool, "Us", NB - 1)
            pool.dma_start(a["hg_sample"][0].rearrange("b h k v -> k b h v"), s0).then_inc(out_s0, 16)

            def page(b, j):
                return pool.value_load(a["page_table"][b:b + 1, j:j + 1], min_val=0, max_val=NPHYS - 1)

            def load_pages(dst, pool_name, b, s):
                for j in range(NPG):
                    src = a[pool_name][0][bass.ds(page(b, j), 1)].rearrange("a r h d -> (a r) (h d)")
                    pool.dma_start(dst[:, j, :], src).then_inc(s, 16)

            for g in range(2):
                for b in range(4 * g, 4 * g + 4):
                    if b == 0:
                        J.wait_filled(pool, "Us", NB - 1)
                        J.wait_emptied(pool, "Us", NB - 1)
                        J.wait_filled(pool, "OT", 3)
                        pool.wait_ge(out_s, 16)
                    if b >= 2:
                        J.wait_filled(pool, "KT", b - 2, 3)
                    load_pages(kbuf[b % 2], "cache_moba_k", b, k_in[b % 2])
                if g:
                    J.wait_filled(pool, "Os", 0)
                for b in range(4 * g, 4 * g + 4):
                    load_pages(vbuf[b % 4], "cache_moba_v", b, v_in)
            J.wait_filled(pool, "KT", NB - 1, 3)
            pool.dma_start(xr[:, 0:NT, :], x_rows).then_inc(xr_in, 16)
            pool.dma_start(xr[0:NS, NT, :], x_samp).then_inc(xr_in, 16)
            J.wait_filled(pool, "Os", 1)
            pool.wait_ge(out_mv, 32)
            pool.dma_start(memx, a["mem_prompt"].rearrange("b (i p) d -> p (b i) d", p=P)).then_inc(mem_in, 16)
            pool.dma_start(gain[:, :], a["g_mem"].to_broadcast([P, D])).then_inc(gain_in, 16)
            pool.wait_ge(normed, 7)
            pool.dma_start(gain[:, :], a["g_cross"].to_broadcast([P, D])).then_inc(gain_in, 16)
            pool.wait_ge(normed, 12)
            pool.dma_start(gain[:, :], a["g_ffn"].to_broadcast([P, D])).then_inc(gain_in, 16)
            for g in range(2):
                for b in range(4 * g, 4 * g + 4):
                    if b == 0:
                        J.wait_filled(pool, "mem", 3, 1)
                    if b >= 2:
                        J.wait_filled(pool, "XKT", b - 2, 3)
                    pool.dma_start(xkbuf[b % 2], a["cache_mem_k"][0][b].rearrange("(m p) h d -> p m (h d)", p=P))\
                        .then_inc(xk_in[b % 2], 16)
                if g:
                    J.wait_filled(pool, "XOs", 0)
                for b in range(4 * g, 4 * g + 4):
                    pool.dma_start(xvbuf[b % 4], a["cache_mem_v"][0][b].rearrange("(m p) h d -> p m (h d)", p=P))\
                        .then_inc(xv_in, 16)
            J.wait_filled(pool, "XOs", 1)
            J.wait_emptied(pool, "XOs", 1)
            wr = rt["wr"].rearrange("p (k n) -> p k n", k=KC)
            pool.dma_start(wr[:, :, 0:NG], a["w_grp"][0].rearrange("(k p) n -> p k n", p=P)).then_inc(rtw_in, 16)
            pool.dma_start(wr[:, :, NG:36], a["w_exp"][0].rearrange("(k p) n -> p k n", p=P)).then_inc(rtw_in, 16)
            pool.dma_start(rt["bias"][:, 0:NG], a["b_grp"].to_broadcast([P, NG])).then_inc(rtw_in, 16)
            pool.dma_start(rt["bias"][:, NG:36], a["b_exp"].to_broadcast([P, NE])).then_inc(rtw_in, 16)
            pool.wait_ge(normed, 17)
            pool.dma_start(gain[:, :], a["g_final"].to_broadcast([P, D])).then_inc(gain_in, 16)

            pool.wait_ge(routed, 1)
            pool.wait_ge(rows_out[0], 48)
            pool.wait_ge(rows_out[1], 32)

            def gather(c):
                if c:
                    pool.wait_ge(xt_full, c)
                pool.indirect_dma_start(xg, None, tok_rows, bass.IndirectOffsetOnAxis(ap=table[:, c:c + 1], axis=0))\
                    .then_inc(xg_in, 16)

            for c in range(NE // 2):
                gather(c)
            n_ov = pool.value_load(ovi[0:1, 0:1], min_val=0, max_val=XBLK)
            for c in range(NE // 2, NBLK // 2):
                with pool.If(n_ov > 2 * c - NE):
                    gather(c)
            pool.wait_ge(moe_done, 1)
            for n in range(2):
                pool.wait_ge(rows_in[n], 32 * NE // 2)
            for i, r in TILES:
                if i >= 2:
                    pool.wait_ge(xr_new, i - 1)
                for k in range(2):
                    pool.indirect_dma_start(yg[i % 2][k][0:r, :], None, out_rows,
                                            bass.IndirectOffsetOnAxis(ap=yidx[0:r, k, i:i + 1], axis=0))\
                        .then_inc(yg_in[i % 2], 16)

        @block.scalar
        def _(act):
            st = Steps(a_step)

            def rstd_root(n, src, width, out_junk):
                r = src.shape[0]
                st.did(act.activation(out_junk, src, ACT.Square, accum_out=ss[0:r, n:n + 1]))
                st.settle(act)
                st.did(act.activation(y0[0:r, n:n + 1], ss[0:r, n:n + 1], ACT.Ln, scale=1.0 / width, bias=EPS))
                st.settle(act)
                act.activation(y0[0:r, n:n + 1], y0[0:r, n:n + 1], ACT.Exp, scale=-0.5).then_inc(rooted, 1)

            def norm_root(n, src):
                r = src.shape[0]
                rstd_root(n, src, D, hn[n % 2][0:r, :])

            def evac(out, *name, view=None):
                J.wait_filled(act, *name)
                src = J.bank(*name)
                J.empties(act.activation(out, view(src) if view else src, ACT.Copy), *name)

            for i, r in TILES:
                act.wait_ge(x_in[i], 16)
                if i >= 2:
                    J.wait_filled(act, "hT", i - 2, 1)
                norm_root(i, xr[0:r, i, :])
                evac(hT[:, 0:4, tok(i)], "hT", i, 0,
                     view=lambda s, r=r: s.rearrange("p (k t) -> p k t", k=4)[:, :, 0:r])
            for c in range(5):
                J.wait_filled(act, "hf", c)
                s = J.bank("hf", c)
                if c < 4:
                    J.empties(act.activation(fk[:, c, 0:SEQ], s, ACT.Exp, scale=-1.0), "hf", c)
                else:
                    J.empties(act.activation(fk[:, :, SEQ:TOK], s[:, 0:128].rearrange("p (c t) -> p c t", c=4),
                                             ACT.Exp, scale=-1.0), "hf", c)
            for c in range(5):
                J.wait_filled(act, "hq", c)
                if c >= 2:
                    J.wait_emptied(act, "hq", c - 2)
                n = SEQ if c < 4 else 128
                act.activation(qtmp[c % 2][:, 0:n], J.bank("hq", c)[:, 0:n], ACT.Exp, scale=-1.0).then_inc(exped, 1)
            for i, r in TILES:
                evac(mkn[0:r, i, :], "mk", i, view=lambda s, r=r: s[0:r, :])
            J.wait_emptied(act, "mk", NT)
            act.dma_start(a["mk_prompt"][0, 0].rearrange("(i p) h d -> p i (h d)", p=P), mkn[:, 0:NT, :]).then_inc(out_mk, 16)
            act.dma_start(a["mk_sample"][0].rearrange("b t h d -> (b t) (h d)"), mkn[0:NS, NT, :]).then_inc(out_mk, 16)
            for c in range(5):
                if c < 4:
                    evac(mkT[:, c, 0:SEQ], "mkT", c)
                else:
                    evac(mkT[:, :, SEQ:TOK], "mkT", c, view=lambda s: s[:, 0:128].rearrange("p (c t) -> p c t", c=4))
            J.wait_emptied(act, "mv", NT)
            act.dma_start(a["mv_prompt"][0, 0].rearrange("(i p) h d -> p i (h d)", p=P), mv[:, 0:NT, :]).then_inc(out_mv, 16)
            act.dma_start(a["mv_sample"][0].rearrange("b t h d -> (b t) (h d)"), mv[0:NS, NT, :]).then_inc(out_mv, 16)
            for i, r in TILES:
                evac(vh[0:r, i, :], "hi", i, view=lambda s, r=r: s[0:r, :])
            for i, r in TILES:
                J.wait_filled(act, "hg", i)
                act.activation(gh[0:r, i, :], J.bank("hg", i)[0:r, :], ACT.Exp, scale=-1.0).then_inc(exped, 1)

            act.wait_ge(hgd, 1)
            act.activation(lb[:, :], lb[:, :], ACT.Exp).then_inc(hga, 1)
            for h in range(HG):
                act.wait_ge(hgd, 2 * h + 2)
                act.activation(hgt["lf"], fk[:, h, :], ACT.Ln).then_inc(hga, 1)
                act.wait_ge(hgd, 2 * h + 3)
                b3 = hgt["b"][:, 0:SEQ].rearrange("p (c t) -> p c t", t=CH)
                bs = hgt["b"][:, SEQ:TOK].rearrange("p (c t) -> p c t", t=NQ)
                act.activation(hgt["tb"], hgt["ta"], ACT.Exp).then_inc(hga, 1)
                act.activation(hgt["bc"], hgt["ta"], ACT.Exp, scale=-1.0).then_inc(hga, 1)
                act.activation(hgt["qo"], hgt["qo"], ACT.Exp).then_inc(hga, 1)
                for j in range(3):
                    v = kb[j].rearrange("p (c t) -> p c t", t=CH)[:, :, 0:SUB * (j + 1)]
                    act.activation(v, v, ACT.Exp).then_inc(hga, 1)
                act.activation(hgt["kdT"], hgt["kdT"], ACT.Exp).then_inc(hga, 1)
                act.activation(dl[:, h, 0:NCH], b3[:, :, CH - 1], ACT.Exp).then_inc(hga, 1)
                act.activation(dl[:, h, NCH:NCH + NB], bs[:, :, NQ - 1], ACT.Exp).then_inc(hga, 1)
                act.activation(hgt["lf"], hgt["b"], ACT.Exp).then_inc(hga, 1)
                evac(kdn[:, :, h, :], "kdn", h, view=lambda s: s.rearrange("p (i k) -> p i k", i=NT))
                evac(kds[0:NS, HD * h:HD * (h + 1)], "kds", h, view=lambda s: s[0:NS, 0:HD])

            def head_roots(i):
                r = rows(i)
                J.wait_filled(act, "o", i)
                if i >= 2:
                    J.wait_filled(act, "hgT", i - 2)
                src = J.bank("o", i)
                for h in range(HG):
                    st.did(act.activation(on[i % 2][0:r, HD * h:HD * (h + 1)], src[0:r, HD * h:HD * (h + 1)],
                                          ACT.Square, accum_out=hss[0:r, i, h:h + 1]))
                st.settle(act)
                st.did(act.activation(hy0[0:r, i, :], hss[0:r, i, :], ACT.Ln, scale=1.0 / HD, bias=EPS))
                st.settle(act)
                act.activation(hy0[0:r, i, :], hy0[0:r, i, :], ACT.Exp, scale=-0.5).then_inc(o_root, 1)

            def turn_heads(i):
                evac(mixT[:, 0:HG, tok(i)], "hgT", i,
                     view=lambda s: s.rearrange("p (h t) -> p h t", h=HG)[:, :, 0:rows(i)])

            for i in range(NT):
                head_roots(i)
                if i:
                    turn_heads(i - 1)
            J.wait_emptied(act, "U", NCH - 1)
            act.dma_start(a["hg_prompt"][0, 0].rearrange("h k v -> k h v"), state[:, NCH % 6, :, :]).then_inc(out_s, 16)
            head_roots(NT)
            turn_heads(NT - 1)
            turn_heads(NT)

            for h in range(MB + 1):
                if h < MB:
                    for i in range(NT):
                        n = NT * h + i
                        act.wait_ge(s_max, n + 1)
                        p = pb[h % 2][i][:, 0:P * (i + 1)]
                        act.activation(p, p, ACT.Exp, bias=stat[:, 1, n % 8:n % 8 + 1],
                                       accum_out=stat[:, 2, n % 8:n % 8 + 1]).then_inc(s_exp, 1)
                if h:
                    for k in range(NT):
                        if h > 2:
                            J.wait_filled(act, "OT", (h - 3) // 2)
                        evac(pt[(h - 1) % 2][:, k, P * k:SEQ], "PT", h - 1, k, view=lambda s: s[:, 0:SEQ - P * k])
                    if h % 2 == 0:
                        evac(mixT[:, 4 + h // 2 - 1, 0:SEQ], "OT", h // 2 - 1)

            for g in range(2):
                for b in range(4 * g, 4 * g + 4):
                    if b >= 2:
                        act.wait_ge(sc_full, b - 1)
                    for c in (0, 2):
                        evac(kT[b % 2][:, c, :], "KT", b, c)
                act.wait_ge(ss_max, g + 1)
                act.activation(sx, sx, ACT.Exp, bias=stat[:, 1, 0:1], accum_out=stat[:, 2, 0:1]).then_inc(ss_exp, 1)
                if g:
                    J.wait_filled(act, "Os", g - 1)
                evac(ptS, "Pt", g, view=lambda s: s.rearrange("p (j n) -> p j n", j=NPG))
                evac(mixT[:, 4:8, SEQ + 16 * g:SEQ + 16 * (g + 1)], "Os", g,
                     view=lambda s: s[:, 0:64].rearrange("p (c n) -> p c n", c=4))

            act.wait_ge(mem_in, 16)
            for i in range(MT):
                norm_root(5 + i, memx[:, i, :])
                evac(memT[:, 0:4, P * i:P * (i + 1)], "memT", i, 0, view=lambda s: s.rearrange("p (k t) -> p k t", k=4))
            for n in range(4):
                dst = (memk, memv)[n // 2]
                evac(dst[:, 0, 512 * (n % 2):512 * (n % 2 + 1)], "mem", n, 0)
                if n % 2:
                    J.wait_emptied(act, "mem", n, 0)
                    J.wait_emptied(act, "mem", n, 1)
                    out = a[("xk_prompt", "xv_prompt")[n // 2]][0, 0].rearrange("(i p) h d -> p i (h d)", p=P)
                    act.dma_start(out, dst).then_inc(out_mem, 16)
            for c in (0, 2):
                evac(memkT[:, 2 * c:2 * c + 2, :], "memKT", c, view=lambda s: s.rearrange("p (k t) -> p k t", k=2))
            for i, r in TILES:
                if i >= 2:
                    J.wait_filled(act, "h2T", i - 2, 1)
                J.wait_emptied(act, "x1", 1, i)
                norm_root(7 + i, xr[0:r, i, :])
                evac(hT[:, 0:4, tok(i)], "h2T", i, 0, view=lambda s, r=r: s.rearrange("p (k t) -> p k t", k=4)[:, :, 0:r])

            def scaled_q(half, c):
                J.wait_filled(act, "xq", half, c)
                s = J.bank("xq", half, c)
                if c < 4:
                    ins = act.activation(qT[:, 4 * half + c, 0:SEQ], s, ACT.Copy, scale=XD ** -0.5)
                else:
                    ins = act.activation(qT[:, 4 * half:4 * half + 4, SEQ:TOK],
                                         s[:, 0:128].rearrange("p (c t) -> p c t", c=4), ACT.Copy, scale=XD ** -0.5)
                J.empties(ins, "xq", half, c)

            for half in range(2):
                for c in (0, 2, 4):
                    scaled_q(half, c)
            act.wait_ge(out_mem, 32)
            for h in range(XH + 1):
                if h < XH:
                    for i2 in range(2):
                        act.wait_ge(xs_max, 2 * h + i2 + 1)
                        s = J.bank("XS", h, i2)
                        for u in range(2):
                            n = (2 * i2 + u) + 4 * (h % 2)
                            ins = act.activation(xp[h % 2][:, 2 * i2 + u, :], s[:, MEM * u:MEM * (u + 1)], ACT.Exp,
                                                 bias=stat[:, 1, n:n + 1], accum_out=stat[:, 2, n:n + 1])
                            if u == 0:
                                st.did(ins)
                        J.empties(ins, "XS", h, i2)
                if h:
                    for c in range(2):
                        evac(oT[:, 2 * (h - 1) + c, 0:SEQ], "XOT", h - 1, c)
            for g in range(2):
                for b in range(4 * g, 4 * g + 4):
                    if b >= 2:
                        act.wait_ge(sc_full, NB + b - 1)
                    for c in (0, 2):
                        evac(xkT[b % 2][:, 2 * c:2 * c + 2, :], "XKT", b, c, view=lambda s: s.rearrange("p (k t) -> p k t", k=2))
                act.wait_ge(xs_max, 2 * XH + g + 1)
                act.activation(xsx, psum[6][:, 0:MEM], ACT.Exp, bias=stat[:, 1, 0:1], accum_out=stat[:, 2, 0:1])\
                    .then_inc(xs_exp, 1)
                if g:
                    J.wait_filled(act, "XOs", g - 1)
                evac(xptS, "XPt", g, view=lambda s: s[:, 0:MT * P].rearrange("p (j n) -> p j n", j=MT))
                evac(oT[:, :, SEQ + 16 * g:SEQ + 16 * (g + 1)], "XOs", g,
                     view=lambda s: s[:, 0:128].rearrange("p (c n) -> p c n", c=KC))
            for i, r in TILES:
                J.wait_emptied(act, "x2", 1, i)
                if i >= 2:
                    J.wait_filled(act, "h3T", i - 2, 1)
                    act.wait_ge(rows_out[i % 2], 16 * (i // 2))
                norm_root(12 + i, xr[0:r, i, :])
                act.wait_ge(normed, 13 + i)
                act.dma_start(tok_rows[P * i:P * i + r, :], hn[i % 2][0:r, :]).then_inc(rows_out[i % 2], 16)
                evac(hT[:, 0:4, tok(i)], "h3T", i, 0, view=lambda s, r=r: s.rearrange("p (k t) -> p k t", k=4)[:, :, 0:r])
            act.wait_ge(r_exp_in, 1)
            act.activation(rt["ge"], rt["ge"], ACT.Exp).then_inc(r_exp, 1)
            act.wait_ge(r_exp_in, 2)
            act.activation(rt["ex"], rt["ex"], ACT.Exp).then_inc(r_exp, 1)

            def pair(j):
                first = isinstance(j, int)
                act.wait_ge(xt_full, j + 1)
                act.activation(xT[:, 4:8, :], psum[1].rearrange("p (k t) -> p k t", k=4), ACT.Copy).then_inc(xt_free, 1)
                for u in range(2):
                    act.wait_ge(w_used, 24 * j + (12 * u + 8))
                    if not first:
                        act.wait_ge(up_free, 2 * j + (u - 1))
                    act.activation(he[u], psum[2 + 2 * u], ACT.Exp, scale=-1.0).then_inc(up_exp, 1)
                    act.wait_ge(ht_full, 2 * j + (u + 1))
                    act.activation(heT[u].rearrange("p c t -> p (c t)"), psum[6], ACT.Copy).then_inc(ht_free, 1)
                    act.wait_ge(w_used, 24 * j + (12 * u + 12))
                    if not first:
                        act.wait_ge(rows_in[u], 32 * j)
                    act.activation(ys[u], psum[7], ACT.Copy).then_inc(y_free, 1)
                    act.wait_ge(y_free, 2 * j + (u + 1))
                    for half in range(2):
                        act.dma_start(out_rows[bass.ds(CAP * (2 * j + u), CAP), 512 * half:512 * (half + 1)],
                                      ys[u][CAP * half:CAP * (half + 1), :]).then_inc(rows_in[u], 16)

            pair(0)
            with act.Fori(1, NE // 2) as j:
                pair(j)
            act.wait_ge(zeros_out, 16)
            n_ov = act.value_load(ovi[0:1, 0:1], min_val=0, max_val=XBLK)
            with act.If(n_ov > 0):
                with act.Fori(NE // 2, NBLK // 2) as j:
                    with act.If(2 * j - NE < n_ov):
                        pair(j)
                        for u in range(2):
                            act.wait_ge(rows_in[u], 32 * j + 32)
                        act.activation(nt[0:1, 3, bass.ds(j - NE // 2, 1)], ss[0:1, 0:1], ACT.Copy).then_inc(late_stored, 1)
            act.activation(nt[0:1, 3, 21:22], ss[0:1, 0:1], ACT.Copy).then_inc(moe_done, 1)
            for i, r in TILES:
                act.wait_ge(xr_new, i + 1)
                if i >= 2:
                    act.wait_ge(fin_out[i % 2], 16 * (i // 2))
                rstd_root(17 + i, xr[0:r, i, :], D, fin[i % 2][0:r, :])
                act.wait_ge(normed, 18 + i)
                dst = y_rows[:, i, :] if i < NT else y_samp
                act.dma_start(dst, fin[i % 2][0:r, :]).then_inc(fin_out[i % 2], 16)
            act.wait_ge(fin_out[0], 48)
            act.wait_ge(fin_out[1], 32)
            act.wait_ge(out_mk, 32)
            act.wait_ge(out_mv, 32)
            act.wait_ge(out_s, 16)
            act.wait_ge(out_mem, 32)
            act.wait_ge(out_s0, 16)

        @block.vector
        def _(dve):
            st = Steps(v_step)

            def v(ins):
                st.did(ins)
                st.settle(dve)

            def evac(out, *name, view=None):
                J.wait_filled(dve, *name)
                src = J.bank(*name)
                J.empties(dve.tensor_copy(out, view(src) if view else src), *name)

            def refined(root, mean_src, width, tmp, cols):
                v(dve.tensor_scalar(tmp[0], mean_src, 1.0 / width, EPS, ALU.mult, ALU.add))
                v(dve.tensor_tensor(tmp[1], tmp[0], root, ALU.mult))
                v(dve.tensor_tensor(tmp[1], tmp[1], root, ALU.mult))
                v(dve.tensor_scalar(tmp[1], tmp[1], -0.5, 1.5, ALU.mult, ALU.add))
                v(dve.tensor_tensor(tmp[2], tmp[1], root, ALU.mult))
                return tmp[2]

            def norm_scale(n, src, out):
                r = src.shape[0]
                dve.wait_ge(rooted, n + 1)
                y = refined(y0[0:r, n:n + 1], ss[0:r, n:n + 1], D, [nt[0:r, k, n:n + 1] for k in range(3)], 1)
                dve.scalar_tensor_tensor(out=out, in0=src, scalar=y, in1=gain[0:r, :], op0=ALU.mult, op1=ALU.mult)\
                    .then_inc(normed, 1)

            dve.wait_ge(gain0_in, 16)
            for i, r in TILES:
                norm_scale(i, xr[0:r, i, :], hn[i % 2][0:r, :])
                evac(hT[:, 4:8, tok(i)], "hT", i, 1, view=lambda s, r=r: s.rearrange("p (k t) -> p k t", k=4)[:, :, 0:r])
            dve.wait_ge(const_in, NCONST)
            dve.tensor_tensor(lb[:, :], lbl[:, 1, :], lbl[:, 0, :], ALU.subtract).then_inc(hgd, 1)
            for c in range(5):
                dve.wait_ge(exped, c + 1)
                n = SEQ if c < 4 else 128
                t = qtmp[c % 2][:, 0:n]
                v(dve.tensor_scalar(t, t, 1.0, None, ALU.add))
                v(dve.reciprocal(t, t))
                s = J.bank("hq", c)
                if c < 4:
                    ins = dve.tensor_tensor(qh[:, c, 0:SEQ], s, t, ALU.mult)
                else:
                    ins = dve.tensor_tensor(qh[:, :, SEQ:TOK], s[:, 0:n].rearrange("p (c t) -> p c t", c=4),
                                            t.rearrange("p (c t) -> p c t", c=4), ALU.mult)
                J.empties(ins, "hq", c)
            for c in range(5):
                J.wait_filled(dve, "mq", c)
                s = J.bank("mq", c)
                if c < 4:
                    ins = dve.tensor_scalar(mqT[:, c, 0:SEQ], s, MD ** -0.5, None, ALU.mult)
                else:
                    ins = dve.tensor_scalar(mqT[:, :, SEQ:TOK], s[:, 0:128].rearrange("p (c t) -> p c t", c=4),
                                            MD ** -0.5, None, ALU.mult)
                J.empties(ins, "mq", c)
            for i, r in TILES:
                evac(mv[0:r, i, :], "mv", i, view=lambda s, r=r: s[0:r, :])
            for i, r in TILES:
                dve.wait_ge(exped, 6 + i)
                g = gh[0:r, i, :]
                v(dve.tensor_scalar(g, g, 1.0, None, ALU.add))
                v(dve.reciprocal(g, g))
                ins = dve.tensor_tensor(g, J.bank("hg", i)[0:r, :], g, ALU.mult)
                J.empties(ins, "hg", i)
                J.wait_emptied(dve, "hg", i)
                g3 = g.rearrange("p (h v) -> p h v", h=HG)
                st.did(dve.tensor_tensor(g3, g3, ghn[0:r, :].unsqueeze(1).to_broadcast([r, HG, HD]), ALU.mult))

            dve.wait_ge(hga, 1)
            v(dve.tensor_scalar(lb[:, :], lb[:, :], 1.0, None, ALU.add))
            v(dve.reciprocal(lb[:, :], lb[:, :]))
            v(dve.tensor_scalar(omlb[:, :], lb[:, :], -1.0, 1.0, ALU.mult, ALU.add))
            J.wait_emptied(dve, "hf", 4)
            allf = fk.rearrange("p h t -> p (h t)")
            v(dve.tensor_scalar(allf, allf, 1.0, None, ALU.add))
            v(dve.reciprocal(allf, allf))
            dve.wait_ge(zeroed, 2)
            dve.wait_ge(out_mk, 32)
            t = hgt
            for h in range(HG):
                f = fk[:, h, :]
                if h:
                    J.wait_filled(dve, "kds", h - 1)
                dve.tensor_scalar(f, f, omlb[:, h:h + 1], lb[:, h:h + 1], ALU.mult, ALU.add).then_inc(hgd, 1)
                dve.wait_ge(hga, 11 * h + 2)
                st.did(dve.tensor_scalar(f, f, -1.0, 1.0, ALU.mult, ALU.add))
                st.did(dve.tensor_scalar(t["tb"], t["lf"], -21.0, None, ALU.max))
                v(dve.tensor_tensor_scan(t["b"], scan[:, :], t["lf"], 0.0, ALU.mult, ALU.add))
                v(dve.tensor_tensor_scan(t["bc"], scan[:, :], t["tb"], 0.0, ALU.mult, ALU.add))

                def cut(x, size, lo, hi):
                    return x[:, lo:hi].rearrange("p (c t) -> p c t", t=size)

                b8 = cut(t["bc"], SUB, 0, SEQ)
                st.did(dve.tensor_tensor(cut(t["ta"], SUB, 0, SEQ), b8,
                                         b8[:, :, 3:4].to_broadcast([P, SEQ // SUB, SUB]), ALU.subtract))
                b4 = cut(t["bc"], NQ, SEQ, TOK)
                st.did(dve.tensor_tensor(cut(t["ta"], NQ, SEQ, TOK), b4,
                                         b4[:, :, 1:2].to_broadcast([P, NB, NQ]), ALU.subtract))
                bj = t["b"][:, 0:SEQ].rearrange("p (c j u) -> p j c u", j=CH // SUB, u=SUB)
                qo = t["qo"].rearrange("p (j c u) -> p j c u", j=3, u=SUB)
                for j in range(3):
                    st.did(dve.tensor_tensor(qo[:, j], bj[:, j + 1],
                                             bj[:, j, :, SUB - 1:SUB].to_broadcast([P, NCH, SUB]), ALU.subtract))
                b32 = cut(t["b"], CH, 0, SEQ)
                for j in range(3):
                    n = SUB * (j + 1)
                    st.did(dve.tensor_tensor(kb[j].rearrange("p (c t) -> p c t", t=CH)[:, :, 0:n],
                                             b32[:, :, n - 1:n].to_broadcast([P, NCH, n]), b32[:, :, 0:n], ALU.subtract))
                st.did(dve.tensor_tensor(cut(t["kdT"], CH, 0, SEQ), b32[:, :, CH - 1:CH].to_broadcast([P, NCH, CH]),
                                         b32, ALU.subtract))
                bs = cut(t["b"], NQ, SEQ, TOK)
                dve.tensor_tensor(cut(t["kdT"], NQ, SEQ, TOK), bs[:, :, NQ - 1:NQ].to_broadcast([P, NB, NQ]),
                                  bs, ALU.subtract).then_inc(hgd, 1)
                q, k = qh[:, h, :], fk[:, h, :]
                dve.wait_ge(hga, 11 * h + 12)
                st.did(dve.tensor_tensor(t["qd"], q, t["tb"], ALU.mult))
                st.did(dve.tensor_tensor(t["kd"], k, t["bc"], ALU.mult))
                q3 = q[:, 0:SEQ].rearrange("p (c j u) -> p j c u", j=CH // SUB, u=SUB)
                k32 = cut(k, CH, 0, SEQ)
                for j in range(3):
                    st.did(dve.tensor_tensor(qo[:, j], qo[:, j], q3[:, j + 1], ALU.mult))
                    kv = kb[j].rearrange("p (c t) -> p c t", t=CH)[:, :, 0:SUB * (j + 1)]
                    st.did(dve.tensor_tensor(kv, kv, k32[:, :, 0:SUB * (j + 1)], ALU.mult))
                st.did(dve.tensor_tensor(t["kdT"], t["kdT"], k, ALU.mult))
                st.settle(dve)
                v(dve.tensor_tensor(q, q, t["lf"], ALU.mult))
                dve.tensor_copy(qx[:, h, :].rearrange("p (b m) -> p b m", m=36)[:, :, 0:NQ], cut(q, NQ, SEQ, TOK))\
                    .then_inc(head_ready, 1)
                J.wait_filled(dve, "attd", h)
                J.empties(dve.copy_predicated(att[:, h, :], maskd[:, :].bitcast(U32), J.bank("attd", h)), "attd", h)
                J.wait_filled(dve, "atto", h)
                J.wait_emptied(dve, "attd", h)
                s = J.bank("atto", h)
                a4 = att[:, h, :].rearrange("p (c j u) -> p j c u", j=CH // SUB, u=SUB)
                for j in range(3):
                    st.did(dve.copy_predicated(a4[:, j + 1], masko[:, P * j:P * (j + 1)].bitcast(U32)
                                               .rearrange("p (c u) -> p c u", u=SUB),
                                               s[:, P * j:P * (j + 1)].rearrange("p (c u) -> p c u", u=SUB)))
                J.empties(dve.copy_predicated(atts[0:NS, NS * h:NS * (h + 1)],
                                              masks[:, 0:NS].bitcast(U32), s[0:NS, 3 * P:3 * P + NS]), "atto", h)
            J.wait_emptied(dve, "kds", HG - 1)

            def new_state(n):
                J.wait_filled(dve, "U", n)
                if n >= 5:
                    J.wait_filled(dve, "o", (n - 5) // 4)
                if n:
                    J.wait_emptied(dve, "U", n - 1)
                for h in range(HG):
                    u = J.bank("U", n)[:, HD * h:HD * (h + 1)]
                    dst = state[:, (n + 1) % 6, h, :]
                    if n == 0:
                        ins = dve.tensor_copy(dst, u)
                    else:
                        ins = dve.scalar_tensor_tensor(out=dst, in0=state[:, n % 6, h, :], scalar=dl[:, h, n:n + 1],
                                                       in1=u, op0=ALU.mult, op1=ALU.add)
                J.empties(ins, "U", n)

            def head_norm(i):
                r = rows(i)
                dve.wait_ge(o_root, i + 1)
                y = refined(hy0[0:r, i, :], hss[0:r, i, :], HD, [hnt[0:r, k, :] for k in range(3)], HG)
                s = J.bank("o", i)
                for h in range(HG):
                    c = slice(HD * h, HD * (h + 1))
                    ins = dve.scalar_tensor_tensor(out=on[i % 2][0:r, c], in0=s[0:r, c], scalar=y[:, h:h + 1],
                                                   in1=gh[0:r, i, c], op0=ALU.mult, op1=ALU.mult)
                J.empties(ins, "o", i)

            for i in range(NT):
                for c in range(P // CH):
                    new_state(i * (P // CH) + c)
                head_norm(i)
            head_norm(NT)
            J.wait_filled(dve, "o", NT)
            dve.wait_ge(out_s, 16)
            for b in range(NB):
                ins = dve.tensor_scalar(kdx[0:NS, b, :], kds[0:NS, :], bsel[:, b:b + 1], None, ALU.mult)
            ins.then_inc(kdx_done, 1)
            for b in range(NB):
                J.wait_filled(dve, "Us", b)
                for h in range(HG):
                    u = J.bank("Us", b)[:, HD * h:HD * (h + 1)]
                    ins = dve.scalar_tensor_tensor(out=s0[:, b, h, :], in0=s0[:, b, h, :],
                                                   scalar=dl[:, h, NCH + b:NCH + b + 1], in1=u,
                                                   op0=ALU.mult, op1=ALU.add)
                J.empties(ins, "Us", b)

            def softmax_stats(src, col, sem_max, n=1):
                v(dve.tensor_reduce(stat[:, 0, col:col + n], src, AX, ALU.max))
                dve.tensor_scalar(stat[:, 1, col:col + n], stat[:, 0, col:col + n], -1.0, None, ALU.mult)\
                    .then_inc(sem_max, 1)

            def probs(p, col, sem_exp, count, sem_prob):
                dve.wait_ge(sem_exp, count)
                v(dve.reciprocal(stat[:, 3, col:col + 1], stat[:, 2, col:col + 1]))
                dve.tensor_scalar(p, p, stat[:, 3, col:col + 1], None, ALU.mult).then_inc(sem_prob, 1)

            for h in range(MB):
                for i in range(NT):
                    n = NT * h + i
                    m = P * (i + 1)
                    J.wait_filled(dve, "S", h, i)
                    if h >= 2:
                        J.wait_filled(dve, "PT", h - 2, NT - 1)
                    p = pb[h % 2][i][:, 0:m]
                    J.empties(dve.scalar_tensor_tensor(out=p, in0=alibi[:, SEQ - P - P * i:SEQ - P - P * i + m],
                                                       scalar=2.0 ** -(h + 1), in1=J.bank("S", h, i)[:, 0:m],
                                                       op0=ALU.mult, op1=ALU.add), "S", h, i)
                    J.wait_emptied(dve, "S", h, i)
                    softmax_stats(p, n % 8, s_max)
                    if i:
                        probs(pb[h % 2][i - 1][:, 0:m - P], (n - 1) % 8, s_exp, n, s_prob)
                probs(pb[h % 2][NT - 1], n % 8, s_exp, n + 1, s_prob)

            J.wait_filled(dve, "o", NT)
            v(dve.memset(part(r_c, 4 * TOK, 4 * NB * 32), 0.0))
            for h in range(MB):
                par, c = h % 2, h // 2
                rr = slice(64 * par, 64 * par + 64)
                ins = dve.tensor_copy(qxm[rr, c, :, NQ * h:NQ * (h + 1)],
                                      mqT[rr, c, SEQ:TOK].rearrange("p (b t) -> p b t", t=NQ))
            ins.then_inc(qx_done, 1)
            for g in range(2):
                for b in range(4 * g, 4 * g + 4):
                    if b < 2:
                        dve.wait_ge(out_s0, 16)
                    if b >= 2:
                        dve.wait_ge(sc_full, b - 1)
                    for c in (1, 3):
                        evac(kT[b % 2][:, c, :], "KT", b, c)
                dve.wait_ge(sc_full, 4 * g + 4)
                if g:
                    J.wait_filled(dve, "Ptn", g - 1)
                dve.tensor_tensor(sx[:, 0:PAST], sbias[:, g, 0:PAST], psum[6], ALU.add).then_inc(sc_free, 1)
                J.wait_filled(dve, "Sn", g)
                J.empties(dve.tensor_tensor(sx[:, PAST:], sbias[:, g, PAST:], J.bank("Sn", g)[:, 0:NS], ALU.add), "Sn", g)
                J.wait_emptied(dve, "Sn", g)
                dve.wait_ge(sc_free, g + 1)
                softmax_stats(sx, 0, ss_max)
                probs(sx, 0, ss_exp, g + 1, ss_prob)
                if g:
                    J.wait_filled(dve, "Os", g - 1)
                evac(ptn[0:NS, :], "Ptn", g, view=lambda s: s[0:NS, 0:P])

            def add_rows(tag, half, i):
                r = rows(i)
                J.wait_filled(dve, tag, half, i)
                x = xr[0:r, i, 512 * half:512 * (half + 1)]
                J.empties(dve.tensor_tensor(x, x, J.bank(tag, half, i)[0:r, :], ALU.add), tag, half, i)

            dve.wait_ge(xr_in, 32)
            for half in range(2):
                for i, r in TILES:
                    add_rows("x1", half, i)
            dve.wait_ge(gain_in, 16)
            for i in range(MT):
                norm_scale(5 + i, memx[:, i, :], hn[(5 + i) % 2])
                evac(memT[:, 4:8, P * i:P * (i + 1)], "memT", i, 1, view=lambda s: s.rearrange("p (k t) -> p k t", k=4))
            for n in range(4):
                evac((memk, memv)[n // 2][:, 1, 512 * (n % 2):512 * (n % 2 + 1)], "mem", n, 1)
            for c in (1, 3):
                evac(memkT[:, 2 * c:2 * c + 2, :], "memKT", c, view=lambda s: s.rearrange("p (k t) -> p k t", k=2))
            dve.wait_ge(gain_in, 32)
            for i, r in TILES:
                norm_scale(7 + i, xr[0:r, i, :], hn[(7 + i) % 2][0:r, :])
                evac(hT[:, 4:8, tok(i)], "h2T", i, 1, view=lambda s, r=r: s.rearrange("p (k t) -> p k t", k=4)[:, :, 0:r])
            for half in range(2):
                for c in (1, 3):
                    J.wait_filled(dve, "xq", half, c)
                    J.empties(dve.tensor_scalar(qT[:, 4 * half + c, 0:SEQ], J.bank("xq", half, c), XD ** -0.5, None,
                                                ALU.mult), "xq", half, c)
            for h in range(XH + 1):
                if h < XH:
                    for i2 in range(2):
                        J.wait_filled(dve, "XS", h, i2)
                        if h >= 2:
                            J.wait_filled(dve, "XPT", h - 2, MT - 1)
                        softmax_stats(J.bank("XS", h, i2).rearrange("p (u m) -> p u m", u=2), 2 * i2 + 4 * (h % 2), xs_max, 2)
                    for i2 in range(2):
                        J.wait_emptied(dve, "XS", h, i2)
                        for u in range(2):
                            n = 2 * i2 + u + 4 * (h % 2)
                            v(dve.reciprocal(stat[:, 3, n:n + 1], stat[:, 2, n:n + 1]))
                            x = xp[h % 2][:, 2 * i2 + u, :]
                            dve.tensor_scalar(x, x, stat[:, 3, n:n + 1], None, ALU.mult).then_inc(xs_prob, 1)
                if h:
                    for k in range(MT):
                        if h >= 3:
                            J.wait_filled(dve, "XOT", h - 3, 1)
                        if h == 1:
                            dve.wait_ge(out_mem, 32)
                        evac(xpt[(h - 1) % 2][:, k, :], "XPT", h - 1, k)
            J.wait_filled(dve, "XPT", XH - 1, MT - 1)
            v(dve.memset(part(r_mix, 2048, KC * NB * 32), 0.0))
            for h in range(XH):
                for c in (2 * h, 2 * h + 1):
                    ins = dve.tensor_copy(qxx[:, c, :, NQ * h:NQ * (h + 1)],
                                          qT[:, c, SEQ:TOK].rearrange("p (b t) -> p b t", t=NQ))
            ins.then_inc(qx_done, 1)
            for g in range(2):
                for b in range(4 * g, 4 * g + 4):
                    if b >= 2:
                        dve.wait_ge(sc_full, NB + b - 1)
                    for c in (1, 3):
                        evac(xkT[b % 2][:, 2 * c:2 * c + 2, :], "XKT", b, c, view=lambda s: s.rearrange("p (k t) -> p k t", k=2))
                dve.wait_ge(sc_full, NB + 4 * g + 4)
                if g:
                    J.wait_filled(dve, "XPt", g - 1)
                softmax_stats(psum[6][:, 0:MEM], 0, xs_max)
                dve.wait_ge(xs_exp, g + 1)
                v(dve.reciprocal(stat[:, 3, 0:1], stat[:, 2, 0:1]))
                dve.tensor_scalar(xsx, xsx, stat[:, 3, 0:1], None, ALU.mult).then_inc(xs_prob, 1)
            for half in range(2):
                for i, r in TILES:
                    add_rows("x2", half, i)
            dve.wait_ge(gain_in, 48)
            for i, r in TILES:
                norm_scale(12 + i, xr[0:r, i, :], hn[(12 + i) % 2][0:r, :])
                evac(hT[:, 4:8, tok(i)], "h3T", i, 1, view=lambda s, r=r: s.rearrange("p (k t) -> p k t", k=4)[:, :, 0:r])

            R = rt
            lg = R["lg"].rearrange("p (i n) -> p i n", n=36)
            iota3 = lambda n: iota[:, 0:n].unsqueeze(1).to_broadcast([P, 5, n])
            dve.wait_ge(rtw_in, 64)
            v(dve.memset(lg, 0.0))
            for i, r in TILES:
                J.wait_filled(dve, "logit", i)
                J.empties(dve.tensor_tensor(lg[0:r, i, :], R["bias"][0:r, :], J.bank("logit", i)[0:r, 0:36], ALU.add),
                          "logit", i)
            v(dve.memset(R["g8"], -3e38))
            J.wait_emptied(dve, "logit", NT)
            g8 = R["g8"].rearrange("p (i n) -> p i n", n=8)
            m8 = R["m8"].rearrange("p (i n) -> p i n", n=8)
            v(dve.tensor_copy(g8[:, :, 0:NG], lg[:, :, 0:NG]))
            for i in range(5):
                ins = dve.max(m8[:, i, :], g8[:, i, :])
            v(ins)
            for i in range(5):
                ins = dve.max_index(i8[:, i, :], m8[:, i, :], g8[:, i, :])
            v(ins)
            gi = R["i8f"]
            v(dve.tensor_copy(gi, i8[:, :, 0]))
            ge = R["ge"].rearrange("p (i n) -> p i n", n=NG)
            dve.tensor_tensor(ge, lg[:, :, 0:NG], m8[:, :, 0:1].to_broadcast([P, 5, NG]), ALU.subtract)\
                .then_inc(r_exp_in, 1)
            ohg = R["ohg"].rearrange("p (i n) -> p i n", n=NG)
            v(dve.tensor_tensor(ohg, iota3(NG), gi.unsqueeze(2).to_broadcast([P, 5, NG]), ALU.is_equal))
            pr = R["pr"].rearrange("p (i g e) -> p i g e", i=5, g=NG)
            for i in range(5):
                ins = dve.tensor_tensor(pr[:, i], lg[:, i, NG:36].rearrange("p (g e) -> p g e", g=NG),
                                        ohg[:, i, :].unsqueeze(2).to_broadcast([P, NG, EPG]), ALU.mult)
            v(ins)
            se = R["se"].rearrange("p (i n) -> p i n", n=8)
            for i in range(5):
                ins = dve.tensor_reduce(se[:, i, :], pr[:, i].rearrange("p g e -> p e g"), AX, ALU.add)
            v(ins)
            me = R["me"].rearrange("p (i n) -> p i n", n=8)
            for i in range(5):
                ins = dve.max(me[:, i, :], se[:, i, :])
            v(ins)
            for i in range(5):
                ins = dve.max_index(i8[:, i, :], me[:, i, :], se[:, i, :])
            v(ins)
            ek = R["ek"].rearrange("p (k i) -> p k i", k=2)
            for k in range(2):
                ins = dve.tensor_copy(ek[:, k, :], i8[:, :, k])
            dve.tensor_tensor(R["ex"], me[:, :, 1], me[:, :, 0], ALU.subtract).then_inc(r_exp_in, 1)
            dve.wait_ge(r_exp_in, 2)
            dve.wait_ge(r_exp, 2)
            v(dve.tensor_reduce(R["gw"], ge, AX, ALU.add))
            v(dve.reciprocal(R["gw"], R["gw"]))
            v(dve.tensor_scalar(R["t1"][:, 0:5], R["ex"], 1.0, None, ALU.add))
            v(dve.reciprocal(R["t1"][:, 0:5], R["t1"][:, 0:5]))
            v(dve.tensor_tensor(gates[:, 0, :], R["gw"], R["t1"][:, 0:5], ALU.mult))
            v(dve.tensor_tensor(gates[:, 1, :], gates[:, 0, :], R["ex"], ALU.mult))
            eid = R["eid"].rearrange("p (k i) -> p k i", k=2)
            for k in range(2):
                ins = dve.scalar_tensor_tensor(out=eid[:, k, :], in0=gi, scalar=float(EPG), in1=ek[:, k, :],
                                               op0=ALU.mult, op1=ALU.add)
            v(ins)
            m = R["m"].rearrange("p (k i n) -> p k i n", k=2, i=5)
            ms = R["ms"].rearrange("p (i n) -> p i n", i=5)
            for k in range(2):
                ins = dve.tensor_tensor(m[:, k], iota3(NE), eid[:, k, :].unsqueeze(2).to_broadcast([P, 5, NE]), ALU.is_equal)
            v(ins)
            dve.tensor_tensor(ms, m[:, 0], m[:, 1], ALU.add).then_inc(onehots, 1)
            J.wait_filled(dve, "rank")
            s = J.bank("rank")
            v(dve.tensor_copy(R["cnt"], s[:, 160:192]))
            tmp = R["tmp"].rearrange("p (i n) -> p i n", i=5)
            rk = R["rk"].rearrange("p (k i) -> p k i", k=2)
            for k in range(2):
                v(dve.tensor_tensor(tmp, m[:, k], s[:, 0:160].rearrange("p (i n) -> p i n", i=5), ALU.mult))
                ins = dve.tensor_reduce(rk[:, k, :], tmp, AX, ALU.add)
                if k == 0:
                    v(ins)
            J.empties(ins, "rank")
            J.wait_emptied(dve, "rank")
            big = R["big"].rearrange("p (e m) -> p e m", e=NE)
            v(dve.tensor_tensor(big, R["cnt"].unsqueeze(2).to_broadcast([P, NE, 8]),
                                steps[:, :].unsqueeze(1).to_broadcast([P, NE, 8]), ALU.is_gt))
            v(dve.tensor_reduce(R["ovn"], big, AX, ALU.add))
            v(dve.tensor_tensor_scan(R["ove"], ones[:, 0:NE], R["ovn"], 0.0, ALU.mult, ALU.add))
            v(dve.tensor_tensor(R["ovs"], R["ove"], R["ovn"], ALU.subtract))
            qk = R["qk"].rearrange("p (k i) -> p k i", k=2)
            ovk = R["ovk"].rearrange("p (k i) -> p k i", k=2)
            b5 = R["big"][:, 0:80].rearrange("p (i m) -> p i m", m=8)
            v(dve.tensor_tensor(b5, R["rk"].unsqueeze(2).to_broadcast([P, 10, 8]),
                                steps[:, :].unsqueeze(1).to_broadcast([P, 10, 8]), ALU.is_ge))
            v(dve.tensor_reduce(R["qk"], b5, AX, ALU.add))
            v(dve.scalar_tensor_tensor(out=R["rr"], in0=R["qk"], scalar=-float(CAP), in1=R["rk"], op0=ALU.mult, op1=ALU.add))
            for k in range(2):
                v(dve.tensor_tensor(tmp, m[:, k], R["ovs"].unsqueeze(1).to_broadcast([P, 5, NE]), ALU.mult))
                v(dve.tensor_reduce(ovk[:, k, :], tmp, AX, ALU.add))
            v(dve.tensor_tensor(R["t1"], R["ovk"], R["qk"], ALU.add))
            v(dve.scalar_tensor_tensor(out=R["t1"], in0=R["t1"], scalar=float(NE - 1), in1=R["eid"], op0=ALU.add, op1=ALU.subtract))
            v(dve.tensor_scalar(R["t2"], R["qk"], 0.0, None, ALU.is_gt))
            v(dve.tensor_tensor(R["t1"], R["t1"], R["t2"], ALU.mult))
            v(dve.tensor_tensor(R["sk"], R["eid"], R["t1"], ALU.add))
            v(dve.scalar_tensor_tensor(out=yidx[:, :, :].rearrange("p k i -> p (k i)"), in0=R["sk"], scalar=float(CAP),
                                       in1=R["rr"], op0=ALU.mult, op1=ALU.add))
            ohs = R["ohs"].rearrange("p (a n) -> p a n", n=NBLK)
            ohr = R["ohr"].rearrange("p (a n) -> p a n", n=CAP)
            v(dve.tensor_tensor(ohs, iota[:, 0:NBLK].unsqueeze(1).to_broadcast([P, 10, NBLK]),
                                R["sk"].unsqueeze(2).to_broadcast([P, 10, NBLK]), ALU.is_equal))
            for k in range(2):
                o5 = ohs[:, 5 * k:5 * k + 5, :]
                ins = dve.tensor_tensor(o5, o5, tokid[:, :].unsqueeze(2).to_broadcast([P, 5, NBLK]), ALU.mult)
            v(ins)
            dve.tensor_tensor(ohr, iota[:, 0:CAP].unsqueeze(1).to_broadcast([P, 10, CAP]),
                              R["rr"].unsqueeze(2).to_broadcast([P, 10, CAP]), ALU.is_equal).then_inc(onehots, 1)
            cmp = R["cmp"].rearrange("p (s e) -> p s e", s=XBLK)
            v(dve.tensor_tensor(cmp[0:1], R["ove"][0:1, :].unsqueeze(1).to_broadcast([1, XBLK, NE]),
                                iota[0:1, 0:XBLK].unsqueeze(2).to_broadcast([1, XBLK, NE]), ALU.is_le))
            v(dve.tensor_reduce(R["exs"][0:1], cmp[0:1], AX, ALU.add))
            dve.tensor_scalar(ovi[0:1, 1:1 + XBLK], R["exs"][0:1], float(NE - 1), None, ALU.min)
            v(dve.tensor_copy(ovi[0:1, 0:1], R["ove"][0:1, NE - 1:NE]))
            J.wait_filled(dve, "table")
            dve.tensor_copy(table[:, :], J.bank("table")[:, 0:NBLK // 2]).then_inc(routed, 1)

            def pair(j):
                first = isinstance(j, int)
                dve.wait_ge(xt_full, j + 1)
                dve.tensor_copy(xT[:, 0:4, :], psum[0].rearrange("p (k t) -> p k t", k=4)).then_inc(xt_free, 1)
                for u in range(2):
                    dve.wait_ge(up_exp, 2 * j + (u + 1))
                    step = 6 * j + 3 * u
                    dve.tensor_scalar(he[u], he[u], 1.0, None, ALU.add).then_inc(dve_moe, 1)
                    dve.wait_ge(dve_moe, step + 1)
                    dve.reciprocal(he[u], he[u]).then_inc(dve_moe, 1)
                    dve.wait_ge(dve_moe, step + 2)
                    if not first:
                        dve.wait_ge(ht_full, 2 * j + (u - 1))
                    dve.tensor_tensor(he[u], he[u], psum[2 + 2 * u], ALU.mult).then_inc(dve_moe, 1)
                    dve.wait_ge(dve_moe, step + 3)
                    dve.tensor_tensor(h2[u], he[u], psum[3 + 2 * u], ALU.mult).then_inc(up_free, 1)

            pair(0)
            with dve.Fori(1, NE // 2) as j:
                pair(j)
            n_ov = dve.value_load(ovi[0:1, 0:1], min_val=0, max_val=XBLK)
            with dve.If(n_ov > 0):
                with dve.Fori(NE // 2, NBLK // 2) as j:
                    with dve.If(2 * j - NE < n_ov):
                        pair(j)
            dve.wait_ge(gain_in, 64)
            for i, r in TILES:
                dve.wait_ge(yg_in[i % 2], 32 * (i // 2 + 1))
                x = xr[0:r, i, :]
                v(dve.scalar_tensor_tensor(out=x, in0=yg[i % 2][0][0:r, :], scalar=gates[0:r, 0, i:i + 1], in1=x,
                                           op0=ALU.mult, op1=ALU.add))
                dve.scalar_tensor_tensor(out=x, in0=yg[i % 2][1][0:r, :], scalar=gates[0:r, 1, i:i + 1], in1=x,
                                         op0=ALU.mult, op1=ALU.add).then_inc(xr_new, 1)
                norm_scale(17 + i, x, fin[i % 2][0:r, :])

        @block.tensor
        def _(pe):
            def turn(what, i, n, ready):
                r = rows(i)
                pe.wait_ge(normed, ready)
                for half in range(2):
                    J.wait_free(pe, what, i, half)
                    s = J.bank(what, i, half)
                    for k in range(4):
                        ins = pe.transpose(s[:, P * k:P * k + r], hn[n % 2][0:r, P * (4 * half + k):P * (4 * half + k + 1)],
                                           ident[0:r, 0:r])
                    J.fills(ins, what, i, half)

            def weights(tag):
                n = WPOS[tag]
                pe.wait_ge(w_in[n % 2], 16 * (n // 2 + 1))
                return wslot[n % 2]

            def features_out(what, *key):
                w = weights(what if not key else f"xq{key[0]}")
                for c in range(5):
                    J.wait_free(pe, what, *key, c)
                    s = J.bank(what, *key, c)
                    for cc in ([c] if c < 4 else range(4)):
                        for k in range(KC):
                            out = s if c < 4 else s[:, NS * cc:NS * (cc + 1)]
                            ins = pe.matmul(out, w[:, k, P * cc:P * (cc + 1)],
                                            hT[:, k, 0:SEQ] if c < 4 else hT[:, k, SEQ:TOK],
                                            start=(k == 0), stop=(k == KC - 1))
                    J.fills(ins, what, *key, c)

            def rows_of(name, i, w, lhs):
                J.wait_free(pe, *name)
                r = rows(i)
                for k in range(KC):
                    ins = pe.matmul(J.bank(*name)[0:r, :], lhs[:, k, tok(i)], w[:, k, :], start=(k == 0), stop=(k == KC - 1))
                J.fills(ins, *name)

            pe.wait_ge(page_in, 16)
            for i, r in TILES:
                turn("hT", i, i, i + 1)
            J.wait_emptied(pe, "hT", NT, 0)
            J.wait_emptied(pe, "hT", NT, 1)
            features_out("hf")
            features_out("hq")
            w = weights("mk")
            for i, r in TILES:
                rows_of(("mk", i), i, w, hT)
            features_out("mq")
            J.wait_emptied(pe, "mk", NT)
            for c in range(5):
                J.wait_free(pe, "mkT", c)
                s = J.bank("mkT", c)
                for n in range(4):
                    if c < 4:
                        ins = pe.transpose(s[:, P * n:P * (n + 1)], mkn[:, n, P * c:P * (c + 1)], ident[:, :])
                    else:
                        ins = pe.transpose(s[:, NS * n:NS * (n + 1)], mkn[0:NS, NT, P * n:P * (n + 1)], ident[0:NS, 0:NS])
                J.fills(ins, "mkT", c)
            for tag in ("mv", "hi", "hg"):
                w = weights(tag)
                for i, r in TILES:
                    rows_of((tag, i), i, w, hT)

            for h in range(HG):
                pe.wait_ge(head_ready, h + 1)
                J.wait_free(pe, "attd", h)
                s = J.bank("attd", h)
                for i in range(NT):
                    ins = pe.matmul(s[:, tok(i)], hgt["kd"][:, tok(i)], hgt["qd"][:, tok(i)], start=True, stop=True)
                J.fills(ins, "attd", h)
                J.wait_free(pe, "atto", h)
                s = J.bank("atto", h)
                for j in range(3):
                    for i in range(NT):
                        c = slice(P * j + NS * i, P * j + NS * (i + 1))
                        pe.matmul(s[:, c], kb[j][:, tok(i)], hgt["qo"][:, c], start=True, stop=True)
                ins = pe.matmul(s[0:NS, 3 * P:3 * P + NS], hgt["kd"][:, SEQ:TOK], hgt["qd"][:, SEQ:TOK], start=True, stop=True)
                J.fills(ins, "atto", h)
                J.wait_free(pe, "kdn", h)
                for i in range(NT):
                    ins = pe.transpose(J.bank("kdn", h)[:, tok(i)], hgt["kdT"][:, tok(i)], ident[:, :])
                J.fills(ins, "kdn", h)
                J.wait_free(pe, "kds", h)
                ins = pe.transpose(J.bank("kds", h)[0:NS, 0:P], hgt["kdT"][:, SEQ:TOK], ident[:, :])
                J.fills(ins, "kds", h)

            def turn_heads(i):
                r = rows(i)
                J.wait_emptied(pe, "o", i)
                J.wait_free(pe, "hgT", i)
                for h in range(HG):
                    ins = pe.transpose(J.bank("hgT", i)[:, P * h:P * h + r], on[i % 2][0:r, HD * h:HD * (h + 1)], ident[0:r, 0:r])
                J.fills(ins, "hgT", i)

            J.wait_emptied(pe, "kdn", HG - 1)
            J.wait_emptied(pe, "kds", HG - 1)
            J.wait_emptied(pe, "atto", HG - 1)
            for i in range(NT):
                for c in range(P // CH):
                    n = i * (P // CH) + c
                    J.wait_free(pe, "U", n)
                    q = slice(CH * c, CH * (c + 1))
                    for h in range(HG):
                        ins = pe.matmul(J.bank("U", n)[:, HD * h:HD * (h + 1)], kdn[q, i, h, :], vh[q, i, HD * h:HD * (h + 1)],
                                        start=True, stop=True, tile_position=(CH * c, 0))
                    J.fills(ins, "U", n)
                J.wait_free(pe, "o", i)
                J.wait_emptied(pe, "U", 4 * i + 2)
                for h in range(HG):
                    c0 = slice(HD * h, HD * (h + 1))
                    s = J.bank("o", i)
                    ins = pe.matmul(s[:, c0], att[:, h, tok(i)], vh[:, i, c0], start=True, stop=True)
                    for c in range(P // CH):
                        n = i * (P // CH) + c
                        if n:
                            ins = pe.matmul(s[CH * c:CH * (c + 1), c0], qh[:, h, CH * n:CH * (n + 1)], state[:, n % 6, h, :],
                                            start=False, stop=True, skip_group_check=True)
                J.fills(ins, "o", i)
                if i:
                    turn_heads(i - 1)
            J.wait_free(pe, "o", NT)
            pe.wait_ge(s0_in, 16)
            s = J.bank("o", NT)
            for h in range(HG):
                c0 = slice(HD * h, HD * (h + 1))
                pe.matmul(s[0:NS, c0], atts[0:NS, NS * h:NS * (h + 1)], vh[0:NS, NT, c0], start=True, stop=False)
                for b in range(NB):
                    ins = pe.matmul(s[0:NS, c0], qx[:, h, NS * b:NS * (b + 1)], s0[:, b, h, :], start=False, stop=(b == NB - 1))
            J.fills(ins, "o", NT)
            turn_heads(NT - 1)
            pe.wait_ge(kdx_done, 1)
            for b in range(NB):
                J.wait_free(pe, "Us", b)
                for h in range(HG):
                    c0 = slice(HD * h, HD * (h + 1))
                    ins = pe.matmul(J.bank("Us", b)[:, c0], kdx[0:NS, b, c0], vh[0:NS, NT, c0], start=True, stop=True)
                J.fills(ins, "Us", b)
            turn_heads(NT)

            J.wait_emptied(pe, "mkT", 4)
            J.wait_emptied(pe, "mq", 4)
            for h in range(MB + 1):
                if h < MB:
                    rr = slice(64 * (h % 2), 64 * (h % 2) + 64)
                    for i in range(NT):
                        J.wait_free(pe, "S", h, i)
                        ins = pe.matmul(J.bank("S", h, i)[:, 0:P * (i + 1)], mqT[rr, h // 2, tok(i)],
                                        mkT[rr, h // 2, 0:P * (i + 1)], start=True, stop=True)
                        J.fills(ins, "S", h, i)
                if h:
                    g = h - 1
                    for k in range(NT):
                        J.wait_free(pe, "PT", g, k)
                        for i in range(k, NT):
                            pe.wait_ge(s_prob, NT * g + i + 1)
                            ins = pe.transpose(J.bank("PT", g, k)[:, P * (i - k):P * (i - k + 1)],
                                               pb[g % 2][i][:, P * k:P * (k + 1)], ident[:, :])
                        J.fills(ins, "PT", g, k)
                    if h % 2 == 0:
                        c = h // 2 - 1
                        J.wait_free(pe, "OT", c)
                        J.wait_emptied(pe, "PT", g, NT - 1)
                        for par in range(2):
                            hh = 2 * c + par
                            for k in range(NT):
                                ins = pe.matmul(J.bank("OT", c)[64 * par:64 * par + 64, P * k:SEQ],
                                                mv[:, k, MD * hh:MD * (hh + 1)], pt[par][:, k, P * k:SEQ],
                                                start=(k == 0), stop=(k == NT - 1), skip_group_check=True)
                        J.fills(ins, "OT", c)

            def scores(g, b):
                if b % 4 == 0 and g:
                    pe.wait_ge(sc_free, g)
                J.wait_emptied(pe, "KT", b, 2)
                J.wait_emptied(pe, "KT", b, 3)
                q = slice(32 * (b % 4), 32 * (b % 4) + 32)
                for c in range(4):
                    ins = pe.matmul(psum[6][q, :], qxm[:, c, b, :], kT[b % 2][:, c, :], start=(c == 0), stop=(c == 3))
                ins.then_inc(sc_full, 1)

            for g in range(2):
                for b in range(4 * g, 4 * g + 4):
                    pe.wait_ge(k_in[b % 2], 16 * NPG * (b // 2 + 1))
                    for c in range(4):
                        J.wait_free(pe, "KT", b, c)
                        for j in range(NPG):
                            ins = pe.transpose(J.bank("KT", b, c)[:, P * j:P * (j + 1)], kbuf[b % 2][:, j, P * c:P * (c + 1)],
                                               ident[:, :])
                        J.fills(ins, "KT", b, c)
                    if b == 0:
                        pe.wait_ge(qx_done, 1)
                    if b > 4 * g:
                        scores(g, b - 1)
                scores(g, 4 * g + 3)
                J.wait_free(pe, "Sn", g)
                for b in range(4 * g, 4 * g + 4):
                    q = slice(32 * (b % 4), 32 * (b % 4) + 32)
                    for c in range(4):
                        ins = pe.matmul(J.bank("Sn", g)[q, 0:NS], qxm[:, c, b, :], mkT[:, c, SEQ:TOK], start=(c == 0), stop=(c == 3))
                J.fills(ins, "Sn", g)
                pe.wait_ge(ss_prob, g + 1)
                J.wait_free(pe, "Pt", g)
                for j in range(NPG):
                    ins = pe.transpose(J.bank("Pt", g)[:, P * j:P * (j + 1)], sx[:, P * j:P * (j + 1)], ident[:, :])
                J.fills(ins, "Pt", g)
                J.wait_free(pe, "Ptn", g)
                ins = pe.transpose(J.bank("Ptn", g)[0:NS, 0:P], sx[:, PAST:], ident[:, :])
                J.fills(ins, "Ptn", g)
                J.wait_free(pe, "Os", g)
                J.wait_emptied(pe, "Pt", g)
                J.wait_emptied(pe, "Ptn", g)
                pe.wait_ge(v_in, 16 * NPG * 4 * (g + 1))
                for b in range(4 * g, 4 * g + 4):
                    for h in range(MB):
                        par, c = h % 2, h // 2
                        out = J.bank("Os", g)[64 * par:64 * par + 64, 16 * c + NQ * (b % 4):16 * c + NQ * (b % 4 + 1)]
                        q = slice(32 * (b % 4) + NQ * h, 32 * (b % 4) + NQ * (h + 1))
                        for j in range(NPG):
                            pe.matmul(out, vbuf[b % 4][:, j, MD * h:MD * (h + 1)], ptS[:, j, q], start=(j == 0), stop=False)
                        ins = pe.matmul(out, mv[0:NS, NT, MD * h:MD * (h + 1)], ptn[0:NS, q], start=False, stop=True)
                J.fills(ins, "Os", g)

            J.wait_emptied(pe, "Os", 1)
            for half in range(2):
                w = weights(f"o{half}")
                for i, r in TILES:
                    rows_of(("x1", half, i), i, w, mixT)
            for i in range(MT):
                turn("memT", i, 5 + i, 6 + i)
            J.wait_emptied(pe, "memT", 1, 0)
            J.wait_emptied(pe, "memT", 1, 1)
            for n in range(4):
                w = weights(("xk0", "xk1", "xv0", "xv1")[n])
                for i in range(MT):
                    J.wait_free(pe, "mem", n, i)
                    for k in range(KC):
                        ins = pe.matmul(J.bank("mem", n, i), memT[:, k, P * i:P * (i + 1)], w[:, k, :], start=(k == 0), stop=(k == KC - 1))
                    J.fills(ins, "mem", n, i)
            for c in range(4):
                J.wait_free(pe, "memKT", c)
                J.wait_emptied(pe, "mem", 1, 0)
                J.wait_emptied(pe, "mem", 1, 1)
                for n in range(4):
                    k, i = 2 * c + n // 2, n % 2
                    ins = pe.transpose(J.bank("memKT", c)[:, P * n:P * (n + 1)], memk[:, i, P * k:P * (k + 1)], ident[:, :])
                J.fills(ins, "memKT", c)
            for i, r in TILES:
                turn("h2T", i, 7 + i, 8 + i)
            J.wait_emptied(pe, "h2T", NT, 0)
            J.wait_emptied(pe, "h2T", NT, 1)
            for half in range(2):
                features_out("xq", half)
            for c in range(5):
                J.wait_emptied(pe, "xq", 1, c)
            J.wait_emptied(pe, "memKT", 2)
            J.wait_emptied(pe, "memKT", 3)
            for h in range(XH + 1):
                if h < XH:
                    for i2 in range(2):
                        J.wait_free(pe, "XS", h, i2)
                        for u in range(2):
                            for c in range(2):
                                ins = pe.matmul(J.bank("XS", h, i2)[:, MEM * u:MEM * (u + 1)], qT[:, 2 * h + c, tok(2 * i2 + u)],
                                                memkT[:, 2 * h + c, :], start=(c == 0), stop=(c == 1))
                        J.fills(ins, "XS", h, i2)
                if h:
                    g = h - 1
                    for k in range(MT):
                        J.wait_free(pe, "XPT", g, k)
                        pe.wait_ge(xs_prob, NT * (g + 1))
                        for i in range(NT):
                            ins = pe.transpose(J.bank("XPT", g, k)[:, tok(i)], xp[g % 2][:, i, P * k:P * (k + 1)], ident[:, :])
                        J.fills(ins, "XPT", g, k)
                    J.wait_emptied(pe, "XPT", g, 1)
                    for c in range(2):
                        J.wait_free(pe, "XOT", g, c)
                        for k in range(MT):
                            ins = pe.matmul(J.bank("XOT", g, c), memv[:, k, P * (2 * g + c):P * (2 * g + c + 1)], xpt[g % 2][:, k, :],
                                            start=(k == 0), stop=(k == MT - 1))
                        J.fills(ins, "XOT", g, c)

            def xscores(g, b):
                if b % 4 == 0:
                    if g:
                        pe.wait_ge(xs_exp, g)
                    else:
                        pe.wait_ge(sc_free, 2)
                J.wait_emptied(pe, "XKT", b, 2)
                J.wait_emptied(pe, "XKT", b, 3)
                q = slice(32 * (b % 4), 32 * (b % 4) + 32)
                for c in range(KC):
                    ins = pe.matmul(psum[6][q, 0:MEM], qxx[:, c, b, :], xkT[b % 2][:, c, :], start=(c == 0), stop=(c == KC - 1))
                ins.then_inc(sc_full, 1)

            for g in range(2):
                for b in range(4 * g, 4 * g + 4):
                    pe.wait_ge(xk_in[b % 2], 16 * (b // 2 + 1))
                    for c in range(4):
                        J.wait_free(pe, "XKT", b, c)
                        for n in range(4):
                            k, i = 2 * c + n // 2, n % 2
                            ins = pe.transpose(J.bank("XKT", b, c)[:, P * n:P * (n + 1)], xkbuf[b % 2][:, i, P * k:P * (k + 1)], ident[:, :])
                        J.fills(ins, "XKT", b, c)
                    if b == 0:
                        pe.wait_ge(qx_done, 2)
                    if b > 4 * g:
                        xscores(g, b - 1)
                xscores(g, 4 * g + 3)
                pe.wait_ge(xs_prob, NT * XH + g + 1)
                J.wait_free(pe, "XPt", g)
                for j in range(MT):
                    ins = pe.transpose(J.bank("XPt", g)[:, P * j:P * (j + 1)], xsx[:, P * j:P * (j + 1)], ident[:, :])
                J.fills(ins, "XPt", g)
                J.wait_free(pe, "XOs", g)
                J.wait_emptied(pe, "XPt", g)
                pe.wait_ge(xv_in, 16 * 4 * (g + 1))
                for b in range(4 * g, 4 * g + 4):
                    for c in range(KC):
                        q = slice(32 * (b % 4) + NQ * (c // 2), 32 * (b % 4) + NQ * (c // 2 + 1))
                        for j in range(MT):
                            ins = pe.matmul(J.bank("XOs", g)[:, 16 * c + NQ * (b % 4):16 * c + NQ * (b % 4 + 1)],
                                            xvbuf[b % 4][:, j, P * c:P * (c + 1)], xptS[:, j, q], start=(j == 0), stop=(j == MT - 1))
                J.fills(ins, "XOs", g)
            J.wait_emptied(pe, "XOs", 1)
            for half in range(2):
                w = weights(f"xo{half}")
                for i, r in TILES:
                    rows_of(("x2", half, i), i, w, oT)
            for i, r in TILES:
                turn("h3T", i, 12 + i, 13 + i)
            J.wait_emptied(pe, "h3T", NT, 0)
            J.wait_emptied(pe, "h3T", NT, 1)
            pe.wait_ge(rtw_in, 64)
            wr = rt["wr"].rearrange("p (k n) -> p k n", k=KC)
            for i, r in TILES:
                J.wait_free(pe, "logit", i)
                for k in range(KC):
                    ins = pe.matmul(J.bank("logit", i)[0:r, 0:36], hT[:, k, tok(i)], wr[:, k, :], start=(k == 0), stop=(k == KC - 1))
                J.fills(ins, "logit", i)
            J.wait_free(pe, "rank")
            pe.wait_ge(onehots, 1)
            ms = rt["ms"].rearrange("p (i n) -> p i n", i=5)
            s = J.bank("rank")
            for i, r in TILES + [(5, P)]:
                for k, rr in TILES[:i + 1]:
                    lhs = before[0:rr, 0:r] if k == i else ones[0:rr, 0:r]
                    ins = pe.matmul(s[0:r, NE * i:NE * (i + 1)], lhs, ms[0:rr, k, :], start=(k == 0), stop=(k == min(i, NT)))
            J.fills(ins, "rank")
            J.wait_free(pe, "table")
            pe.wait_ge(onehots, 2)
            ohs = rt["ohs"].rearrange("p (a n) -> p a n", n=NBLK)
            ohr = rt["ohr"].rearrange("p (a n) -> p a n", n=CAP)
            for k in range(2):
                for i, r in TILES:
                    for u in range(2):
                        ins = pe.matmul(J.bank("table")[CAP * u:CAP * (u + 1), 0:NBLK // 2], ohr[0:r, 5 * k + i, :],
                                        ohs[0:r, 5 * k + i, :].rearrange("p (c u) -> p u c", u=2)[:, u, :],
                                        start=(k == 0 and i == 0), stop=(k == 1 and i == NT), skip_group_check=True)
            J.fills(ins, "table")

            pe.wait_ge(routed, 1)

            def pair(j):
                first = isinstance(j, int)
                pe.wait_ge(xg_in, 16 * j + 16)
                if not first:
                    pe.wait_ge(xt_free, 2 * j)
                for k in range(KC):
                    ins = pe.transpose(psum[k // 4][:, P * (k % 4):P * (k % 4 + 1)], xg[:, P * k:P * (k + 1)], ident[:, :])
                ins.then_inc(xt_full, 1)
                pe.wait_ge(xt_free, 2 * j + 2)
                for u in range(2):
                    e = 2 * j + u
                    if not first:
                        pe.wait_ge(up_free, 2 * j + (u - 1))
                    for q in range(4):
                        for m in range(2):
                            pe.wait_ge(wm_in[2 * q + m], 32 * j + 16 * (u + 1))
                            for kk in range(2):
                                k = 2 * q + kk
                                for half in range(2):
                                    ins = pe.matmul(psum[2 + 2 * u + m][CAP * half:CAP * (half + 1), :],
                                                    xT[:, k, CAP * u:CAP * (u + 1)],
                                                    ring[:, 2 * q + m, kk, 512 * half:512 * (half + 1)],
                                                    start=(k == 0), stop=(k == KC - 1), skip_group_check=True)
                            ins.then_inc(w_used, 1)
                    pe.wait_ge(up_free, 2 * j + (u + 1))
                    if not first or u:
                        pe.wait_ge(ht_free, 2 * j + u)
                    for c in range(4):
                        ins = pe.transpose(psum[6][:, P * c:P * (c + 1)], h2[u][:, P * c:P * (c + 1)], ident[:, :])
                    ins.then_inc(ht_full, 1)
                    pe.wait_ge(ht_free, 2 * j + (u + 1))
                    if not first or u:
                        pe.wait_ge(y_free, 2 * j + u)
                    for q in range(4):
                        pe.wait_ge(wm_in[8 + q], 32 * j + 16 * (u + 1))
                        for kk in range(2):
                            k = 2 * q + kk
                            for half in range(2):
                                ins = pe.matmul(psum[7][CAP * half:CAP * (half + 1), :],
                                                heT[u][:, k % 4, CAP * (k // 4):CAP * (k // 4 + 1)],
                                                ring[:, 8 + q, kk, 512 * half:512 * (half + 1)],
                                                start=(k == 0), stop=(k == KC - 1), skip_group_check=True)
                        ins.then_inc(w_used, 1)

            pair(0)
            with pe.Fori(1, NE // 2) as j:
                pair(j)
            n_ov = pe.value_load(ovi[0:1, 0:1], min_val=0, max_val=XBLK)
            with pe.If(n_ov > 0):
                with pe.Fori(NE // 2, NBLK // 2) as j:
                    with pe.If(2 * j - NE < n_ov):
                        pair(j)


INS = ["x_prompt", "x_sample", "state_hgrn", "cache_moba_k", "cache_moba_v", "cache_mem_k", "cache_mem_v", "page_table",
       "mem_prompt", "g_mix", "w_in", "hg_lb", "hg_norm", "w_out", "g_cross", "g_mem", "w_xq", "w_xk", "w_xv", "w_xo",
       "g_ffn", "w_grp", "b_grp", "w_exp", "b_exp", "w1", "w3", "w2", "g_final"]


def kernel(**inputs):
    import concourse.bacc as bacc
    from concourse.bass_utils import run_bass_kernel_spmd

    nc = bacc.Bacc("TRN2", target_bir_lowering=False, num_devices=1)
    arrays = {name: np.ascontiguousarray(inputs[name]) for name in INS}
    arrays["g_final"] = arrays["g_final"].reshape(1, D)
    arrays.update(constants())
    aps = {name: nc.dram_tensor(name, x.shape, mybir.dt.from_np(x.dtype), kind="ExternalInput").ap()
           for name, x in arrays.items()}
    for name, shape in OUTS:
        aps[name] = nc.dram_tensor(name, shape, F32, kind="ExternalOutput").ap()
    step_kernel(nc, aps)
    r = run_bass_kernel_spmd(nc, [arrays], core_ids=[0])
    return tuple(r.results[0][name] for name, _ in OUTS)
```

```python
from contextlib import ExitStack

import numpy as np

import concourse.bass as bass
from concourse import mybir

F32 = mybir.dt.float32
U32 = mybir.dt.uint32
I32 = mybir.dt.int32
ACT = mybir.ActivationFunctionType
ALU = mybir.AluOpType
AX = mybir.AxisListType.X

P = 128
D = 1024
KC = D // P
SEQ = 512
NT = SEQ // P
NB, NQ = 8, 4
NS = NB * NQ
TOK = SEQ + NS
TILES = [(i, P) for i in range(NT)] + [(NT, NS)]
HG, HD = 4, 128
CH, SUB = 32, 8
NCH = SEQ // CH
MB, MD = 8, 64
PAGE, NPG, NPHYS = 128, 4, 40
PAST = NPG * PAGE
XH, XD, MEM = 4, 256, 256
MT = MEM // P
NG, EPG = 4, 8
NE = NG * EPG
CAP = 64
XBLK = 16
NBLK = NE + XBLK
EPS = 1e-6
NEG = -1e30


def constants():
    p = np.arange(P)
    c = {}
    c["c_ident"] = np.eye(P)
    t = np.arange(SEQ)
    tt = t % P
    c["c_maskd"] = ((p[:, None] // SUB == tt[None] // SUB) & (p[:, None] <= tt[None]))
    off = np.zeros((P, 3, SEQ // CH, SUB))
    for j in range(1, CH // SUB):
        for ch in range(NCH):
            s0 = (ch % (P // CH)) * CH
            off[s0:s0 + j * SUB, j - 1, ch, :] = 1
    c["c_masko"] = off.reshape(P, 3 * SEQ // CH * SUB)
    r = np.arange(NS)
    ms = (r[:, None] // NQ == r[None] // NQ) & (r[:, None] <= r[None])
    c["c_masks"] = np.tile(ms, (1, HG))
    c["c_bsel"] = (r[:, None] // NQ == np.arange(NB)[None])
    scan = np.ones(TOK)
    scan[0:SEQ:CH] = 0
    scan[SEQ::NQ] = 0
    c["c_scan"] = np.broadcast_to(scan, (P, TOK))
    x = np.arange(SEQ + SEQ - P)[None] - p[:, None] - (SEQ - P)
    c["c_alibi"] = np.where(x <= 0, x, NEG)
    b, h, q = p // 32, (p % 32) // NQ, p % NQ
    slope = 2.0 ** (-(h + 1.0))
    sb = np.full((P, PAST + 2 * NS), NEG)
    sb[:, :PAST] = -slope[:, None] * (PAST + q[:, None] - np.arange(PAST)[None])
    for g in range(2):
        for k in range(NS):
            ok = (k // NQ == 4 * g + b) & (k % NQ <= q)
            sb[:, PAST + NS * g + k] = np.where(ok, -slope * (q - k % NQ), NEG)
    c["c_sbias"] = sb
    c["c_before"] = (p[:, None] < p[None])
    c["c_ones"] = np.ones((P, P))
    c["c_iota"] = np.broadcast_to(np.arange(P), (P, P))
    c["c_tokid"] = np.arange(5)[None] * P + p[:, None]
    c["c_steps"] = np.broadcast_to(CAP * np.arange(1, 9), (P, 8))
    return {k: np.ascontiguousarray(v, dtype=np.float32) for k, v in c.items()}


OUTS = [("y_prompt", (1, SEQ, D)), ("y_sample", (NB, NQ, D)), ("hg_prompt", (1, 1, HG, HD, HD)),
        ("mk_prompt", (1, 1, SEQ, MB, MD)), ("mv_prompt", (1, 1, SEQ, MB, MD)),
        ("xk_prompt", (1, 1, MEM, XH, XD)), ("xv_prompt", (1, 1, MEM, XH, XD)),
        ("hg_sample", (1, NB, HG, HD, HD)), ("mk_sample", (1, NB, NQ, MB, MD)),
        ("mv_sample", (1, NB, NQ, MB, MD))]

IN = {"hq": 0, "hf": 1, "hi": 2, "hg": 3, "mq": 4, "mk": 5, "mv": 6}
WBLOCKS = [("w_in", IN[n], n) for n in ("hf", "hq", "mk", "mq", "mv", "hi", "hg")] + \
          [("w_xk", 0, "xk0"), ("w_xk", 1, "xk1"), ("w_xv", 0, "xv0"), ("w_xv", 1, "xv1"),
           ("w_out", 0, "o0"), ("w_out", 1, "o1"), ("w_xq", 0, "xq0"), ("w_xq", 1, "xq1"),
           ("w_xo", 0, "xo0"), ("w_xo", 1, "xo1")]
WPOS = {n: i for i, (_, _, n) in enumerate(WBLOCKS)}


RING = 6


def plan_jobs():
    jobs = []

    def add(eng, *name):
        jobs.append((name, eng))

    def turned(what, tiles):
        for i, _ in tiles:
            add("A", what, i, 0)
            add("V", what, i, 1)

    def all_of(eng, what, numbers=range(5)):
        for n in numbers:
            add(eng, what, n)

    def weights_inside(h):
        add("V", "attd", h)
        add("V", "atto", h)

    turned("hT", TILES)
    add("A", "hf", "rows")
    all_of("A", "hf")
    add("A", "hq", "rows")
    all_of("V", "hq")
    all_of("A", "mk")
    add("A", "mq", "rows")
    all_of("A", "mq", [0])
    weights_inside(0)
    all_of("A", "mq", [1, 2, 3, 4])
    all_of("A", "mkT")
    weights_inside(1)
    all_of("A", "mv")
    all_of("A", "hi", [0])
    weights_inside(2)
    all_of("A", "hi", [1, 2, 3, 4])
    all_of("V", "hg", [0])
    weights_inside(3)
    all_of("V", "hg", [1, 2, 3, 4])
    all_of("A", "kdn", range(HG))
    all_of("A", "kds", range(HG))

    def moba_step(h):
        if h < MB:
            for i in range(NT):
                add("V", "S", h, i)
        if h:
            for k in range(NT):
                add("A", "PT", h - 1, k)
            if h % 2 == 0:
                add("A", "OT", h // 2 - 1)

    for i in range(NT):
        all_of("V", "U", range(4 * i, 4 * i + 4))
        moba_step(2 * i)
        add("V", "o", i)
        if i:
            add("A", "hgT", i - 1)
        moba_step(2 * i + 1)
    add("A", "hgT", NT - 1)
    moba_step(MB)
    add("V", "o", NT)
    all_of("V", "Us", range(NB))
    add("A", "hgT", NT)
    turned("memT", TILES[:MT])
    for n in range(4):
        for i in range(MT):
            add("AV"[i], "mem", n, i)
        if n == 1:
            for c in range(4):
                add("AV"[c % 2], "memKT", c)

    def keys_turned(what, b):
        for c in range(4):
            add("AV"[c % 2], what, b, c)

    for b in range(4):
        keys_turned("KT", b)
    add("V", "Sn", 0)
    keys_turned("KT", 4)
    add("A", "Pt", 0)
    add("V", "Ptn", 0)
    add("A", "Os", 0)
    keys_turned("KT", 5)
    add("V", "OsT", 0)
    for b in range(6, 8):
        keys_turned("KT", b)
    add("V", "Sn", 1)
    add("A", "Pt", 1)
    add("V", "Ptn", 1)
    add("A", "Os", 1)

    def summed(what, turn, samples):
        for i, _ in TILES:
            add("V", what, 0, i)
            if i == 0:
                for name in samples:
                    add("V", *name)
        for i, _ in TILES:
            add("V", what, 1, i)
            if i >= 2:
                turned(turn, TILES[i - 2:i - 1])
            if what == "x2" and i == NT:
                add("V", "logit", 0)
                add("V", "logit", 1)
        for i in (NT - 1, NT):
            turned(turn, TILES[i:i + 1])
            if what == "x2":
                add("V", "logit", i - 1)
        if what == "x2":
            add("V", "logit", NT)

    summed("x1", "h2T", [("OsT", 1)])
    for half in range(2):
        add("A", "xq", half, "rows")
        for c in range(5):
            add("AV"[c % 2], "xq", half, c)
    for h in range(XH + 1):
        if h < XH:
            for i in range(2):
                add("A", "XS", h, i)
        if h:
            for k in range(MT):
                add("V", "XPT", h - 1, k)
            for c in range(2):
                add("A", "XOT", h - 1, c)
    for b in range(4):
        keys_turned("XKT", b)
    keys_turned("XKT", 4)
    add("A", "XPt", 0)
    add("A", "XOs", 0, 0)
    add("V", "XOs", 0, 1)
    keys_turned("XKT", 5)
    add("V", "XOsT", 0, 0)
    add("V", "XOsT", 0, 1)
    for b in range(6, 8):
        keys_turned("XKT", b)
    add("A", "XPt", 1)
    add("A", "XOs", 1, 0)
    add("V", "XOs", 1, 1)
    summed("x2", "h3T", [("XOsT", 1, 0), ("XOsT", 1, 1)])
    add("V", "rank")
    add("V", "table")
    return jobs


class Banks:

    def __init__(self, nc, psum, sem):
        self.psum = psum
        self.jobs = plan_jobs()
        self.number, self.rank, seen = {}, {}, {"A": 0, "V": 0}
        for n, (name, eng) in enumerate(self.jobs):
            self.number[name] = n
            self.rank[name] = seen[eng]
            seen[eng] += 1
        assert len(self.number) == len(self.jobs)
        self.total = seen
        self.filled = sem("psum_filled")
        self.emptied = {"A": sem("act_emptied"), "V": sem("dve_emptied")}

    def bank(self, *name):
        return self.psum[self.number[name] % RING]

    def wait_filled(self, eng, *name):
        eng.wait_ge(self.filled, self.number[name] + 1)

    def wait_emptied(self, eng, *name):
        who = self.jobs[self.number[name]][1]
        eng.wait_ge(self.emptied[who], self.rank[name] + 1)

    def wait_free(self, pe, *name):
        n = self.number[name] - RING
        if n >= 0:
            self.wait_emptied(pe, *self.jobs[n][0])

    def fills(self, ins, *name):
        ins.then_inc(self.filled, 1)

    def empties(self, ins, *name):
        ins.then_inc(self.emptied[self.jobs[self.number[name]][1]], 1)


class Steps:

    def __init__(self, sem):
        self.sem, self.n = sem, 0

    def did(self, ins):
        ins.then_inc(self.sem, 1)
        self.n += 1
        return self.n

    def settle(self, eng):
        eng.wait_ge(self.sem, self.n)


def step_kernel(nc, a):
    with ExitStack() as ctx:
        def sb(name, shape, dt=F32):
            return ctx.enter_context(nc.sbuf_tensor(name, shape, dt))

        def sem(name):
            return ctx.enter_context(nc.semaphore(name))

        ring = sb("ring", [P, 12, 2, D])
        r_x = sb("r_x", [P, 5 * D])
        r_h = sb("r_h", [P, KC * TOK])
        r_mix = sb("r_mix", [P, KC * TOK])
        r_c = sb("r_c", [P, 16 * TOK])
        gain = sb("gain", [P, D])
        ident = sb("ident", [P, P])
        maskd = sb("maskd", [P, SEQ])
        masko = sb("masko", [P, 3 * P])
        masks = sb("masks", [NS, HG * NS])
        bsel = sb("bsel", [NS, NB])
        scan = sb("scan", [P, TOK])
        alibi = sb("alibi", [P, 2 * SEQ - P])
        sbias = sb("sbias", [P, PAST + 2 * NS])
        mvs = sb("mvs", [NS, 512])
        srows = sb("srows", [P, P])
        before = sb("before", [P, P])
        ones = sb("ones", [P, P])
        iota = sb("iota", [P, P])
        tokid = sb("tokid", [P, 5])
        steps = sb("steps", [P, 8])
        lbl = sb("lbl", [P, 2, HG])
        lb = sb("lb", [P, HG])
        omlb = sb("omlb", [P, HG])
        ghn = sb("ghn", [P, HD])
        ss = sb("ss", [P, 22])
        y0 = sb("y0", [P, 22])
        nt = sb("nt", [P, 4, 22])
        hss = sb("hss", [P, 5, HG])
        hy0 = sb("hy0", [P, 5, HG])
        hnt = sb("hnt", [P, 3, HG])
        dl = sb("dl", [P, HG, NCH + NB])
        stat = sb("stat", [P, 4, 2 * NT])
        table = sb("table", [P, NBLK // 2], U32)
        zeros = sb("zeros", [P, P])
        yidx = sb("yidx", [P, 2, 5], U32)
        ovi = sb("ovi", [1, 1 + XBLK], I32)
        gates = sb("gates", [P, 2, 5])
        psum_t = ctx.enter_context(nc.psum_tensor("psum", [P, 8, 512], F32))
        psum = [psum_t[:, n, :] for n in range(8)]
        tok_rows = nc.dram_tensor("tok_rows", [TOK, D], F32, kind="Internal").ap()
        out_rows = nc.dram_tensor("out_rows", [NBLK * CAP, D], F32, kind="Internal").ap()

        def part(buf, at, *shape):
            n = int(np.prod(shape))
            v = buf[:, at:at + n]
            if len(shape) == 1:
                return v
            names = "abcd"[:len(shape)]
            kw = {c: s for c, s in zip(names[1:], shape[1:])}
            return v.rearrange(f"p ({' '.join(names)}) -> p {' '.join(names)}", **kw)

        flat = ring[:, :, :, :].rearrange("p a b n -> p (a b n)")
        W0, KV, TAIL = 0, 8192, 16384
        wslot = [part(flat, W0 + 4096 * n, KC, 512) for n in range(2)]
        xr = part(r_x, 0, 5, D)
        hT = part(r_h, 0, KC, TOK)
        mixT = part(r_mix, 0, KC, TOK)
        hn = [part(r_c, D * n, D) for n in range(2)]
        qh = part(r_c, 0, HG, TOK)
        fk = part(r_c, 4 * TOK, HG, TOK)
        mqT = part(r_c, 8 * TOK, 4, TOK)
        mkT = part(r_c, 12 * TOK, 4, TOK)
        vh = part(flat, TAIL, 5, 512)
        gh = part(flat, TAIL + 2560, 5, 512)
        mv = part(flat, TAIL + 5120, NT, 512)
        kds = part(flat, TAIL + 7168, 512)
        mkn = part(r_mix, 0, 5, 512)
        qtmp = [part(r_mix, 2560 + 512 * n, 512) for n in range(2)]
        at = KV
        hgt = {}
        for name, n in (("lf", TOK), ("b", TOK), ("bc", TOK), ("ta", TOK), ("tb", TOK), ("qd", TOK), ("dec", TOK),
                        ("qo", 3 * P), ("k1", SEQ), ("k2", SEQ), ("k3", SEQ)):
            hgt[name] = part(flat, at, n)
            at += n
        assert at <= TAIL
        hgt["kd"] = hgt["bc"]
        kb = [hgt["k1"], hgt["k2"], hgt["k3"]]
        atts = sb("atts", [NS, HG * NS])
        att = part(r_x, 0, HG, SEQ)
        state = part(r_x, 2048, 6, HG, HD)
        kdn = part(r_h, 0, NT, HG, HD)
        on = [part(gain, 512 * n, 512) for n in range(2)]
        s0 = part(r_h, 0, NB, HG, HD)
        kdx = part(r_x, 0, NB, 512)
        qx = part(r_x, 4096, HG, NB * NS)
        pb = [[part(flat, KV + 512 * (4 * n + i), SEQ) for i in range(NT)] for n in range(2)]
        pt = [part(flat, KV + 4096 + 2048 * n, NT, SEQ) for n in range(2)]
        kbuf = [part(r_x, 2048 * n, NPG, 512) for n in range(2)]
        vbuf = [part(flat, KV + 2048 * n, NPG, 512) for n in range(4)]
        kT = [part(r_h, 2048 * n, 4, PAST) for n in range(2)]
        sx = part(r_c, 0, PAST + NS)
        ptS = part(r_c, TOK, NPG, P)
        ptn = part(r_c, TOK + 512, P)
        osb = part(r_c, TOK + 512 + P, 512)
        qxm = part(r_c, 4 * TOK, 4, NB, 32)
        memx = part(r_c, 4 * TOK, MT, D)
        memT = part(flat, TAIL, KC, MEM)
        memk = part(flat, TAIL + 2048, MT, D)
        memv = part(flat, TAIL + 4096, MT, D)
        memkT = part(flat, TAIL + 6144, KC, MEM)
        qT = part(r_c, 0, KC, TOK)
        oT = part(r_c, 8 * TOK, KC, TOK)
        xp = [part(r_mix, 1024 * n, NT, MEM) for n in range(2)]
        xpt = [part(r_mix, 2048 + 1024 * n, MT, SEQ) for n in range(2)]
        xkbuf = [part(flat, TAIL + 2048 * n, MT, D) for n in range(2)]
        xvbuf = [part(flat, KV + 2048 * n, MT, D) for n in range(4)]
        xkT = [part(r_h, 2048 * n, KC, MEM) for n in range(2)]
        xsx = part(r_mix, 0, MEM)
        xptS = part(r_mix, MEM, MT, P)
        xosb = part(r_mix, 2 * MEM, 2, 512)
        qxx = part(flat, TAIL + 6144, KC, NB, 32)
        rt = {}
        at = 0
        for name, n in (("lg", 5 * 36), ("g8", 40), ("m8", 40), ("i8f", 5), ("ohg", 20), ("ge", 20), ("gw", 5),
                        ("pr", 5 * 32), ("se", 40), ("me", 40), ("ek", 10), ("ex", 5), ("eid", 10),
                        ("m", 2 * 5 * 32), ("ms", 5 * 32), ("cnt", 32), ("big", 32 * 8), ("ovn", 32),
                        ("ove", 32), ("ovs", 32), ("tmp", 2 * 5 * 32), ("rk", 10), ("qk", 10), ("rr", 10),
                        ("ovk", 10), ("sk", 10), ("t1", 10), ("t2", 10), ("ohs", 2 * 5 * NBLK),
                        ("ohr", 2 * 5 * CAP), ("cmp", XBLK * 32), ("exs", XBLK), ("bias", 36), ("wr", KC * 36)):
            rt[name] = part(r_mix, at, n)
            at += n
        assert at <= KC * TOK
        i8 = sb("i8", [P, 5, 8], U32)
        xg = part(r_c, 0, D)
        xT = part(r_c, 2048, KC, P)
        he = [part(r_c, 3072 + 512 * n, 512) for n in range(2)]
        h2 = [part(r_c, 4096 + 512 * n, 512) for n in range(2)]
        heT = [part(r_c, 5120 + 512 * n, 4, P) for n in range(2)]
        ys = [part(r_c, 6144 + 512 * n, 512) for n in range(2)]
        yg = [[part(b, at, D) for b, at in pair] for pair in
              (((r_c, 0), (r_c, D)), ((r_c, 2 * D), (r_c, 3 * D)), ((r_c, 4 * D), (r_c, 5 * D)),
               ((r_c, 6 * D), (r_c, 7 * D)), ((r_h, 0), (r_h, D)))]

        J = Banks(nc, psum, sem)
        x_in = [sem(f"x{i}_in") for i in range(5)]
        gain0_in, gain_in = sem("gain0_in"), sem("gain_in")
        const_in = sem("const_in")
        page_in = sem("pages_in")
        w_in = [sem(f"wslot{n}_in") for n in range(2)]
        mem_in = sem("mem_in")
        s0_in = sem("s0_in")
        k_in = [sem(f"k{n}_in") for n in range(2)]
        v_in = sem("v_in")
        xk_in = [sem(f"xk{n}_in") for n in range(2)]
        xv_in = sem("xv_in")
        xr_in = sem("xr_in")
        rtw_in = sem("router_weights_in")
        rooted = sem("rooted")
        normed = sem("normed")
        exped = sem("exped")
        hgd, hga = sem("hg_exponents"), sem("hg_exps")
        zeroed = sem("zeroed")
        head_ready = sem("head_ready")
        o_root, o_normed = sem("o_root"), sem("o_normed")
        kdx_done = sem("kdx_done")
        s_max, s_exp, s_prob = sem("s_max"), sem("s_exp"), sem("s_prob")
        qx_done = sem("qx_done")
        sc_full, sc_free = sem("sample_scores_full"), sem("sample_scores_free")
        ss_max, ss_exp, ss_prob = sem("ss_max"), sem("ss_exp"), sem("ss_prob")
        xs_max, xs_exp, xs_prob = sem("xs_max"), sem("xs_exp"), sem("xs_prob")
        xr_new = sem("xr_new")
        r_exp_in, r_exp = sem("router_exp_in"), sem("router_exp")
        onehots, routed = sem("onehots"), sem("routed")
        rank_in = sem("rank_in")
        out_mk, out_mv, out_s, out_mem, out_s0 = (sem(f"out_{n}") for n in ("mk", "mv", "s", "mem", "s0"))
        rows_out = [sem(f"rows{n}_out") for n in range(2)]
        zeros_out = sem("zeros_out")
        a_step, v_step, p_step = sem("act_step"), sem("dve_step"), sem("pool_step")
        wm_in = [sem(f"moe_w{r}_in") for r in range(12)]
        w_used = sem("moe_w_used")
        xg_in = sem("xg_in")
        xt_full, xt_free = sem("xt_full"), sem("xt_free")
        up_exp, up_free = sem("up_exp"), sem("up_free")
        ht_full, ht_free = sem("ht_full"), sem("ht_free")
        y_free = sem("y_free")
        dve_moe = sem("dve_moe_steps")
        rows_in = [sem(f"out_rows{n}_in") for n in range(2)]
        moe_done, late_stored = sem("moe_done"), sem("late_stored")
        yg_in = [sem(f"yg{n}_in") for n in range(5)]
        fin_out = sem("fin_out")

        block = ctx.enter_context(nc.Block())
        CONSTS = [(ident, "c_ident"), (maskd, "c_maskd"), (masko, "c_masko"), (masks, "c_masks"),
                  (bsel, "c_bsel"), (scan, "c_scan"), (alibi, "c_alibi"), (sbias, "c_sbias"),
                  (before, "c_before"), (ones, "c_ones"), (iota, "c_iota"), (tokid, "c_tokid"),
                  (steps, "c_steps")]
        NCONST = 16 * (len(CONSTS) - 1 + 2)
        x_rows = a["x_prompt"].rearrange("b (i p) d -> p (b i) d", p=P)
        x_samp = a["x_sample"].rearrange("b t d -> (b t) d")
        y_rows = a["y_prompt"].rearrange("b (i p) d -> p (b i) d", p=P)
        y_samp = a["y_sample"].rearrange("b t d -> (b t) d")

        def rows(i):
            return P if i < NT else NS

        def tok(i):
            return slice(P * i, P * i + rows(i))

        last = {"hf": ("hf", 4), "hq": ("hq", 4), "mk": ("mk", 4), "mq": ("mq", 4), "mv": ("mv", 4),
                "hi": ("hi", 4), "hg": ("hg", 4)}
        for n in range(2):
            last[f"o{n}"] = ("x1", n, 4)
            last[f"xk{n}"] = ("mem", n, 1)
            last[f"xv{n}"] = ("mem", 2 + n, 1)
            last[f"xq{n}"] = ("xq", n, 4)
            last[f"xo{n}"] = ("x2", n, 4)

        w_moe = [a["w1"][0], a["w3"][0], a["w2"][0]]

        def moe_chunk(r, e):
            m, q = (r % 2, r // 2) if r < 8 else (2, r - 8)
            return w_moe[m][e][256 * q:256 * (q + 1), :].rearrange("(a p) n -> p a n", p=P)

        def load_pages(eng, dst, pool_name, b, s):
            for j in range(NPG):
                page = eng.value_load(a["page_table"][b:b + 1, j:j + 1], min_val=0, max_val=NPHYS - 1)
                src = a[pool_name][0][bass.ds(page, 1)].rearrange("a r h d -> (a r) (h d)")
                eng.dma_start(dst[:, j, :], src).then_inc(s, 16)

        @block.sync
        def _(sp):
            for i in range(NT):
                sp.dma_start(xr[:, i, :], x_rows[:, i, :]).then_inc(x_in[i], 16)
                if i == 0:
                    sp.dma_start(gain[:, :], a["g_mix"].to_broadcast([P, D])).then_inc(gain0_in, 16)
            sp.dma_start(xr[0:NS, NT, :], x_samp).then_inc(x_in[NT], 16)
            def weights(tag):
                n = WPOS[tag]
                name, col, _ = WBLOCKS[n]
                if n >= 2:
                    J.wait_filled(sp, *last[WBLOCKS[n - 2][2]])
                src = a[name][0].rearrange("(k p) n -> p k n", p=P)[:, :, 512 * col:512 * (col + 1)]
                sp.dma_start(wslot[n % 2], src).then_inc(w_in[n % 2], 16)

            def value_pages(g):
                for b in range(4 * g, 4 * g + 4):
                    load_pages(sp, vbuf[b % 4], "cache_moba_v", b, v_in)

            def mem_values(g):
                for b in range(4 * g, 4 * g + 4):
                    sp.dma_start(xvbuf[b % 4], a["cache_mem_v"][0][b].rearrange("(m p) h d -> p m (h d)", p=P))\
                        .then_inc(xv_in, 16)

            for tag in ("hf", "hq", "mk", "mq", "mv", "hi", "hg", "xk0", "xk1"):
                weights(tag)
            J.wait_filled(sp, "OT", 3)
            value_pages(0)
            for tag in ("xv0", "xv1", "o0", "o1"):
                weights(tag)
            J.wait_filled(sp, "Os", 0)
            value_pages(1)
            J.wait_filled(sp, "Os", 1)
            mem_values(0)
            for tag in ("xq0", "xq1", "xo0", "xo1"):
                weights(tag)
            J.wait_filled(sp, "XOs", 0, 1)
            mem_values(1)
            J.wait_filled(sp, "XOs", 1, 1)
            for r in range(4, 12):
                sp.dma_start(ring[:, r, :, :], moe_chunk(r, 0)).then_inc(wm_in[r], 16)
            for half in range(2):
                J.wait_filled(sp, "x2", half, NT)
                slot = WPOS[f"xo{half}"] % 2
                for r in (2 * slot, 2 * slot + 1):
                    sp.dma_start(ring[:, r, :, :], moe_chunk(r, 0)).then_inc(wm_in[r], 16)
            with sp.Fori(1, NE) as e:
                for r in range(12):
                    sp.wait_ge(w_used, 12 * e + (r - 11))
                    sp.dma_start(ring[:, r, :, :], moe_chunk(r, e)).then_inc(wm_in[r], 16)
            sp.wait_ge(routed, 1)
            n_ov = sp.value_load(ovi[0:1, 0:1], min_val=0, max_val=XBLK)
            with sp.If(n_ov > 0):
                with sp.Fori(0, XBLK // 2) as j:
                    with sp.If(2 * j < n_ov):
                        for u in range(2):
                            ex = sp.value_load(ovi[0:1, bass.ds(2 * j + (u + 1), 1)], min_val=0, max_val=NE - 1)
                            for r in range(12):
                                sp.wait_ge(w_used, 24 * j + (12 * (NE + u) + r - 11))
                                sp.dma_start(ring[:, r, :, :], moe_chunk(r, ex)).then_inc(wm_in[r], 16)
            for i, r in TILES:
                sp.wait_ge(normed, 18 + i)
                sp.dma_start(y_rows[:, i, :] if i < NT else y_samp, yg[i][0][0:r, :]).then_inc(fin_out, 16)
            sp.wait_ge(fin_out, 80)

        @block.gpsimd
        def _(pool):
            for buf, name in CONSTS[:8] + CONSTS[8:]:
                full = buf[:, :] if len(buf.shape) == 2 else buf[:, :, :].rearrange("p a b -> p (a b)")
                q = page_in if name == "c_ident" else const_in
                pool.dma_start(full, a[name]).then_inc(q, 16)
            pool.dma_start(lbl[:, :, :], a["hg_lb"].rearrange("l (h k) -> k l h", k=HD),
                           allow_slow_non_contiguous=True).then_inc(const_in, 16)
            pool.dma_start(ghn[:, :], a["hg_norm"].to_broadcast([P, HD])).then_inc(const_in, 16)
            pool.memset(zeros[:, :], 0.0).then_inc(p_step, 1)
            pool.wait_ge(p_step, 1)
            n = XBLK * CAP * D // P // P
            pool.dma_start(out_rows[NE * CAP:, :].rearrange("(p r) (c d) -> p (r c) d", p=P, d=P),
                           zeros[:, :].unsqueeze(1).to_broadcast([P, n, P])).then_inc(zeros_out, 16)
            pool.wait_ge(normed, 5)
            pool.memset(part(r_x, 0, 2048), 0.0).then_inc(zeroed, 1)
            pool.memset(part(flat, KV + 7 * TOK + 3 * P, 3 * SEQ), 0.0).then_inc(zeroed, 1)
            pool.memset(atts[:, :], 0.0).then_inc(zeroed, 1)
            J.wait_filled(pool, "kds", HG - 1)
            pool.dma_start(memx, a["mem_prompt"].rearrange("b (i p) d -> p (b i) d", p=P)).then_inc(mem_in, 16)
            J.wait_filled(pool, "U", NCH - 1)
            pool.dma_start(s0, a["state_hgrn"][0].rearrange("b h k v -> k b h v")).then_inc(s0_in, 16)
            J.wait_emptied(pool, "o", NT)
            J.wait_filled(pool, "hgT", NT)
            pool.dma_start(gain[:, :], a["g_mem"].to_broadcast([P, D])).then_inc(gain_in, 16)
            J.wait_emptied(pool, "Us", NB - 1)
            pool.dma_start(a["hg_sample"][0].rearrange("b h k v -> k b h v"), s0).then_inc(out_s0, 16)
            for b in range(2):
                load_pages(pool, kbuf[b], "cache_moba_k", b, k_in[b])
            pool.wait_ge(normed, 7)
            pool.dma_start(gain[:, :], a["g_cross"].to_broadcast([P, D])).then_inc(gain_in, 16)
            for b in range(2, NB):
                J.wait_filled(pool, "KT", b - 2, 3)
                load_pages(pool, kbuf[b % 2], "cache_moba_k", b, k_in[b % 2])
            J.wait_filled(pool, "KT", NB - 1, 3)
            pool.dma_start(xr[:, 0:NT, :], x_rows).then_inc(xr_in, 16)
            pool.dma_start(xr[0:NS, NT, :], x_samp).then_inc(xr_in, 16)
            J.wait_filled(pool, "mem", 3, 1)
            pool.wait_ge(out_mem, 32)
            for b in range(NB):
                if b >= 2:
                    if b == 2:
                        pool.wait_ge(normed, 12)
                        pool.dma_start(gain[:, :], a["g_ffn"].to_broadcast([P, D])).then_inc(gain_in, 16)
                    J.wait_filled(pool, "XKT", b - 2, 3)
                pool.dma_start(xkbuf[b % 2], a["cache_mem_k"][0][b].rearrange("(m p) h d -> p m (h d)", p=P))\
                    .then_inc(xk_in[b % 2], 16)
            J.wait_filled(pool, "XOsT", 1, 1)
            wr = rt["wr"].rearrange("p (k n) -> p k n", k=KC)
            pool.dma_start(wr[:, :, 0:NG], a["w_grp"][0].rearrange("(k p) n -> p k n", p=P)).then_inc(rtw_in, 16)
            pool.dma_start(wr[:, :, NG:36], a["w_exp"][0].rearrange("(k p) n -> p k n", p=P)).then_inc(rtw_in, 16)
            pool.dma_start(rt["bias"][:, 0:NG], a["b_grp"].to_broadcast([P, NG])).then_inc(rtw_in, 16)
            pool.dma_start(rt["bias"][:, NG:36], a["b_exp"].to_broadcast([P, NE])).then_inc(rtw_in, 16)
            pool.wait_ge(normed, 17)
            pool.dma_start(gain[:, :], a["g_final"].to_broadcast([P, D])).then_inc(gain_in, 16)

            pool.wait_ge(routed, 1)
            pool.wait_ge(rows_out[0], 48)
            pool.wait_ge(rows_out[1], 32)

            def gather(c):
                if c:
                    pool.wait_ge(xt_full, c)
                pool.indirect_dma_start(xg, None, tok_rows, bass.IndirectOffsetOnAxis(ap=table[:, c:c + 1], axis=0))\
                    .then_inc(xg_in, 16)

            for c in range(NE // 2):
                gather(c)
            n_ov = pool.value_load(ovi[0:1, 0:1], min_val=0, max_val=XBLK)
            for c in range(NE // 2, NBLK // 2):
                with pool.If(n_ov > 2 * c - NE):
                    gather(c)
            pool.wait_ge(moe_done, 1)
            for n in range(2):
                pool.wait_ge(rows_in[n], 32 * NE // 2)
            for i, r in TILES:
                for k in range(2):
                    pool.indirect_dma_start(yg[i][k][0:r, :], None, out_rows,
                                            bass.IndirectOffsetOnAxis(ap=yidx[0:r, k, i:i + 1], axis=0))\
                        .then_inc(yg_in[i], 16)

        @block.scalar
        def _(act):
            st = Steps(a_step)

            def rstd_root(n, src, width, out_junk):
                r = src.shape[0]
                st.did(act.activation(out_junk, src, ACT.Square, accum_out=ss[0:r, n:n + 1]))
                st.settle(act)
                act.activation(y0[0:r, n:n + 1], ss[0:r, n:n + 1], ACT.Sqrt, scale=1.0 / width, bias=EPS)\
                    .then_inc(rooted, 1)

            def norm_root(n, src):
                r = src.shape[0]
                rstd_root(n, src, D, hn[n % 2][0:r, :])

            def evac(out, *name, view=None):
                J.wait_filled(act, *name)
                src = J.bank(*name)
                J.empties(act.activation(out, view(src) if view else src, ACT.Copy), *name)

            def sample_rows(*what):
                evac(srows[:, :], *what, "rows", view=lambda s: s[:, 0:P])

            for i, r in TILES:
                act.wait_ge(x_in[i], 16)
                if i >= 2:
                    J.wait_filled(act, "hT", i - 2, 1)
                norm_root(i, xr[0:r, i, :])
                evac(hT[:, 0:4, tok(i)], "hT", i, 0,
                     view=lambda s, r=r: s.rearrange("p (k t) -> p k t", k=4)[:, :, 0:r])
            sample_rows("hf")
            for c in range(5):
                J.wait_filled(act, "hf", c)
                s = J.bank("hf", c)
                if c < 4:
                    J.empties(act.activation(fk[:, c, 0:SEQ], s, ACT.Exp, scale=-1.0), "hf", c)
                else:
                    J.empties(act.activation(fk[:, :, SEQ:TOK], s[:, 0:128].rearrange("p (c t) -> p c t", c=4),
                                             ACT.Exp, scale=-1.0), "hf", c)
            sample_rows("hq")
            for c in range(5):
                J.wait_filled(act, "hq", c)
                if c >= 2:
                    J.wait_emptied(act, "hq", c - 2)
                n = SEQ if c < 4 else 128
                act.activation(qtmp[c % 2][:, 0:n], J.bank("hq", c)[:, 0:n], ACT.Exp, scale=-1.0).then_inc(exped, 1)
            act.wait_ge(hgd, 1)
            act.activation(lb[:, :], lb[:, :], ACT.Exp).then_inc(hga, 1)

            def head_exps(h):
                act.wait_ge(hgd, 2 * h + 2)
                act.activation(hgt["lf"], fk[:, h, :], ACT.Ln).then_inc(hga, 1)
                act.wait_ge(hgd, 2 * h + 3)
                b3 = hgt["b"][:, 0:SEQ].rearrange("p (c t) -> p c t", t=CH)
                bs = hgt["b"][:, SEQ:TOK].rearrange("p (c t) -> p c t", t=NQ)
                act.activation(hgt["tb"], hgt["ta"], ACT.Exp).then_inc(hga, 1)
                act.activation(hgt["bc"], hgt["ta"], ACT.Exp, scale=-1.0).then_inc(hga, 1)
                act.activation(hgt["qo"], hgt["qo"], ACT.Exp).then_inc(hga, 1)
                for j in range(3):
                    v = kb[j].rearrange("p (c t) -> p c t", t=CH)[:, :, 0:SUB * (j + 1)]
                    act.activation(v, v, ACT.Exp).then_inc(hga, 1)
                act.activation(hgt["dec"], hgt["dec"], ACT.Exp).then_inc(hga, 1)
                act.activation(dl[:, h, 0:NCH], b3[:, :, CH - 1], ACT.Exp).then_inc(hga, 1)
                act.activation(dl[:, h, NCH:NCH + NB], bs[:, :, NQ - 1], ACT.Exp).then_inc(hga, 1)
                act.activation(hgt["lf"], hgt["b"], ACT.Exp).then_inc(hga, 1)

            def rows_evac(dst, what, i):
                if i < NT:
                    evac(dst, what, i)
                    return
                J.wait_filled(act, what, i)
                for n in range(4):
                    ins = act.activation(dst[0:NS, P * n:P * (n + 1)], J.bank(what, i)[NS * n:NS * (n + 1), 0:P], ACT.Copy)
                J.empties(ins, what, i)

            for i, r in TILES:
                rows_evac(mkn[:, i, :], "mk", i)
                if i == 1:
                    head_exps(0)
            J.wait_emptied(act, "mk", NT)
            act.dma_start(a["mk_prompt"][0, 0].rearrange("(i p) h d -> p i (h d)", p=P), mkn[:, 0:NT, :]).then_inc(out_mk, 16)
            act.dma_start(a["mk_sample"][0].rearrange("b t h d -> (b t) (h d)"), mkn[0:NS, NT, :]).then_inc(out_mk, 16)
            sample_rows("mq")
            for c in range(5):
                J.wait_filled(act, "mq", c)
                s = J.bank("mq", c)
                if c < 4:
                    ins = act.activation(mqT[:, c, 0:SEQ], s, ACT.Copy, scale=MD ** -0.5)
                else:
                    ins = act.activation(mqT[:, :, SEQ:TOK], s[:, 0:128].rearrange("p (c t) -> p c t", c=4),
                                         ACT.Copy, scale=MD ** -0.5)
                J.empties(ins, "mq", c)
                if c == 2:
                    head_exps(1)
            for c in range(5):
                if c < 4:
                    evac(mkT[:, c, 0:SEQ], "mkT", c)
                else:
                    evac(mkT[:, :, SEQ:TOK], "mkT", c, view=lambda s: s[:, 0:128].rearrange("p (c t) -> p c t", c=4))
            for i, r in TILES:
                rows_evac(mv[:, i, :] if i < NT else mvs, "mv", i)
                if i == 1:
                    head_exps(2)
            J.wait_emptied(act, "mv", NT)
            act.dma_start(a["mv_prompt"][0, 0].rearrange("(i p) h d -> p i (h d)", p=P), mv).then_inc(out_mv, 16)
            act.dma_start(a["mv_sample"][0].rearrange("b t h d -> (b t) (h d)"), mvs[:, :]).then_inc(out_mv, 16)
            for i, r in TILES:
                rows_evac(vh[:, i, :], "hi", i)
                if i == 2:
                    head_exps(3)
            for i, r in TILES:
                J.wait_filled(act, "hg", i)
                if i < NT:
                    ins = act.activation(gh[:, i, :], J.bank("hg", i), ACT.Exp, scale=-1.0)
                else:
                    for n in range(4):
                        ins = act.activation(gh[0:NS, i, P * n:P * (n + 1)], J.bank("hg", i)[NS * n:NS * (n + 1), 0:P],
                                             ACT.Exp, scale=-1.0)
                ins.then_inc(exped, 1)
            for h in range(HG):
                evac(kdn[:, :, h, :], "kdn", h, view=lambda s: s.rearrange("p (i k) -> p i k", i=NT))
            for h in range(HG):
                evac(kds[0:NS, HD * h:HD * (h + 1)], "kds", h, view=lambda s: s[0:NS, 0:HD])

            def head_roots(i):
                r = rows(i)
                J.wait_filled(act, "o", i)
                if i >= 2:
                    J.wait_filled(act, "hgT", i - 2)
                src = J.bank("o", i)
                for h in range(HG):
                    st.did(act.activation(on[i % 2][0:r, HD * h:HD * (h + 1)], src[0:r, HD * h:HD * (h + 1)],
                                          ACT.Square, accum_out=hss[0:r, i, h:h + 1]))
                st.settle(act)
                act.activation(hy0[0:r, i, :], hss[0:r, i, :], ACT.Sqrt, scale=1.0 / HD, bias=EPS).then_inc(o_root, 1)

            def turn_heads(i):
                evac(mixT[:, 0:HG, tok(i)], "hgT", i,
                     view=lambda s: s.rearrange("p (h t) -> p h t", h=HG)[:, :, 0:rows(i)])

            def moba_step(h):
                if h < MB:
                    for i in range(NT):
                        n = NT * h + i
                        act.wait_ge(s_max, n + 1)
                        p = pb[h % 2][i][:, 0:P * (i + 1)]
                        act.activation(p, p, ACT.Exp, bias=stat[:, 1, n % 8:n % 8 + 1],
                                       accum_out=stat[:, 2, n % 8:n % 8 + 1]).then_inc(s_exp, 1)
                if h:
                    for k in range(NT):
                        if h > 2:
                            J.wait_filled(act, "OT", (h - 3) // 2)
                        evac(pt[(h - 1) % 2][:, k, P * k:SEQ], "PT", h - 1, k, view=lambda s: s[:, 0:SEQ - P * k])
                    if h % 2 == 0:
                        evac(mixT[:, 4 + h // 2 - 1, 0:SEQ], "OT", h // 2 - 1)

            act.wait_ge(out_mk, 32)
            J.wait_emptied(act, "hq", 4)
            for i in range(NT):
                moba_step(2 * i)
                head_roots(i)
                if i:
                    turn_heads(i - 1)
                moba_step(2 * i + 1)
            J.wait_emptied(act, "U", NCH - 1)
            act.dma_start(a["hg_prompt"][0, 0].rearrange("h k v -> k h v"), state[:, NCH % 6, :, :]).then_inc(out_s, 16)
            turn_heads(NT - 1)
            moba_step(MB)
            head_roots(NT)
            turn_heads(NT)

            act.wait_ge(mem_in, 16)
            for i in range(MT):
                norm_root(5 + i, memx[:, i, :])
            for i in range(MT):
                evac(memT[:, 0:4, P * i:P * (i + 1)], "memT", i, 0, view=lambda s: s.rearrange("p (k t) -> p k t", k=4))
            act.wait_ge(out_mv, 32)
            for n in range(4):
                dst = (memk, memv)[n // 2]
                evac(dst[:, 0, 512 * (n % 2):512 * (n % 2 + 1)], "mem", n, 0)
                if n == 1:
                    for c in (0, 2):
                        evac(memkT[:, 2 * c:2 * c + 2, :], "memKT", c, view=lambda s: s.rearrange("p (k t) -> p k t", k=2))
                if n % 2:
                    J.wait_emptied(act, "mem", n, 0)
                    J.wait_emptied(act, "mem", n, 1)
                    out = a[("xk_prompt", "xv_prompt")[n // 2]][0, 0].rearrange("(i p) h d -> p i (h d)", p=P)
                    act.dma_start(out, dst).then_inc(out_mem, 16)

            def keys_turned(b):
                if b >= 2:
                    act.wait_ge(sc_full, b // 2)
                else:
                    act.wait_ge(out_s0, 16)
                for c in (0, 2):
                    evac(kT[b % 2][:, c, :], "KT", b, c)

            def sample_exps(g):
                act.wait_ge(ss_max, g + 1)
                act.activation(sx, sx, ACT.Exp, bias=stat[:, 1, 0:1], accum_out=stat[:, 2, 0:1]).then_inc(ss_exp, 1)

            def sample_probs(g):
                if g:
                    J.wait_filled(act, "Os", g - 1)
                evac(ptS, "Pt", g, view=lambda s: s.rearrange("p (j n) -> p j n", j=NPG))

            def sample_out(g):
                if g:
                    J.wait_filled(act, "OsT", g - 1)
                evac(osb, "Os", g)

            for b in range(4):
                keys_turned(b)
            sample_exps(0)
            keys_turned(4)
            sample_probs(0)
            sample_out(0)
            keys_turned(5)
            keys_turned(6)
            keys_turned(7)
            sample_exps(1)
            sample_probs(1)
            sample_out(1)

            def turned(what, i):
                evac(hT[:, 0:4, tok(i)], what, i, 0,
                     view=lambda s: s.rearrange("p (k t) -> p k t", k=4)[:, :, 0:rows(i)])

            for i, r in TILES:
                if i >= 2:
                    turned("h2T", i - 2)
                    J.wait_filled(act, "h2T", i - 2, 1)
                J.wait_emptied(act, "x1", 1, i)
                norm_root(7 + i, xr[0:r, i, :])
            for i in range(3, 5):
                turned("h2T", i)

            def scaled_q(half, c):
                J.wait_filled(act, "xq", half, c)
                s = J.bank("xq", half, c)
                if c < 4:
                    ins = act.activation(qT[:, 4 * half + c, 0:SEQ], s, ACT.Copy, scale=XD ** -0.5)
                else:
                    ins = act.activation(qT[:, 4 * half:4 * half + 4, SEQ:TOK],
                                         s[:, 0:128].rearrange("p (c t) -> p c t", c=4), ACT.Copy, scale=XD ** -0.5)
                J.empties(ins, "xq", half, c)

            for half in range(2):
                sample_rows("xq", half)
                for c in (0, 2, 4):
                    scaled_q(half, c)
            act.wait_ge(out_mem, 32)
            for h in range(XH + 1):
                if h < XH:
                    for i2 in range(2):
                        act.wait_ge(xs_max, 2 * h + i2 + 1)
                        s = J.bank("XS", h, i2)
                        for u in range(2):
                            n = (2 * i2 + u) + 4 * (h % 2)
                            ins = act.activation(xp[h % 2][:, 2 * i2 + u, :], s[:, MEM * u:MEM * (u + 1)], ACT.Exp,
                                                 bias=stat[:, 1, n:n + 1], accum_out=stat[:, 2, n:n + 1])
                            if u == 0:
                                st.did(ins)
                        J.empties(ins, "XS", h, i2)
                if h:
                    for c in range(2):
                        evac(oT[:, 2 * (h - 1) + c, 0:SEQ], "XOT", h - 1, c)

            def mem_keys_turned(b):
                if b >= 2:
                    act.wait_ge(sc_full, NB // 2 + b // 2)
                for c in (0, 2):
                    evac(xkT[b % 2][:, 2 * c:2 * c + 2, :], "XKT", b, c, view=lambda s: s.rearrange("p (k t) -> p k t", k=2))

            def mem_exps(g):
                act.wait_ge(xs_max, 2 * XH + g + 1)
                act.activation(xsx, psum[6][:, 0:MEM], ACT.Exp, bias=stat[:, 1, 0:1], accum_out=stat[:, 2, 0:1])\
                    .then_inc(xs_exp, 1)

            def mem_probs(g):
                if g:
                    J.wait_filled(act, "XOs", g - 1, 1)
                evac(xptS, "XPt", g, view=lambda s: s[:, 0:MT * P].rearrange("p (j n) -> p j n", j=MT))

            def mem_out(g):
                if g:
                    J.wait_filled(act, "XOsT", g - 1, 0)
                evac(xosb[:, 0, :], "XOs", g, 0)

            for b in range(4):
                mem_keys_turned(b)
            mem_exps(0)
            mem_keys_turned(4)
            mem_probs(0)
            mem_out(0)
            mem_keys_turned(5)
            mem_keys_turned(6)
            mem_keys_turned(7)
            mem_exps(1)
            mem_probs(1)
            mem_out(1)

            def stored_and_turned(i):
                act.wait_ge(normed, 13 + i)
                act.dma_start(tok_rows[P * i:P * i + rows(i), :], hn[i % 2][0:rows(i), :]).then_inc(rows_out[i % 2], 16)
                turned("h3T", i)

            for i, r in TILES:
                if i >= 2:
                    stored_and_turned(i - 2)
                    J.wait_filled(act, "h3T", i - 2, 1)
                    act.wait_ge(rows_out[i % 2], 16 * (i // 2))
                J.wait_emptied(act, "x2", 1, i)
                norm_root(12 + i, xr[0:r, i, :])
            for i in range(3, 5):
                stored_and_turned(i)
            act.wait_ge(r_exp_in, 1)
            act.activation(rt["ge"], rt["ge"], ACT.Exp).then_inc(r_exp, 1)
            act.wait_ge(r_exp_in, 2)
            act.activation(rt["ex"], rt["ex"], ACT.Exp).then_inc(r_exp, 1)

            def pair(j):
                first = isinstance(j, int)
                act.wait_ge(xt_full, j + 1)
                act.activation(xT[:, 4:8, :], psum[1].rearrange("p (k t) -> p k t", k=4), ACT.Copy).then_inc(xt_free, 1)
                for u in range(2):
                    act.wait_ge(w_used, 24 * j + (12 * u + 8))
                    if not first:
                        act.wait_ge(up_free, 2 * j + (u - 1))
                    act.activation(he[u], psum[2 + 2 * u], ACT.Exp, scale=-1.0).then_inc(up_exp, 1)
                    act.wait_ge(ht_full, 2 * j + (u + 1))
                    act.activation(heT[u].rearrange("p c t -> p (c t)"), psum[6], ACT.Copy).then_inc(ht_free, 1)
                    act.wait_ge(w_used, 24 * j + (12 * u + 12))
                    if not first:
                        act.wait_ge(rows_in[u], 32 * j)
                    act.activation(ys[u], psum[7], ACT.Copy).then_inc(y_free, 1)
                    act.wait_ge(y_free, 2 * j + (u + 1))
                    for half in range(2):
                        act.dma_start(out_rows[bass.ds(CAP * (2 * j + u), CAP), 512 * half:512 * (half + 1)],
                                      ys[u][CAP * half:CAP * (half + 1), :]).then_inc(rows_in[u], 16)

            pair(0)
            with act.Fori(1, NE // 2) as j:
                pair(j)
            act.wait_ge(zeros_out, 16)
            n_ov = act.value_load(ovi[0:1, 0:1], min_val=0, max_val=XBLK)
            with act.If(n_ov > 0):
                with act.Fori(NE // 2, NBLK // 2) as j:
                    with act.If(2 * j - NE < n_ov):
                        pair(j)
                        for u in range(2):
                            act.wait_ge(rows_in[u], 32 * j + 32)
                        act.activation(nt[0:1, 3, bass.ds(j - NE // 2, 1)], ss[0:1, 0:1], ACT.Copy).then_inc(late_stored, 1)
            act.activation(nt[0:1, 3, 21:22], ss[0:1, 0:1], ACT.Copy).then_inc(moe_done, 1)
            for i, r in TILES:
                act.wait_ge(xr_new, i + 1)
                rstd_root(17 + i, xr[0:r, i, :], D, yg[i][0][0:r, :])
            act.wait_ge(out_mk, 32)
            act.wait_ge(out_mv, 32)
            act.wait_ge(out_s, 16)
            act.wait_ge(out_mem, 32)
            act.wait_ge(out_s0, 16)

        @block.vector
        def _(dve):
            st = Steps(v_step)

            def v(ins):
                st.did(ins)
                st.settle(dve)

            def evac(out, *name, view=None):
                J.wait_filled(dve, *name)
                src = J.bank(*name)
                J.empties(dve.tensor_copy(out, view(src) if view else src), *name)

            def refined(root, mean_src, width, tmp, cols):
                v(dve.reciprocal(root, root))
                v(dve.tensor_scalar(tmp[0], mean_src, 1.0 / width, EPS, ALU.mult, ALU.add))
                v(dve.tensor_tensor(tmp[1], tmp[0], root, ALU.mult))
                v(dve.tensor_tensor(tmp[1], tmp[1], root, ALU.mult))
                v(dve.tensor_scalar(tmp[1], tmp[1], -0.5, 1.5, ALU.mult, ALU.add))
                v(dve.tensor_tensor(tmp[2], tmp[1], root, ALU.mult))
                return tmp[2]

            def norm_scale(n, src, out):
                r = src.shape[0]
                dve.wait_ge(rooted, n + 1)
                y = refined(y0[0:r, n:n + 1], ss[0:r, n:n + 1], D, [nt[0:r, k, n:n + 1] for k in range(3)], 1)
                dve.scalar_tensor_tensor(out=out, in0=src, scalar=y, in1=gain[0:r, :], op0=ALU.mult, op1=ALU.mult)\
                    .then_inc(normed, 1)

            dve.wait_ge(gain0_in, 16)
            for i, r in TILES:
                norm_scale(i, xr[0:r, i, :], hn[i % 2][0:r, :])
                evac(hT[:, 4:8, tok(i)], "hT", i, 1, view=lambda s, r=r: s.rearrange("p (k t) -> p k t", k=4)[:, :, 0:r])
            dve.wait_ge(const_in, NCONST)
            dve.tensor_tensor(lb[:, :], lbl[:, 1, :], lbl[:, 0, :], ALU.subtract).then_inc(hgd, 1)
            for c in range(5):
                dve.wait_ge(exped, c + 1)
                n = SEQ if c < 4 else 128
                t = qtmp[c % 2][:, 0:n]
                v(dve.tensor_scalar(t, t, 1.0, None, ALU.add))
                v(dve.reciprocal(t, t))
                s = J.bank("hq", c)
                if c < 4:
                    ins = dve.tensor_tensor(qh[:, c, 0:SEQ], s, t, ALU.mult)
                else:
                    ins = dve.tensor_tensor(qh[:, :, SEQ:TOK], s[:, 0:n].rearrange("p (c t) -> p c t", c=4),
                                            t.rearrange("p (c t) -> p c t", c=4), ALU.mult)
                J.empties(ins, "hq", c)
            dve.wait_ge(hga, 1)
            v(dve.tensor_scalar(lb[:, :], lb[:, :], 1.0, None, ALU.add))
            v(dve.reciprocal(lb[:, :], lb[:, :]))
            v(dve.tensor_scalar(omlb[:, :], lb[:, :], -1.0, 1.0, ALU.mult, ALU.add))
            J.wait_emptied(dve, "hf", 4)
            allf = fk.rearrange("p h t -> p (h t)")
            v(dve.tensor_scalar(allf, allf, 1.0, None, ALU.add))
            v(dve.reciprocal(allf, allf))
            dve.wait_ge(zeroed, 3)
            t = hgt

            def cut(x, size, lo, hi):
                return x[:, lo:hi].rearrange("p (c t) -> p c t", t=size)

            def decayed(h):
                f = fk[:, h, :]
                dve.tensor_scalar(f, f, omlb[:, h:h + 1], lb[:, h:h + 1], ALU.mult, ALU.add).then_inc(hgd, 1)
                dve.wait_ge(hga, 11 * h + 2)
                st.did(dve.tensor_scalar(f, f, -1.0, 1.0, ALU.mult, ALU.add))
                st.did(dve.tensor_scalar(t["tb"], t["lf"], -21.0, None, ALU.max))
                v(dve.tensor_tensor_scan(t["b"], scan[:, :], t["lf"], 0.0, ALU.mult, ALU.add))
                v(dve.tensor_tensor_scan(t["bc"], scan[:, :], t["tb"], 0.0, ALU.mult, ALU.add))
                b8 = cut(t["bc"], SUB, 0, SEQ)
                st.did(dve.tensor_tensor(cut(t["ta"], SUB, 0, SEQ), b8,
                                         b8[:, :, 3:4].to_broadcast([P, SEQ // SUB, SUB]), ALU.subtract))
                b4 = cut(t["bc"], NQ, SEQ, TOK)
                st.did(dve.tensor_tensor(cut(t["ta"], NQ, SEQ, TOK), b4,
                                         b4[:, :, 1:2].to_broadcast([P, NB, NQ]), ALU.subtract))
                bj = t["b"][:, 0:SEQ].rearrange("p (c j u) -> p j c u", j=CH // SUB, u=SUB)
                qo = t["qo"].rearrange("p (j c u) -> p j c u", j=3, u=SUB)
                for j in range(3):
                    st.did(dve.tensor_tensor(qo[:, j], bj[:, j + 1],
                                             bj[:, j, :, SUB - 1:SUB].to_broadcast([P, NCH, SUB]), ALU.subtract))
                b32 = cut(t["b"], CH, 0, SEQ)
                for j in range(3):
                    n = SUB * (j + 1)
                    st.did(dve.tensor_tensor(kb[j].rearrange("p (c t) -> p c t", t=CH)[:, :, 0:n],
                                             b32[:, :, n - 1:n].to_broadcast([P, NCH, n]), b32[:, :, 0:n], ALU.subtract))
                st.did(dve.tensor_tensor(cut(t["dec"], CH, 0, SEQ), b32[:, :, CH - 1:CH].to_broadcast([P, NCH, CH]),
                                         b32, ALU.subtract))
                bs = cut(t["b"], NQ, SEQ, TOK)
                dve.tensor_tensor(cut(t["dec"], NQ, SEQ, TOK), bs[:, :, NQ - 1:NQ].to_broadcast([P, NB, NQ]),
                                  bs, ALU.subtract).then_inc(hgd, 1)
                q, k = qh[:, h, :], fk[:, h, :]
                dve.wait_ge(hga, 11 * h + 12)
                st.did(dve.tensor_tensor(t["qd"], q, t["tb"], ALU.mult))
                st.did(dve.tensor_tensor(t["kd"], k, t["bc"], ALU.mult))
                q3 = q[:, 0:SEQ].rearrange("p (c j u) -> p j c u", j=CH // SUB, u=SUB)
                k32 = cut(k, CH, 0, SEQ)
                for j in range(3):
                    st.did(dve.tensor_tensor(qo[:, j], qo[:, j], q3[:, j + 1], ALU.mult))
                    kv = kb[j].rearrange("p (c t) -> p c t", t=CH)[:, :, 0:SUB * (j + 1)]
                    st.did(dve.tensor_tensor(kv, kv, k32[:, :, 0:SUB * (j + 1)], ALU.mult))
                st.settle(dve)
                st.did(dve.tensor_tensor(k, t["dec"], k, ALU.mult))
                dve.tensor_tensor(q, q, t["lf"], ALU.mult).then_inc(head_ready, 1)

            def weights_inside(h):
                J.wait_filled(dve, "attd", h)
                J.empties(dve.copy_predicated(att[:, h, :], maskd[:, :].bitcast(U32), J.bank("attd", h)), "attd", h)
                J.wait_filled(dve, "atto", h)
                J.wait_emptied(dve, "attd", h)
                s = J.bank("atto", h)
                a4 = att[:, h, :].rearrange("p (c j u) -> p j c u", j=CH // SUB, u=SUB)
                for j in range(3):
                    st.did(dve.copy_predicated(a4[:, j + 1], masko[:, P * j:P * (j + 1)].bitcast(U32)
                                               .rearrange("p (c u) -> p c u", u=SUB),
                                               s[:, P * j:P * (j + 1)].rearrange("p (c u) -> p c u", u=SUB)))
                J.empties(dve.copy_predicated(atts[0:NS, NS * h:NS * (h + 1)],
                                              masks[:, 0:NS].bitcast(U32), s[0:NS, 3 * P:3 * P + NS]), "atto", h)

            def gated(i):
                r = rows(i)
                dve.wait_ge(exped, 6 + i)
                g = gh[0:r, i, :]
                v(dve.tensor_scalar(g, g, 1.0, None, ALU.add))
                v(dve.reciprocal(g, g))
                if i < NT:
                    ins = dve.tensor_tensor(g, J.bank("hg", i)[0:r, :], g, ALU.mult)
                else:
                    for n in range(4):
                        c = slice(P * n, P * (n + 1))
                        ins = dve.tensor_tensor(g[:, c], J.bank("hg", i)[NS * n:NS * (n + 1), 0:P], g[:, c], ALU.mult)
                J.empties(ins, "hg", i)
                J.wait_emptied(dve, "hg", i)
                g3 = g.rearrange("p (h v) -> p h v", h=HG)
                st.did(dve.tensor_tensor(g3, g3, ghn[0:r, :].unsqueeze(1).to_broadcast([r, HG, HD]), ALU.mult))

            for h in range(HG):
                decayed(h)
                if h == HG - 1:
                    gated(0)
                weights_inside(h)
            for i in range(1, 5):
                gated(i)

            def new_state(n):
                J.wait_filled(dve, "U", n)
                if n >= 5:
                    J.wait_filled(dve, "o", (n - 5) // 4)
                if n:
                    J.wait_emptied(dve, "U", n - 1)
                for h in range(HG):
                    u = J.bank("U", n)[:, HD * h:HD * (h + 1)]
                    dst = state[:, (n + 1) % 6, h, :]
                    if n == 0:
                        ins = dve.tensor_copy(dst, u)
                    else:
                        ins = dve.scalar_tensor_tensor(out=dst, in0=state[:, n % 6, h, :], scalar=dl[:, h, n:n + 1],
                                                       in1=u, op0=ALU.mult, op1=ALU.add)
                J.empties(ins, "U", n)

            def head_norm(i):
                r = rows(i)
                dve.wait_ge(o_root, i + 1)
                y = refined(hy0[0:r, i, :], hss[0:r, i, :], HD, [hnt[0:r, k, :] for k in range(3)], HG)
                s = J.bank("o", i)
                for h in range(HG):
                    c = slice(HD * h, HD * (h + 1))
                    ins = dve.scalar_tensor_tensor(out=on[i % 2][0:r, c], in0=s[0:r, c], scalar=y[:, h:h + 1],
                                                   in1=gh[0:r, i, c], op0=ALU.mult, op1=ALU.mult)
                J.empties(ins, "o", i)

            def softmax_stats(src, col, sem_max, n=1):
                v(dve.tensor_reduce(stat[:, 0, col:col + n], src, AX, ALU.max))
                dve.tensor_scalar(stat[:, 1, col:col + n], stat[:, 0, col:col + n], -1.0, None, ALU.mult)\
                    .then_inc(sem_max, 1)

            def probs(p, col, sem_exp, count, sem_prob):
                dve.wait_ge(sem_exp, count)
                v(dve.reciprocal(stat[:, 3, col:col + 1], stat[:, 2, col:col + 1]))
                dve.tensor_scalar(p, p, stat[:, 3, col:col + 1], None, ALU.mult).then_inc(sem_prob, 1)

            def moba_step(h):
                for i in range(NT):
                    n = NT * h + i
                    m = P * (i + 1)
                    J.wait_filled(dve, "S", h, i)
                    if h >= 2:
                        J.wait_filled(dve, "PT", h - 2, NT - 1)
                    p = pb[h % 2][i][:, 0:m]
                    J.empties(dve.scalar_tensor_tensor(out=p, in0=alibi[:, SEQ - P - P * i:SEQ - P - P * i + m],
                                                       scalar=2.0 ** -(h + 1), in1=J.bank("S", h, i)[:, 0:m],
                                                       op0=ALU.mult, op1=ALU.add), "S", h, i)
                    J.wait_emptied(dve, "S", h, i)
                    softmax_stats(p, n % 8, s_max)
                    if i:
                        probs(pb[h % 2][i - 1][:, 0:m - P], (n - 1) % 8, s_exp, n, s_prob)
                probs(pb[h % 2][NT - 1], n % 8, s_exp, n + 1, s_prob)

            for i in range(NT):
                for c in range(P // CH):
                    new_state(i * (P // CH) + c)
                moba_step(2 * i)
                head_norm(i)
                moba_step(2 * i + 1)
            J.wait_filled(dve, "o", NT - 1)
            dve.wait_ge(out_s, 16)
            v(dve.memset(qx, 0.0))
            for h in range(HG):
                q = qh[:, h, SEQ:TOK]
                dve.tensor_copy(qx[:, h, 0:252].rearrange("p (b m) -> p b m", m=36)[:, :, 0:NQ],
                                q[:, 0:NS - NQ].rearrange("p (b t) -> p b t", t=NQ))
                dve.tensor_copy(qx[:, h, 252:256], q[:, NS - NQ:NS])
            J.wait_emptied(dve, "kds", HG - 1)
            for b in range(NB):
                ins = dve.tensor_scalar(kdx[0:NS, b, :], kds[0:NS, :], bsel[:, b:b + 1], None, ALU.mult)
            ins.then_inc(kdx_done, 1)
            head_norm(NT)
            for b in range(NB):
                J.wait_filled(dve, "Us", b)
                for h in range(HG):
                    u = J.bank("Us", b)[:, HD * h:HD * (h + 1)]
                    ins = dve.scalar_tensor_tensor(out=s0[:, b, h, :], in0=s0[:, b, h, :],
                                                   scalar=dl[:, h, NCH + b:NCH + b + 1], in1=u,
                                                   op0=ALU.mult, op1=ALU.add)
                J.empties(ins, "Us", b)

            dve.wait_ge(gain_in, 16)
            for i in range(MT):
                norm_scale(5 + i, memx[:, i, :], hn[(5 + i) % 2])
            for i in range(MT):
                evac(memT[:, 4:8, P * i:P * (i + 1)], "memT", i, 1, view=lambda s: s.rearrange("p (k t) -> p k t", k=4))
            v(dve.memset(part(r_c, 4 * TOK, 4 * NB * 32), 0.0))
            for h in range(MB):
                par, c = h % 2, h // 2
                rr = slice(64 * par, 64 * par + 64)
                ins = dve.tensor_copy(qxm[rr, c, :, NQ * h:NQ * (h + 1)],
                                      mqT[rr, c, SEQ:TOK].rearrange("p (b t) -> p b t", t=NQ))
            ins.then_inc(qx_done, 1)
            dve.wait_ge(out_mv, 32)
            for n in range(4):
                evac((memk, memv)[n // 2][:, 1, 512 * (n % 2):512 * (n % 2 + 1)], "mem", n, 1)
                if n == 1:
                    for c in (1, 3):
                        evac(memkT[:, 2 * c:2 * c + 2, :], "memKT", c, view=lambda s: s.rearrange("p (k t) -> p k t", k=2))

            def keys_turned(b):
                if b < 2:
                    dve.wait_ge(out_s0, 16)
                else:
                    dve.wait_ge(sc_full, b // 2)
                for c in (1, 3):
                    evac(kT[b % 2][:, c, :], "KT", b, c)

            def sample_probs(g):
                dve.wait_ge(sc_full, 2 * g + 2)
                if g:
                    J.wait_filled(dve, "Ptn", g - 1)
                dve.tensor_tensor(sx[:, 0:PAST], sbias[:, 0:PAST], psum[6], ALU.add).then_inc(sc_free, 1)
                J.wait_filled(dve, "Sn", g)
                J.empties(dve.tensor_tensor(sx[:, PAST:], sbias[:, PAST + NS * g:PAST + NS * (g + 1)],
                                            J.bank("Sn", g)[:, 0:NS], ALU.add), "Sn", g)
                J.wait_emptied(dve, "Sn", g)
                dve.wait_ge(sc_free, g + 1)
                softmax_stats(sx, 0, ss_max)
                probs(sx, 0, ss_exp, g + 1, ss_prob)

            def new_probs_turned(g):
                if g:
                    J.wait_filled(dve, "Os", g - 1)
                evac(ptn[0:NS, :], "Ptn", g, view=lambda s: s[0:NS, 0:P])

            def out_turned(g):
                J.wait_filled(dve, "OsT", g)
                s = J.bank("OsT", g).rearrange("p (c b m) -> p c b m", c=4, b=4)
                for h in range(MB):
                    rr = slice(64 * (h % 2), 64 * (h % 2) + 64)
                    ins = dve.tensor_copy(mixT[rr, 4 + h // 2, SEQ + 16 * g:SEQ + 16 * (g + 1)]
                                          .rearrange("p (b t) -> p b t", b=4), s[rr, h // 2, :, NQ * h:NQ * (h + 1)])
                J.empties(ins, "OsT", g)

            for b in range(4):
                keys_turned(b)
            sample_probs(0)
            keys_turned(4)
            new_probs_turned(0)
            keys_turned(5)
            out_turned(0)
            keys_turned(6)
            keys_turned(7)
            sample_probs(1)
            new_probs_turned(1)

            def add_rows(tag, half, i):
                J.wait_filled(dve, tag, half, i)
                x = xr[0:rows(i), i, 512 * half:512 * (half + 1)]
                if i < NT:
                    ins = dve.tensor_tensor(x, x, J.bank(tag, half, i), ALU.add)
                else:
                    for n in range(4):
                        c = slice(P * n, P * (n + 1))
                        ins = dve.tensor_tensor(x[:, c], x[:, c], J.bank(tag, half, i)[NS * n:NS * (n + 1), 0:P], ALU.add)
                J.empties(ins, tag, half, i)

            def summed(what, turned, n0, meanwhile, logit=None):
                def norm(i):
                    norm_scale(n0 + i, xr[0:rows(i), i, :], hn[(n0 + i) % 2][0:rows(i), :])

                def turn(i):
                    evac(hT[:, 4:8, tok(i)], turned, i, 1,
                         view=lambda s: s.rearrange("p (k t) -> p k t", k=4)[:, :, 0:rows(i)])

                for i, _ in TILES:
                    add_rows(what, 0, i)
                    if i == 0:
                        meanwhile()
                for i, _ in TILES:
                    add_rows(what, 1, i)
                    if i:
                        norm(i - 1)
                    if i >= 2:
                        turn(i - 2)
                norm(NT)
                if logit:
                    logit(0)
                    logit(1)
                for i in (NT - 1, NT):
                    turn(i)
                    if logit:
                        logit(i - 1)
                if logit:
                    logit(NT)

            dve.wait_ge(xr_in, 32)
            dve.wait_ge(gain_in, 32)
            summed("x1", "h2T", 7, lambda: out_turned(1))
            for half in range(2):
                for c in (1, 3):
                    J.wait_filled(dve, "xq", half, c)
                    J.empties(dve.tensor_scalar(qT[:, 4 * half + c, 0:SEQ], J.bank("xq", half, c), XD ** -0.5, None,
                                                ALU.mult), "xq", half, c)
            for h in range(XH + 1):
                if h < XH:
                    for i2 in range(2):
                        J.wait_filled(dve, "XS", h, i2)
                        if h >= 2:
                            J.wait_filled(dve, "XPT", h - 2, MT - 1)
                        softmax_stats(J.bank("XS", h, i2).rearrange("p (u m) -> p u m", u=2), 2 * i2 + 4 * (h % 2), xs_max, 2)
                    for i2 in range(2):
                        J.wait_emptied(dve, "XS", h, i2)
                        for u in range(2):
                            n = 2 * i2 + u + 4 * (h % 2)
                            v(dve.reciprocal(stat[:, 3, n:n + 1], stat[:, 2, n:n + 1]))
                            x = xp[h % 2][:, 2 * i2 + u, :]
                            dve.tensor_scalar(x, x, stat[:, 3, n:n + 1], None, ALU.mult).then_inc(xs_prob, 1)
                if h:
                    for k in range(MT):
                        if h >= 3:
                            J.wait_filled(dve, "XOT", h - 3, 1)
                        if h == 1:
                            dve.wait_ge(out_mem, 32)
                        evac(xpt[(h - 1) % 2][:, k, :], "XPT", h - 1, k)
            J.wait_filled(dve, "XPT", XH - 1, MT - 1)
            v(dve.memset(part(flat, TAIL + 6144, KC * NB * 32), 0.0))
            for h in range(XH):
                for c in (2 * h, 2 * h + 1):
                    ins = dve.tensor_copy(qxx[:, c, :, NQ * h:NQ * (h + 1)],
                                          qT[:, c, SEQ:TOK].rearrange("p (b t) -> p b t", t=NQ))
            ins.then_inc(qx_done, 1)

            def mem_keys_turned(b):
                if b >= 2:
                    dve.wait_ge(sc_full, NB // 2 + b // 2)
                for c in (1, 3):
                    evac(xkT[b % 2][:, 2 * c:2 * c + 2, :], "XKT", b, c, view=lambda s: s.rearrange("p (k t) -> p k t", k=2))

            def mem_probs(g):
                dve.wait_ge(sc_full, NB // 2 + 2 * g + 2)
                if g:
                    J.wait_filled(dve, "XPt", g - 1)
                softmax_stats(psum[6][:, 0:MEM], 0, xs_max)
                probs(xsx, 0, xs_exp, g + 1, xs_prob)

            def mem_out(g):
                if g:
                    J.wait_filled(dve, "XOsT", g - 1, 1)
                evac(xosb[:, 1, :], "XOs", g, 1)

            def mem_out_turned(g):
                for half in range(2):
                    J.wait_filled(dve, "XOsT", g, half)
                    s = J.bank("XOsT", g, half).rearrange("p (c b m) -> p c b m", c=4, b=4)
                    for h in (2 * half, 2 * half + 1):
                        for u in range(2):
                            ins = dve.tensor_copy(oT[:, 2 * h + u, SEQ + 16 * g:SEQ + 16 * (g + 1)]
                                                  .rearrange("p (b t) -> p b t", b=4),
                                                  s[:, 2 * (h % 2) + u, :, NQ * h:NQ * (h + 1)])
                    J.empties(ins, "XOsT", g, half)

            for b in range(4):
                mem_keys_turned(b)
            mem_probs(0)
            mem_keys_turned(4)
            mem_out(0)
            mem_keys_turned(5)
            mem_out_turned(0)
            mem_keys_turned(6)
            mem_keys_turned(7)
            mem_probs(1)
            mem_out(1)

            lg = rt["lg"].rearrange("p (i n) -> p i n", n=36)

            def logit(i):
                if i == 0:
                    dve.wait_ge(rtw_in, 64)
                    v(dve.memset(lg, 0.0))
                r = rows(i)
                J.wait_filled(dve, "logit", i)
                J.empties(dve.tensor_tensor(lg[0:r, i, :], rt["bias"][0:r, :], J.bank("logit", i)[0:r, 0:36], ALU.add),
                          "logit", i)

            dve.wait_ge(gain_in, 48)
            summed("x2", "h3T", 12, lambda: mem_out_turned(1), logit)

            R = rt
            iota3 = lambda n: iota[:, 0:n].unsqueeze(1).to_broadcast([P, 5, n])
            v(dve.memset(R["g8"], -3e38))
            J.wait_emptied(dve, "logit", NT)
            g8 = R["g8"].rearrange("p (i n) -> p i n", n=8)
            m8 = R["m8"].rearrange("p (i n) -> p i n", n=8)
            v(dve.tensor_copy(g8[:, :, 0:NG], lg[:, :, 0:NG]))
            for i in range(5):
                ins = dve.max(m8[:, i, :], g8[:, i, :])
            v(ins)
            for i in range(5):
                ins = dve.max_index(i8[:, i, :], m8[:, i, :], g8[:, i, :])
            v(ins)
            gi = R["i8f"]
            v(dve.tensor_copy(gi, i8[:, :, 0]))
            ge = R["ge"].rearrange("p (i n) -> p i n", n=NG)
            dve.tensor_tensor(ge, lg[:, :, 0:NG], m8[:, :, 0:1].to_broadcast([P, 5, NG]), ALU.subtract)\
                .then_inc(r_exp_in, 1)
            ohg = R["ohg"].rearrange("p (i n) -> p i n", n=NG)
            v(dve.tensor_tensor(ohg, iota3(NG), gi.unsqueeze(2).to_broadcast([P, 5, NG]), ALU.is_equal))
            pr = R["pr"].rearrange("p (i g e) -> p i g e", i=5, g=NG)
            for i in range(5):
                ins = dve.tensor_tensor(pr[:, i], lg[:, i, NG:36].rearrange("p (g e) -> p g e", g=NG),
                                        ohg[:, i, :].unsqueeze(2).to_broadcast([P, NG, EPG]), ALU.mult)
            v(ins)
            se = R["se"].rearrange("p (i n) -> p i n", n=8)
            for i in range(5):
                ins = dve.tensor_reduce(se[:, i, :], pr[:, i].rearrange("p g e -> p e g"), AX, ALU.add)
            v(ins)
            me = R["me"].rearrange("p (i n) -> p i n", n=8)
            for i in range(5):
                ins = dve.max(me[:, i, :], se[:, i, :])
            v(ins)
            for i in range(5):
                ins = dve.max_index(i8[:, i, :], me[:, i, :], se[:, i, :])
            v(ins)
            ek = R["ek"].rearrange("p (k i) -> p k i", k=2)
            for k in range(2):
                ins = dve.tensor_copy(ek[:, k, :], i8[:, :, k])
            dve.tensor_tensor(R["ex"], me[:, :, 1], me[:, :, 0], ALU.subtract).then_inc(r_exp_in, 1)
            dve.wait_ge(r_exp_in, 2)
            dve.wait_ge(r_exp, 2)
            v(dve.tensor_reduce(R["gw"], ge, AX, ALU.add))
            v(dve.reciprocal(R["gw"], R["gw"]))
            v(dve.tensor_scalar(R["t1"][:, 0:5], R["ex"], 1.0, None, ALU.add))
            v(dve.reciprocal(R["t1"][:, 0:5], R["t1"][:, 0:5]))
            v(dve.tensor_tensor(gates[:, 0, :], R["gw"], R["t1"][:, 0:5], ALU.mult))
            v(dve.tensor_tensor(gates[:, 1, :], gates[:, 0, :], R["ex"], ALU.mult))
            eid = R["eid"].rearrange("p (k i) -> p k i", k=2)
            for k in range(2):
                ins = dve.scalar_tensor_tensor(out=eid[:, k, :], in0=gi, scalar=float(EPG), in1=ek[:, k, :],
                                               op0=ALU.mult, op1=ALU.add)
            v(ins)
            m = R["m"].rearrange("p (k i n) -> p k i n", k=2, i=5)
            ms = R["ms"].rearrange("p (i n) -> p i n", i=5)
            for k in range(2):
                ins = dve.tensor_tensor(m[:, k], iota3(NE), eid[:, k, :].unsqueeze(2).to_broadcast([P, 5, NE]), ALU.is_equal)
            v(ins)
            dve.tensor_tensor(ms, m[:, 0], m[:, 1], ALU.add).then_inc(onehots, 1)
            J.wait_filled(dve, "rank")
            s = J.bank("rank")
            v(dve.tensor_copy(R["cnt"], s[:, 160:192]))
            tmp = R["tmp"].rearrange("p (k i n) -> p k i n", k=2, i=5)
            rk = R["rk"].rearrange("p (k i) -> p k i", k=2)
            J.empties(dve.tensor_tensor(tmp, m, s[:, 0:160].rearrange("p (i n) -> p i n", i=5).unsqueeze(1)
                                        .to_broadcast([P, 2, 5, NE]), ALU.mult), "rank")
            J.wait_emptied(dve, "rank")
            v(dve.tensor_reduce(rk, tmp, AX, ALU.add))
            big = R["big"].rearrange("p (e m) -> p e m", e=NE)
            v(dve.tensor_tensor(big, R["cnt"].unsqueeze(2).to_broadcast([P, NE, 8]),
                                steps[:, :].unsqueeze(1).to_broadcast([P, NE, 8]), ALU.is_gt))
            v(dve.tensor_reduce(R["ovn"], big, AX, ALU.add))
            v(dve.tensor_tensor_scan(R["ove"], ones[:, 0:NE], R["ovn"], 0.0, ALU.mult, ALU.add))
            v(dve.tensor_tensor(R["ovs"], R["ove"], R["ovn"], ALU.subtract))
            qk = R["qk"].rearrange("p (k i) -> p k i", k=2)
            b5 = R["big"][:, 0:80].rearrange("p (i m) -> p i m", m=8)
            v(dve.tensor_tensor(b5, R["rk"].unsqueeze(2).to_broadcast([P, 10, 8]),
                                steps[:, :].unsqueeze(1).to_broadcast([P, 10, 8]), ALU.is_ge))
            v(dve.tensor_reduce(R["qk"], b5, AX, ALU.add))
            v(dve.scalar_tensor_tensor(out=R["rr"], in0=R["qk"], scalar=-float(CAP), in1=R["rk"], op0=ALU.mult, op1=ALU.add))
            tmp = R["tmp"].rearrange("p (a n) -> p a n", a=10)
            v(dve.tensor_tensor(tmp, R["m"].rearrange("p (a n) -> p a n", a=10),
                                R["ovs"].unsqueeze(1).to_broadcast([P, 10, NE]), ALU.mult))
            v(dve.tensor_reduce(R["ovk"], tmp, AX, ALU.add))
            v(dve.tensor_tensor(R["t1"], R["ovk"], R["qk"], ALU.add))
            v(dve.scalar_tensor_tensor(out=R["t1"], in0=R["t1"], scalar=float(NE - 1), in1=R["eid"], op0=ALU.add, op1=ALU.subtract))
            v(dve.tensor_scalar(R["t2"], R["qk"], 0.0, None, ALU.is_gt))
            v(dve.tensor_tensor(R["t1"], R["t1"], R["t2"], ALU.mult))
            v(dve.tensor_tensor(R["sk"], R["eid"], R["t1"], ALU.add))
            v(dve.scalar_tensor_tensor(out=yidx[:, :, :].rearrange("p k i -> p (k i)"), in0=R["sk"], scalar=float(CAP),
                                       in1=R["rr"], op0=ALU.mult, op1=ALU.add))
            ohs = R["ohs"].rearrange("p (a n) -> p a n", n=NBLK)
            ohr = R["ohr"].rearrange("p (a n) -> p a n", n=CAP)
            v(dve.tensor_tensor(ohs, iota[:, 0:NBLK].unsqueeze(1).to_broadcast([P, 10, NBLK]),
                                R["sk"].unsqueeze(2).to_broadcast([P, 10, NBLK]), ALU.is_equal))
            for k in range(2):
                o5 = ohs[:, 5 * k:5 * k + 5, :]
                ins = dve.tensor_tensor(o5, o5, tokid[:, :].unsqueeze(2).to_broadcast([P, 5, NBLK]), ALU.mult)
            v(ins)
            dve.tensor_tensor(ohr, iota[:, 0:CAP].unsqueeze(1).to_broadcast([P, 10, CAP]),
                              R["rr"].unsqueeze(2).to_broadcast([P, 10, CAP]), ALU.is_equal).then_inc(onehots, 1)
            cmp = R["cmp"].rearrange("p (s e) -> p s e", s=XBLK)
            v(dve.tensor_tensor(cmp[0:1], R["ove"][0:1, :].unsqueeze(1).to_broadcast([1, XBLK, NE]),
                                iota[0:1, 0:XBLK].unsqueeze(2).to_broadcast([1, XBLK, NE]), ALU.is_le))
            v(dve.tensor_reduce(R["exs"][0:1], cmp[0:1], AX, ALU.add))
            dve.tensor_scalar(ovi[0:1, 1:1 + XBLK], R["exs"][0:1], float(NE - 1), None, ALU.min)
            v(dve.tensor_copy(ovi[0:1, 0:1], R["ove"][0:1, NE - 1:NE]))
            J.wait_filled(dve, "table")
            dve.tensor_copy(table[:, :], J.bank("table")[:, 0:NBLK // 2]).then_inc(routed, 1)

            def pair(j):
                first = isinstance(j, int)
                dve.wait_ge(xt_full, j + 1)
                dve.tensor_copy(xT[:, 0:4, :], psum[0].rearrange("p (k t) -> p k t", k=4)).then_inc(xt_free, 1)
                for u in range(2):
                    dve.wait_ge(up_exp, 2 * j + (u + 1))
                    step = 6 * j + 3 * u
                    dve.tensor_scalar(he[u], he[u], 1.0, None, ALU.add).then_inc(dve_moe, 1)
                    dve.wait_ge(dve_moe, step + 1)
                    dve.reciprocal(he[u], he[u]).then_inc(dve_moe, 1)
                    dve.wait_ge(dve_moe, step + 2)
                    if not first:
                        dve.wait_ge(ht_full, 2 * j + (u - 1))
                    dve.tensor_tensor(he[u], he[u], psum[2 + 2 * u], ALU.mult).then_inc(dve_moe, 1)
                    dve.wait_ge(dve_moe, step + 3)
                    dve.tensor_tensor(h2[u], he[u], psum[3 + 2 * u], ALU.mult).then_inc(up_free, 1)

            pair(0)
            with dve.Fori(1, NE // 2) as j:
                pair(j)
            n_ov = dve.value_load(ovi[0:1, 0:1], min_val=0, max_val=XBLK)
            with dve.If(n_ov > 0):
                with dve.Fori(NE // 2, NBLK // 2) as j:
                    with dve.If(2 * j - NE < n_ov):
                        pair(j)
            dve.wait_ge(gain_in, 64)

            def expert_rows_added(i):
                r = rows(i)
                dve.wait_ge(yg_in[i], 32)
                x = xr[0:r, i, :]
                v(dve.scalar_tensor_tensor(out=x, in0=yg[i][0][0:r, :], scalar=gates[0:r, 0, i:i + 1], in1=x,
                                           op0=ALU.mult, op1=ALU.add))
                dve.scalar_tensor_tensor(out=x, in0=yg[i][1][0:r, :], scalar=gates[0:r, 1, i:i + 1], in1=x,
                                         op0=ALU.mult, op1=ALU.add).then_inc(xr_new, 1)

            expert_rows_added(0)
            for i, r in TILES:
                if i < NT:
                    expert_rows_added(i + 1)
                norm_scale(17 + i, xr[0:r, i, :], yg[i][0][0:r, :])

        @block.tensor
        def _(pe):
            def turn(what, i, n, ready):
                r = rows(i)
                pe.wait_ge(normed, ready)
                for half in range(2):
                    J.wait_free(pe, what, i, half)
                    s = J.bank(what, i, half)
                    for k in range(4):
                        ins = pe.transpose(s[:, P * k:P * k + r], hn[n % 2][0:r, P * (4 * half + k):P * (4 * half + k + 1)],
                                           ident[0:r, 0:r])
                    J.fills(ins, what, i, half)

            def weights(tag):
                n = WPOS[tag]
                pe.wait_ge(w_in[n % 2], 16 * (n // 2 + 1))
                return wslot[n % 2]

            def quarters(s, i, w, lhs):
                for k in range(KC):
                    for n in range(4):
                        ins = pe.matmul(s[NS * n:NS * (n + 1), 0:P], lhs[:, k, tok(i)], w[:, k, P * n:P * (n + 1)],
                                        start=(k == 0), stop=(k == KC - 1), skip_group_check=True)
                return ins

            def features_out(what, *key, chunks=range(5)):
                w = weights(what if not key else f"xq{key[0]}")
                for c in chunks:
                    if c == 0:
                        J.wait_free(pe, what, *key, "rows")
                        J.fills(quarters(J.bank(what, *key, "rows"), NT, w, hT), what, *key, "rows")
                    J.wait_free(pe, what, *key, c)
                    s = J.bank(what, *key, c)
                    if c < 4:
                        for k in range(KC):
                            ins = pe.matmul(s, w[:, k, P * c:P * (c + 1)], hT[:, k, 0:SEQ], start=(k == 0), stop=(k == KC - 1))
                    else:
                        J.wait_emptied(pe, what, *key, "rows")
                        ins = pe.transpose(s[:, 0:P], srows[:, :], ident[:, :])
                    J.fills(ins, what, *key, c)

            def rows_of(name, i, w, lhs):
                J.wait_free(pe, *name)
                if i == NT:
                    J.fills(quarters(J.bank(*name), i, w, lhs), *name)
                    return
                for k in range(KC):
                    ins = pe.matmul(J.bank(*name), lhs[:, k, tok(i)], w[:, k, :], start=(k == 0), stop=(k == KC - 1))
                J.fills(ins, *name)

            def weights_inside(h):
                pe.wait_ge(head_ready, h + 1)
                J.wait_free(pe, "attd", h)
                s = J.bank("attd", h)
                for i in range(NT):
                    ins = pe.matmul(s[:, tok(i)], hgt["kd"][:, tok(i)], hgt["qd"][:, tok(i)], start=True, stop=True)
                J.fills(ins, "attd", h)
                J.wait_free(pe, "atto", h)
                s = J.bank("atto", h)
                for j in range(3):
                    for i in range(NT):
                        c = slice(P * j + NS * i, P * j + NS * (i + 1))
                        pe.matmul(s[:, c], kb[j][:, tok(i)], hgt["qo"][:, c], start=True, stop=True)
                ins = pe.matmul(s[0:NS, 3 * P:3 * P + NS], hgt["kd"][:, SEQ:TOK], hgt["qd"][:, SEQ:TOK], start=True, stop=True)
                J.fills(ins, "atto", h)

            pe.wait_ge(page_in, 16)
            for i, r in TILES:
                turn("hT", i, i, i + 1)
            J.wait_emptied(pe, "hT", NT, 0)
            J.wait_emptied(pe, "hT", NT, 1)
            features_out("hf")
            features_out("hq")
            w = weights("mk")
            for i, r in TILES:
                rows_of(("mk", i), i, w, hT)
            features_out("mq", chunks=[0])
            weights_inside(0)
            features_out("mq", chunks=[1, 2, 3, 4])
            J.wait_emptied(pe, "mk", NT)
            for c in range(5):
                J.wait_free(pe, "mkT", c)
                s = J.bank("mkT", c)
                for n in range(4):
                    if c < 4:
                        ins = pe.transpose(s[:, P * n:P * (n + 1)], mkn[:, n, P * c:P * (c + 1)], ident[:, :])
                    else:
                        ins = pe.transpose(s[:, NS * n:NS * (n + 1)], mkn[0:NS, NT, P * n:P * (n + 1)], ident[0:NS, 0:NS])
                J.fills(ins, "mkT", c)
            weights_inside(1)
            w = weights("mv")
            for i, r in TILES:
                rows_of(("mv", i), i, w, hT)
            w = weights("hi")
            rows_of(("hi", 0), 0, w, hT)
            weights_inside(2)
            for i in range(1, 5):
                rows_of(("hi", i), i, w, hT)
            w = weights("hg")
            rows_of(("hg", 0), 0, w, hT)
            weights_inside(3)
            for i in range(1, 5):
                rows_of(("hg", i), i, w, hT)
            for h in range(HG):
                J.wait_free(pe, "kdn", h)
                for i in range(NT):
                    ins = pe.transpose(J.bank("kdn", h)[:, tok(i)], fk[:, h, tok(i)], ident[:, :])
                J.fills(ins, "kdn", h)
            for h in range(HG):
                J.wait_free(pe, "kds", h)
                ins = pe.transpose(J.bank("kds", h)[0:NS, 0:P], fk[:, h, SEQ:TOK], ident[:, :])
                J.fills(ins, "kds", h)

            def turn_heads(i):
                r = rows(i)
                J.wait_emptied(pe, "o", i)
                J.wait_free(pe, "hgT", i)
                for h in range(HG):
                    ins = pe.transpose(J.bank("hgT", i)[:, P * h:P * h + r], on[i % 2][0:r, HD * h:HD * (h + 1)], ident[0:r, 0:r])
                J.fills(ins, "hgT", i)

            def moba_step(h):
                if h < MB:
                    rr = slice(64 * (h % 2), 64 * (h % 2) + 64)
                    for i in range(NT):
                        J.wait_free(pe, "S", h, i)
                        ins = pe.matmul(J.bank("S", h, i)[:, 0:P * (i + 1)], mqT[rr, h // 2, tok(i)],
                                        mkT[rr, h // 2, 0:P * (i + 1)], start=True, stop=True)
                        J.fills(ins, "S", h, i)
                if h:
                    g = h - 1
                    for k in range(NT):
                        J.wait_free(pe, "PT", g, k)
                        for i in range(k, NT):
                            pe.wait_ge(s_prob, NT * g + i + 1)
                            ins = pe.transpose(J.bank("PT", g, k)[:, P * (i - k):P * (i - k + 1)],
                                               pb[g % 2][i][:, P * k:P * (k + 1)], ident[:, :])
                        J.fills(ins, "PT", g, k)
                    if h % 2 == 0:
                        c = h // 2 - 1
                        J.wait_free(pe, "OT", c)
                        J.wait_emptied(pe, "PT", g, NT - 1)
                        for k in range(NT):
                            for par in range(2):
                                hh = 2 * c + par
                                ins = pe.matmul(J.bank("OT", c)[64 * par:64 * par + 64, P * k:SEQ],
                                                mv[:, k, MD * hh:MD * (hh + 1)], pt[par][:, k, P * k:SEQ],
                                                start=(k == 0), stop=(k == NT - 1), skip_group_check=True)
                        J.fills(ins, "OT", c)

            J.wait_emptied(pe, "kdn", HG - 1)
            J.wait_emptied(pe, "kds", HG - 1)
            J.wait_emptied(pe, "atto", HG - 1)
            for i in range(NT):
                for c in range(P // CH):
                    n = i * (P // CH) + c
                    J.wait_free(pe, "U", n)
                    q = slice(CH * c, CH * (c + 1))
                    for h in range(HG):
                        ins = pe.matmul(J.bank("U", n)[:, HD * h:HD * (h + 1)], kdn[q, i, h, :], vh[q, i, HD * h:HD * (h + 1)],
                                        start=True, stop=True, tile_position=(CH * c, 0))
                    J.fills(ins, "U", n)
                moba_step(2 * i)
                J.wait_free(pe, "o", i)
                J.wait_emptied(pe, "U", 4 * i + 2)
                for h in range(HG):
                    c0 = slice(HD * h, HD * (h + 1))
                    s = J.bank("o", i)
                    ins = pe.matmul(s[:, c0], att[:, h, tok(i)], vh[:, i, c0], start=True, stop=True)
                    for c in range(P // CH):
                        n = i * (P // CH) + c
                        if n:
                            ins = pe.matmul(s[CH * c:CH * (c + 1), c0], qh[:, h, CH * n:CH * (n + 1)], state[:, n % 6, h, :],
                                            start=False, stop=True, skip_group_check=True)
                J.fills(ins, "o", i)
                if i:
                    turn_heads(i - 1)
                moba_step(2 * i + 1)
            turn_heads(NT - 1)
            moba_step(MB)
            J.wait_free(pe, "o", NT)
            pe.wait_ge(s0_in, 16)
            pe.wait_ge(kdx_done, 1)
            s = J.bank("o", NT)
            for h in range(HG):
                c0 = slice(HD * h, HD * (h + 1))
                pe.matmul(s[0:NS, c0], atts[0:NS, NS * h:NS * (h + 1)], vh[0:NS, NT, c0], start=True, stop=False)
                for b in range(NB):
                    ins = pe.matmul(s[0:NS, c0], qx[:, h, NS * b:NS * (b + 1)], s0[:, b, h, :], start=False, stop=(b == NB - 1))
            J.fills(ins, "o", NT)
            for b in range(NB):
                J.wait_free(pe, "Us", b)
                for h in range(HG):
                    c0 = slice(HD * h, HD * (h + 1))
                    ins = pe.matmul(J.bank("Us", b)[:, c0], kdx[0:NS, b, c0], vh[0:NS, NT, c0], start=True, stop=True)
                J.fills(ins, "Us", b)
            turn_heads(NT)

            for i in range(MT):
                turn("memT", i, 5 + i, 6 + i)
            J.wait_emptied(pe, "memT", 1, 0)
            J.wait_emptied(pe, "memT", 1, 1)
            for n in range(4):
                w = weights(("xk0", "xk1", "xv0", "xv1")[n])
                for i in range(MT):
                    J.wait_free(pe, "mem", n, i)
                    for k in range(KC):
                        ins = pe.matmul(J.bank("mem", n, i), memT[:, k, P * i:P * (i + 1)], w[:, k, :], start=(k == 0), stop=(k == KC - 1))
                    J.fills(ins, "mem", n, i)
                if n == 1:
                    for c in range(4):
                        J.wait_free(pe, "memKT", c)
                        J.wait_emptied(pe, "mem", 1, 0)
                        J.wait_emptied(pe, "mem", 1, 1)
                        for m in range(4):
                            k, i = 2 * c + m // 2, m % 2
                            ins = pe.transpose(J.bank("memKT", c)[:, P * m:P * (m + 1)], memk[:, i, P * k:P * (k + 1)], ident[:, :])
                        J.fills(ins, "memKT", c)

            def keys_turned(b):
                pe.wait_ge(k_in[b % 2], 16 * NPG * (b // 2 + 1))
                for c in range(4):
                    J.wait_free(pe, "KT", b, c)
                    for j in range(NPG):
                        ins = pe.transpose(J.bank("KT", b, c)[:, P * j:P * (j + 1)], kbuf[b % 2][:, j, P * c:P * (c + 1)],
                                           ident[:, :])
                    J.fills(ins, "KT", b, c)

            def scores(b0):
                if b0 == 4:
                    pe.wait_ge(sc_free, 1)
                J.wait_emptied(pe, "KT", b0 + 1, 2)
                J.wait_emptied(pe, "KT", b0 + 1, 3)
                for c in range(4):
                    for b in (b0, b0 + 1):
                        ins = pe.matmul(psum[6][32 * (b % 4):32 * (b % 4) + 32, :], qxm[:, c, b, :], kT[b % 2][:, c, :],
                                        start=(c == 0), stop=(c == 3), skip_group_check=True)
                ins.then_inc(sc_full, 1)

            def new_scores(g):
                J.wait_free(pe, "Sn", g)
                for c in range(4):
                    for b in range(4 * g, 4 * g + 4):
                        q = slice(32 * (b % 4), 32 * (b % 4) + 32)
                        ins = pe.matmul(J.bank("Sn", g)[q, 0:NS], qxm[:, c, b, :], mkT[:, c, SEQ:TOK], start=(c == 0),
                                        stop=(c == 3), skip_group_check=True)
                J.fills(ins, "Sn", g)

            def probs_turned(g):
                pe.wait_ge(ss_prob, g + 1)
                J.wait_free(pe, "Pt", g)
                for j in range(NPG):
                    ins = pe.transpose(J.bank("Pt", g)[:, P * j:P * (j + 1)], sx[:, P * j:P * (j + 1)], ident[:, :])
                J.fills(ins, "Pt", g)
                J.wait_free(pe, "Ptn", g)
                ins = pe.transpose(J.bank("Ptn", g)[0:NS, 0:P], sx[:, PAST:], ident[:, :])
                J.fills(ins, "Ptn", g)

            def sample_out(g):
                J.wait_free(pe, "Os", g)
                J.wait_emptied(pe, "Pt", g)
                J.wait_emptied(pe, "Ptn", g)
                pe.wait_ge(v_in, 16 * NPG * 4 * (g + 1))
                s = J.bank("Os", g)
                ins = pe.matmul(s, ptn[0:NS, :], mvs[0:NS, :], start=True, stop=True, skip_group_check=True)
                for j in range(NPG):
                    for b in range(4):
                        ins = pe.matmul(s[32 * b:32 * b + 32, :], ptS[:, j, 32 * b:32 * b + 32], vbuf[b][:, j, :],
                                        start=False, stop=True, skip_group_check=True)
                J.fills(ins, "Os", g)

            def out_turned(g):
                J.wait_free(pe, "OsT", g)
                J.wait_emptied(pe, "Os", g)
                for c in range(4):
                    ins = pe.transpose(J.bank("OsT", g)[:, P * c:P * (c + 1)], osb[:, P * c:P * (c + 1)], ident[:, :])
                J.fills(ins, "OsT", g)

            keys_turned(0)
            keys_turned(1)
            keys_turned(2)
            pe.wait_ge(qx_done, 1)
            scores(0)
            keys_turned(3)
            scores(2)
            new_scores(0)
            keys_turned(4)
            probs_turned(0)
            sample_out(0)
            keys_turned(5)
            out_turned(0)
            keys_turned(6)
            scores(4)
            keys_turned(7)
            scores(6)
            new_scores(1)
            probs_turned(1)
            sample_out(1)

            def summed(what, wtag, lhs, turned, n0, meanwhile, samples, logit=None):
                for half in range(2):
                    w = weights(f"{wtag}{half}")
                    for i, r in TILES:
                        if i == NT and half == 0:
                            J.wait_emptied(pe, *samples)
                        rows_of((what, half, i), i, w, lhs)
                        if i == 0 and half == 0:
                            meanwhile()
                        if half and i >= 2:
                            turn(turned, i - 2, n0 + i - 2, n0 + i - 1)
                if logit:
                    logit(0)
                    logit(1)
                for i in range(NT - 1, NT + 1):
                    turn(turned, i, n0 + i, n0 + i + 1)
                    if logit:
                        logit(i - 1)
                if logit:
                    logit(NT)

            J.wait_emptied(pe, "OsT", 0)
            summed("x1", "o", mixT, "h2T", 7, lambda: out_turned(1), ("OsT", 1))
            J.wait_emptied(pe, "h2T", NT, 0)
            J.wait_emptied(pe, "h2T", NT, 1)
            for half in range(2):
                features_out("xq", half)
            for c in range(5):
                J.wait_emptied(pe, "xq", 1, c)
            J.wait_emptied(pe, "memKT", 2)
            J.wait_emptied(pe, "memKT", 3)
            for h in range(XH + 1):
                if h < XH:
                    for i2 in range(2):
                        J.wait_free(pe, "XS", h, i2)
                        for u in range(2):
                            for c in range(2):
                                ins = pe.matmul(J.bank("XS", h, i2)[:, MEM * u:MEM * (u + 1)], qT[:, 2 * h + c, tok(2 * i2 + u)],
                                                memkT[:, 2 * h + c, :], start=(c == 0), stop=(c == 1))
                        J.fills(ins, "XS", h, i2)
                if h:
                    g = h - 1
                    for k in range(MT):
                        J.wait_free(pe, "XPT", g, k)
                        pe.wait_ge(xs_prob, NT * (g + 1))
                        for i in range(NT):
                            ins = pe.transpose(J.bank("XPT", g, k)[:, tok(i)], xp[g % 2][:, i, P * k:P * (k + 1)], ident[:, :])
                        J.fills(ins, "XPT", g, k)
                    J.wait_emptied(pe, "XPT", g, 1)
                    for c in range(2):
                        J.wait_free(pe, "XOT", g, c)
                        for k in range(MT):
                            ins = pe.matmul(J.bank("XOT", g, c), memv[:, k, P * (2 * g + c):P * (2 * g + c + 1)], xpt[g % 2][:, k, :],
                                            start=(k == 0), stop=(k == MT - 1))
                        J.fills(ins, "XOT", g, c)

            def mem_keys_turned(b):
                pe.wait_ge(xk_in[b % 2], 16 * (b // 2 + 1))
                for c in range(4):
                    J.wait_free(pe, "XKT", b, c)
                    for n in range(4):
                        k, i = 2 * c + n // 2, n % 2
                        ins = pe.transpose(J.bank("XKT", b, c)[:, P * n:P * (n + 1)], xkbuf[b % 2][:, i, P * k:P * (k + 1)], ident[:, :])
                    J.fills(ins, "XKT", b, c)

            def mem_scores(b0):
                if b0 == 0:
                    pe.wait_ge(sc_free, 2)
                if b0 == 4:
                    pe.wait_ge(xs_exp, 1)
                J.wait_emptied(pe, "XKT", b0 + 1, 2)
                J.wait_emptied(pe, "XKT", b0 + 1, 3)
                for c in range(KC):
                    for b in (b0, b0 + 1):
                        ins = pe.matmul(psum[6][32 * (b % 4):32 * (b % 4) + 32, 0:MEM], qxx[:, c, b, :], xkT[b % 2][:, c, :],
                                        start=(c == 0), stop=(c == KC - 1), skip_group_check=True)
                ins.then_inc(sc_full, 1)

            def mem_probs_turned(g):
                pe.wait_ge(xs_prob, NT * XH + g + 1)
                J.wait_free(pe, "XPt", g)
                for j in range(MT):
                    ins = pe.transpose(J.bank("XPt", g)[:, P * j:P * (j + 1)], xsx[:, P * j:P * (j + 1)], ident[:, :])
                J.fills(ins, "XPt", g)

            def mem_out(g):
                J.wait_emptied(pe, "XPt", g)
                pe.wait_ge(xv_in, 16 * 4 * (g + 1))
                for half in range(2):
                    J.wait_free(pe, "XOs", g, half)
                    for j in range(MT):
                        for b in range(4):
                            ins = pe.matmul(J.bank("XOs", g, half)[32 * b:32 * b + 32, :], xptS[:, j, 32 * b:32 * b + 32],
                                            xvbuf[b][:, j, 512 * half:512 * (half + 1)], start=(j == 0), stop=(j == MT - 1),
                                            skip_group_check=True)
                    J.fills(ins, "XOs", g, half)

            def mem_out_turned(g):
                for half in range(2):
                    J.wait_free(pe, "XOsT", g, half)
                    J.wait_emptied(pe, "XOs", g, half)
                    for c in range(4):
                        ins = pe.transpose(J.bank("XOsT", g, half)[:, P * c:P * (c + 1)], xosb[:, half, P * c:P * (c + 1)],
                                           ident[:, :])
                    J.fills(ins, "XOsT", g, half)

            mem_keys_turned(0)
            mem_keys_turned(1)
            mem_keys_turned(2)
            pe.wait_ge(qx_done, 2)
            mem_scores(0)
            mem_keys_turned(3)
            mem_scores(2)
            mem_keys_turned(4)
            mem_probs_turned(0)
            mem_out(0)
            mem_keys_turned(5)
            mem_out_turned(0)
            mem_keys_turned(6)
            mem_scores(4)
            mem_keys_turned(7)
            mem_scores(6)
            mem_probs_turned(1)
            mem_out(1)

            wr = rt["wr"].rearrange("p (k n) -> p k n", k=KC)

            def logit(i):
                if i == 0:
                    pe.wait_ge(rtw_in, 64)
                J.wait_free(pe, "logit", i)
                J.wait_emptied(pe, "h3T", i, 0)
                J.wait_emptied(pe, "h3T", i, 1)
                for k in range(KC):
                    ins = pe.matmul(J.bank("logit", i)[0:rows(i), 0:36], hT[:, k, tok(i)], wr[:, k, :], start=(k == 0), stop=(k == KC - 1))
                J.fills(ins, "logit", i)

            summed("x2", "xo", oT, "h3T", 12, lambda: mem_out_turned(1), ("XOsT", 1, 1), logit)
            J.wait_free(pe, "rank")
            pe.wait_ge(onehots, 1)
            ms = rt["ms"].rearrange("p (i n) -> p i n", i=5)
            s = J.bank("rank")
            pe.matmul(s[:, 0:NE * NT], before[:, :], ms[:, 0:NT, :], start=True, stop=True, skip_group_check=True)
            pe.matmul(s[:, NE * NT:NE * (NT + 1)], before[0:NS, :], ms[0:NS, NT, :], start=False, stop=True,
                      skip_group_check=True)
            for k, rr in TILES:
                ins = pe.matmul(s[:, NE * (k + 1):NE * (NT + 2)].rearrange("p (i n) -> p i n", n=NE), ones[0:rr, :],
                                ms[0:rr, k, :].unsqueeze(1).to_broadcast([rr, NT + 1 - k, NE]), start=False, stop=True,
                                skip_group_check=True)
            J.fills(ins, "rank")
            J.wait_free(pe, "table")
            pe.wait_ge(onehots, 2)
            ohs = rt["ohs"].rearrange("p (a n) -> p a n", n=NBLK)
            ohr = rt["ohr"].rearrange("p (a n) -> p a n", n=CAP)
            for k in range(2):
                for i, r in TILES:
                    for u in range(2):
                        ins = pe.matmul(J.bank("table")[CAP * u:CAP * (u + 1), 0:NBLK // 2], ohr[0:r, 5 * k + i, :],
                                        ohs[0:r, 5 * k + i, :].rearrange("p (c u) -> p u c", u=2)[:, u, :],
                                        start=(k == 0 and i == 0), stop=(k == 1 and i == NT), skip_group_check=True)
            J.fills(ins, "table")

            pe.wait_ge(routed, 1)

            def pair(j):
                first = isinstance(j, int)
                pe.wait_ge(xg_in, 16 * j + 16)
                if not first:
                    pe.wait_ge(xt_free, 2 * j)
                for k in range(KC):
                    ins = pe.transpose(psum[k // 4][:, P * (k % 4):P * (k % 4 + 1)], xg[:, P * k:P * (k + 1)], ident[:, :])
                ins.then_inc(xt_full, 1)
                pe.wait_ge(xt_free, 2 * j + 2)
                for u in range(2):
                    e = 2 * j + u
                    if not first:
                        pe.wait_ge(up_free, 2 * j + (u - 1))
                    for q in range(4):
                        for m in range(2):
                            pe.wait_ge(wm_in[2 * q + m], 32 * j + 16 * (u + 1))
                            for kk in range(2):
                                k = 2 * q + kk
                                for half in range(2):
                                    ins = pe.matmul(psum[2 + 2 * u + m][CAP * half:CAP * (half + 1), :],
                                                    xT[:, k, CAP * u:CAP * (u + 1)],
                                                    ring[:, 2 * q + m, kk, 512 * half:512 * (half + 1)],
                                                    start=(k == 0), stop=(k == KC - 1), skip_group_check=True)
                            ins.then_inc(w_used, 1)
                    pe.wait_ge(up_free, 2 * j + (u + 1))
                    if not first or u:
                        pe.wait_ge(ht_free, 2 * j + u)
                    for c in range(4):
                        ins = pe.transpose(psum[6][:, P * c:P * (c + 1)], h2[u][:, P * c:P * (c + 1)], ident[:, :])
                    ins.then_inc(ht_full, 1)
                    pe.wait_ge(ht_free, 2 * j + (u + 1))
                    if not first or u:
                        pe.wait_ge(y_free, 2 * j + u)
                    for q in range(4):
                        pe.wait_ge(wm_in[8 + q], 32 * j + 16 * (u + 1))
                        for kk in range(2):
                            k = 2 * q + kk
                            for half in range(2):
                                ins = pe.matmul(psum[7][CAP * half:CAP * (half + 1), :],
                                                heT[u][:, k % 4, CAP * (k // 4):CAP * (k // 4 + 1)],
                                                ring[:, 8 + q, kk, 512 * half:512 * (half + 1)],
                                                start=(k == 0), stop=(k == KC - 1), skip_group_check=True)
                        ins.then_inc(w_used, 1)

            pair(0)
            with pe.Fori(1, NE // 2) as j:
                pair(j)
            n_ov = pe.value_load(ovi[0:1, 0:1], min_val=0, max_val=XBLK)
            with pe.If(n_ov > 0):
                with pe.Fori(NE // 2, NBLK // 2) as j:
                    with pe.If(2 * j - NE < n_ov):
                        pair(j)


INS = ["x_prompt", "x_sample", "state_hgrn", "cache_moba_k", "cache_moba_v", "cache_mem_k", "cache_mem_v", "page_table",
       "mem_prompt", "g_mix", "w_in", "hg_lb", "hg_norm", "w_out", "g_cross", "g_mem", "w_xq", "w_xk", "w_xv", "w_xo",
       "g_ffn", "w_grp", "b_grp", "w_exp", "b_exp", "w1", "w3", "w2", "g_final"]


def kernel(**inputs):
    import concourse.bacc as bacc
    from concourse.bass_utils import run_bass_kernel_spmd

    nc = bacc.Bacc("TRN2", target_bir_lowering=False, num_devices=1)
    arrays = {name: np.ascontiguousarray(inputs[name]) for name in INS}
    arrays["g_final"] = arrays["g_final"].reshape(1, D)
    arrays.update(constants())
    aps = {name: nc.dram_tensor(name, x.shape, mybir.dt.from_np(x.dtype), kind="ExternalInput").ap()
           for name, x in arrays.items()}
    for name, shape in OUTS:
        aps[name] = nc.dram_tensor(name, shape, F32, kind="ExternalOutput").ap()
    step_kernel(nc, aps)
    r = run_bass_kernel_spmd(nc, [arrays], core_ids=[0])
    return tuple(r.results[0][name] for name, _ in OUTS)
```

```python
from contextlib import ExitStack

import numpy as np

import concourse.bass as bass
from concourse import mybir

F32 = mybir.dt.float32
U32 = mybir.dt.uint32
I32 = mybir.dt.int32
ACT = mybir.ActivationFunctionType
ALU = mybir.AluOpType
AX = mybir.AxisListType.X

P = 128
D = 1024
KC = D // P
SEQ = 512
NT = SEQ // P
NB, NQ = 8, 4
NS = NB * NQ
TOK = SEQ + NS
TILES = [(i, P) for i in range(NT)] + [(NT, NS)]
HG, HD = 4, 128
CH, SUB = 32, 8
NCH = SEQ // CH
MB, MD = 8, 64
PAGE, NPG, NPHYS = 128, 4, 40
PAST = NPG * PAGE
XH, XD, MEM = 4, 256, 256
MT = MEM // P
NG, EPG = 4, 8
NE = NG * EPG
CAP = 64
XBLK = 16
NBLK = NE + XBLK
EPS = 1e-6
NEG = -1e30


def constants():
    p = np.arange(P)
    c = {}
    c["c_ident"] = np.eye(P)
    t = np.arange(SEQ)
    tt = t % P
    c["c_maskd"] = ((p[:, None] // SUB == tt[None] // SUB) & (p[:, None] <= tt[None]))
    off = np.zeros((P, 3, SEQ // CH, SUB))
    for j in range(1, CH // SUB):
        for ch in range(NCH):
            s0 = (ch % (P // CH)) * CH
            off[s0:s0 + j * SUB, j - 1, ch, :] = 1
    c["c_masko"] = off.reshape(P, 3 * SEQ // CH * SUB)
    r = np.arange(NS)
    ms = (r[:, None] // NQ == r[None] // NQ) & (r[:, None] <= r[None])
    c["c_masks"] = np.tile(ms, (1, HG))
    c["c_bsel"] = (r[:, None] // NQ == np.arange(NB)[None])
    scan = np.ones(TOK)
    scan[0:SEQ:CH] = 0
    scan[SEQ::NQ] = 0
    c["c_scan"] = np.broadcast_to(scan, (P, TOK))
    x = np.arange(SEQ + SEQ - P)[None] - p[:, None] - (SEQ - P)
    c["c_alibi"] = np.where(x <= 0, x, NEG)
    b, h, q = p // 32, (p % 32) // NQ, p % NQ
    slope = 2.0 ** (-(h + 1.0))
    sb = np.full((P, PAST + 2 * NS), NEG)
    sb[:, :PAST] = -slope[:, None] * (PAST + q[:, None] - np.arange(PAST)[None])
    for g in range(2):
        for k in range(NS):
            ok = (k // NQ == 4 * g + b) & (k % NQ <= q)
            sb[:, PAST + NS * g + k] = np.where(ok, -slope * (q - k % NQ), NEG)
    c["c_sbias"] = sb
    c["c_before"] = (p[:, None] < p[None])
    c["c_ones"] = np.ones((P, P))
    c["c_iota"] = np.broadcast_to(np.arange(P), (P, P))
    c["c_tokid"] = np.arange(5)[None] * P + p[:, None]
    c["c_steps"] = np.broadcast_to(CAP * np.arange(1, 9), (P, 8))
    return {k: np.ascontiguousarray(v, dtype=np.float32) for k, v in c.items()}


OUTS = [("y_prompt", (1, SEQ, D)), ("y_sample", (NB, NQ, D)), ("hg_prompt", (1, 1, HG, HD, HD)),
        ("mk_prompt", (1, 1, SEQ, MB, MD)), ("mv_prompt", (1, 1, SEQ, MB, MD)),
        ("xk_prompt", (1, 1, MEM, XH, XD)), ("xv_prompt", (1, 1, MEM, XH, XD)),
        ("hg_sample", (1, NB, HG, HD, HD)), ("mk_sample", (1, NB, NQ, MB, MD)),
        ("mv_sample", (1, NB, NQ, MB, MD))]

IN = {"hq": 0, "hf": 1, "hi": 2, "hg": 3, "mq": 4, "mk": 5, "mv": 6}
WBLOCKS = [("w_in", IN[n], n) for n in ("mk", "hf", "hq", "mq", "mv", "hg", "hi")] + \
          [("w_xk", 0, "xk0"), ("w_xk", 1, "xk1"), ("w_xv", 0, "xv0"), ("w_xv", 1, "xv1"),
           ("w_out", 0, "o0"), ("w_out", 1, "o1"), ("w_xq", 0, "xq0"), ("w_xq", 1, "xq1"),
           ("w_xo", 0, "xo0"), ("w_xo", 1, "xo1")]
WPOS = {n: i for i, (_, _, n) in enumerate(WBLOCKS)}


LAST_HALF = [NT] + list(range(NT))

RING = 6


def plan_jobs():
    jobs = []

    def add(eng, *name):
        jobs.append((name, eng))

    def turned(what, tiles):
        for i, _ in tiles:
            add("A", what, i, 0)
            add("V", what, i, 1)

    def all_of(eng, what, numbers=range(5)):
        for n in numbers:
            add(eng, what, n)

    def weights_inside(h):
        add("V", "attd", h)
        add("V", "atto", h)

    for i, _ in TILES:
        turned("hT", TILES[i:i + 1])
        if i:
            add("A", "mk", i - 1)
    add("A", "mk", NT)
    add("A", "hf", "rows")
    all_of("A", "hf")
    add("A", "hq", "rows")
    all_of("V", "hq")
    add("A", "mq", "rows")
    all_of("A", "mq")
    all_of("A", "mkT")
    weights_inside(0)
    all_of("A", "mv")
    weights_inside(1)
    all_of("V", "hg", [0, 1, 2, 3])
    weights_inside(2)
    all_of("V", "hg", [4])
    all_of("A", "hi")
    weights_inside(3)
    all_of("A", "kdn", range(HG))
    all_of("A", "kds", range(HG))

    def moba_step(h):
        if h < MB:
            for i in range(NT):
                add("V", "S", h, i)
        if h:
            for k in range(NT):
                add("A", "PT", h - 1, k)
            if h % 2 == 0:
                add("A", "OT", h // 2 - 1)

    for i in range(NT):
        all_of("V", "U", range(4 * i, 4 * i + 4))
        moba_step(2 * i)
        add("A", "o", i)
        moba_step(2 * i + 1)
    moba_step(MB)
    add("A", "o", NT)
    all_of("V", "Us", range(NB))
    all_of("A", "hgT")
    turned("memT", TILES[:MT])
    for n in range(4):
        for i in range(MT):
            add("AV"[i], "mem", n, i)
        if n == 1:
            for c in range(4):
                add("AV"[c % 2], "memKT", c)

    def keys_turned(what, b):
        for c in range(4):
            add("AV"[c % 2], what, b, c)

    for b in range(4):
        keys_turned("KT", b)
    add("V", "Sn", 0)
    keys_turned("KT", 4)
    keys_turned("KT", 5)
    add("A", "Pt", 0)
    add("V", "Ptn", 0)
    add("A", "Os", 0)
    keys_turned("KT", 6)
    add("V", "OsT", 0)
    keys_turned("KT", 7)
    add("V", "Sn", 1)
    add("A", "Pt", 1)
    add("V", "Ptn", 1)
    add("A", "Os", 1)

    def summed(what, turn, samples):
        for i, _ in TILES:
            add("V", what, 0, i)
            if i == 0:
                for name in samples:
                    add("V", *name)
        for n, i in enumerate(LAST_HALF):
            add("V", what, 1, i)
            if n >= 2:
                turned(turn, [(LAST_HALF[n - 2], 0)])
        logit = [("logit", i) for i in LAST_HALF] if what == "x2" else []
        for name in logit[:2]:
            add("V", *name)
        for n in (NT - 1, NT):
            turned(turn, [(LAST_HALF[n], 0)])
            for name in logit[n - 1:n]:
                add("V", *name)
        for name in logit[NT:]:
            add("V", *name)

    summed("x1", "h2T", [("OsT", 1)])
    for half in range(2):
        add("A", "xq", half, "rows")
        for c in range(5):
            add("AV"[c % 2], "xq", half, c)
    for h in range(XH + 1):
        if h < XH:
            for i in range(2):
                add("A", "XS", h, i)
        if h:
            for k in range(MT):
                add("V", "XPT", h - 1, k)
            for c in range(2):
                add("A", "XOT", h - 1, c)
    for b in range(4):
        keys_turned("XKT", b)
    keys_turned("XKT", 4)
    add("A", "XPt", 0)
    add("A", "XOs", 0, 0)
    add("V", "XOs", 0, 1)
    keys_turned("XKT", 5)
    add("V", "XOsT", 0, 0)
    add("V", "XOsT", 0, 1)
    for b in range(6, 8):
        keys_turned("XKT", b)
    add("A", "XPt", 1)
    add("A", "XOs", 1, 0)
    add("V", "XOs", 1, 1)
    summed("x2", "h3T", [("XOsT", 1, 0), ("XOsT", 1, 1)])
    add("V", "rank")
    add("V", "table")
    return jobs


class Banks:

    def __init__(self, nc, psum, sem):
        self.psum = psum
        self.jobs = plan_jobs()
        self.number, self.rank, seen = {}, {}, {"A": 0, "V": 0}
        for n, (name, eng) in enumerate(self.jobs):
            self.number[name] = n
            self.rank[name] = seen[eng]
            seen[eng] += 1
        assert len(self.number) == len(self.jobs)
        self.total = seen
        self.filled = sem("psum_filled")
        self.emptied = {"A": sem("act_emptied"), "V": sem("dve_emptied")}

    def bank(self, *name):
        return self.psum[self.number[name] % RING]

    def wait_filled(self, eng, *name):
        eng.wait_ge(self.filled, self.number[name] + 1)

    def wait_emptied(self, eng, *name):
        who = self.jobs[self.number[name]][1]
        eng.wait_ge(self.emptied[who], self.rank[name] + 1)

    def wait_free(self, pe, *name):
        n = self.number[name] - RING
        if n >= 0:
            self.wait_emptied(pe, *self.jobs[n][0])

    def fills(self, ins, *name):
        ins.then_inc(self.filled, 1)

    def empties(self, ins, *name):
        ins.then_inc(self.emptied[self.jobs[self.number[name]][1]], 1)


class Steps:

    def __init__(self, sem):
        self.sem, self.n = sem, 0

    def did(self, ins):
        ins.then_inc(self.sem, 1)
        self.n += 1
        return self.n

    def settle(self, eng):
        eng.wait_ge(self.sem, self.n)


def step_kernel(nc, a):
    with ExitStack() as ctx:
        def sb(name, shape, dt=F32):
            return ctx.enter_context(nc.sbuf_tensor(name, shape, dt))

        def sem(name):
            return ctx.enter_context(nc.semaphore(name))

        ring = sb("ring", [P, 12, 2, D])
        r_x = sb("r_x", [P, 5 * D])
        r_h = sb("r_h", [P, KC * TOK])
        r_mix = sb("r_mix", [P, KC * TOK])
        r_c = sb("r_c", [P, 16 * TOK])
        gain = sb("gain", [P, D])
        ident = sb("ident", [P, P])
        maskd = sb("maskd", [P, SEQ])
        masko = sb("masko", [P, 3 * P])
        masks = sb("masks", [NS, HG * NS])
        bsel = sb("bsel", [NS, NB])
        scan = sb("scan", [P, TOK])
        alibi = sb("alibi", [P, 2 * SEQ - P])
        sbias = sb("sbias", [P, PAST + 2 * NS])
        mvs = sb("mvs", [NS, 512])
        srows = sb("srows", [P, P])
        before = sb("before", [P, P])
        ones = sb("ones", [P, P])
        iota = sb("iota", [P, P])
        tokid = sb("tokid", [P, 5])
        steps = sb("steps", [P, 8])
        lbl = sb("lbl", [P, 2, HG])
        lb = sb("lb", [P, HG])
        omlb = sb("omlb", [P, HG])
        ghn = sb("ghn", [P, HD])
        ss = sb("ss", [P, 22])
        y0 = sb("y0", [P, 22])
        nt = sb("nt", [P, 4, 22])
        hss = sb("hss", [P, 5, HG])
        hy0 = sb("hy0", [P, 5, HG])
        hnt = nt[:, :, 0:5 * HG].rearrange("p k (i h) -> p k i h", h=HG)
        dl = sb("dl", [P, HG, NCH + NB])
        stat = sb("stat", [P, 4, 2 * NT])
        table = sb("table", [P, NBLK // 2], U32)
        zeros = sb("zeros", [P, P])
        yidx = sb("yidx", [P, 2, 5], U32)
        ovi = sb("ovi", [1, 1 + XBLK], I32)
        gates = sb("gates", [P, 2, 5])
        psum_t = ctx.enter_context(nc.psum_tensor("psum", [P, 8, 512], F32))
        psum = [psum_t[:, n, :] for n in range(8)]
        tok_rows = nc.dram_tensor("tok_rows", [TOK, D], F32, kind="Internal").ap()
        out_rows = nc.dram_tensor("out_rows", [NBLK * CAP, D], F32, kind="Internal").ap()

        def part(buf, at, *shape):
            n = int(np.prod(shape))
            v = buf[:, at:at + n]
            if len(shape) == 1:
                return v
            names = "abcd"[:len(shape)]
            kw = {c: s for c, s in zip(names[1:], shape[1:])}
            return v.rearrange(f"p ({' '.join(names)}) -> p {' '.join(names)}", **kw)

        flat = ring[:, :, :, :].rearrange("p a b n -> p (a b n)")
        W0, KV, TAIL = 0, 8192, 16384
        wslot = [part(flat, W0 + 4096 * n, KC, 512) for n in range(2)]
        xr = part(r_x, 0, 5, D)
        hT = part(r_h, 0, KC, TOK)
        mixT = part(r_mix, 0, KC, TOK)
        hn = [part(r_c, D * n, D) for n in range(2)]
        qh = part(r_c, 0, HG, TOK)
        fk = part(r_c, 4 * TOK, HG, TOK)
        mqT = part(r_c, 8 * TOK, 4, TOK)
        mkT = part(r_c, 12 * TOK, 4, TOK)
        vh = part(flat, TAIL, 5, 512)
        gh = part(flat, TAIL + 2560, 5, 512)
        mv = part(flat, TAIL + 5120, NT, 512)
        kds = part(flat, TAIL + 7168, 512)
        mkn = part(r_mix, 0, 5, 512)
        qtmp = [part(r_mix, 2560 + 512 * n, 512) for n in range(2)]
        at = KV
        hgt = {}
        for name, n in (("lf", TOK), ("b", TOK), ("bc", TOK), ("ta", TOK), ("tb", TOK), ("qd", TOK), ("dec", TOK),
                        ("qo", 3 * P), ("k1", SEQ), ("k2", SEQ), ("k3", SEQ)):
            hgt[name] = part(flat, at, n)
            at += n
        assert at <= TAIL
        hgt["kd"] = hgt["bc"]
        kb = [hgt["k1"], hgt["k2"], hgt["k3"]]
        atts = sb("atts", [NS, HG * NS])
        att = part(r_x, 0, HG, SEQ)
        state = part(r_x, 2048, 6, HG, HD)
        kdn = part(r_h, 0, NT, HG, HD)
        osq = part(r_mix, 0, 512)
        s0 = part(r_h, 0, NB, HG, HD)
        kdx = part(r_x, 0, NB, 512)
        qx = part(r_x, 4096, HG, NB * NS)
        pb = [[part(flat, KV + 512 * (4 * n + i), SEQ) for i in range(NT)] for n in range(2)]
        pt = [part(flat, KV + 4096 + 2048 * n, NT, SEQ) for n in range(2)]
        kbuf = [part(r_x, 0, NPG, 512), part(r_x, 2048, NPG, 512), part(r_c, 8 * TOK, NPG, 512)]
        vbuf = [part(flat, KV + 2048 * n, NPG, 512) for n in range(4)]
        kT = [part(r_h, 2048 * n, 4, PAST) for n in range(2)]
        sx = part(r_c, 0, PAST + NS)
        ptS = part(r_c, TOK, NPG, P)
        ptn = part(r_c, TOK + 512, P)
        osb = part(r_c, TOK + 512 + P, 512)
        qxm = part(r_c, 4 * TOK, 4, NB, 32)
        memx = part(r_c, 4 * TOK, MT, D)
        memT = part(flat, TAIL, KC, MEM)
        memk = part(flat, TAIL + 2048, MT, D)
        memv = part(flat, TAIL + 4096, MT, D)
        memkT = part(flat, TAIL + 6144, KC, MEM)
        qT = part(r_c, 0, KC, TOK)
        oT = part(r_c, 8 * TOK, KC, TOK)
        xp = [part(r_mix, 1024 * n, NT, MEM) for n in range(2)]
        xpt = [part(r_mix, 2048 + 1024 * n, MT, SEQ) for n in range(2)]
        xkbuf = [part(flat, TAIL + 2048 * n, MT, D) for n in range(3)]
        xvbuf = [part(flat, KV + 2048 * n, MT, D) for n in range(4)]
        xkT = [part(r_h, 2048 * n, KC, MEM) for n in range(2)]
        xsx = part(r_mix, 0, MEM)
        xptS = part(r_mix, MEM, MT, P)
        xosb = part(r_mix, 2 * MEM, 2, 512)
        qxx = part(flat, TAIL + 6144, KC, NB, 32)
        rt = {}
        at = 0
        for name, n in (("lg", 5 * 36), ("g8", 40), ("m8", 40), ("i8f", 5), ("ohg", 20), ("ge", 20), ("gw", 5),
                        ("pr", 5 * 32), ("se", 40), ("me", 40), ("ek", 10), ("ex", 5), ("eid", 10),
                        ("m", 2 * 5 * 32), ("ms", 5 * 32), ("cnt", 32), ("big", 32 * 8), ("ovn", 32),
                        ("ove", 32), ("ovs", 32), ("tmp", 2 * 5 * 32), ("rk", 10), ("qk", 10), ("rr", 10),
                        ("ovk", 10), ("sk", 10), ("t1", 10), ("t2", 10), ("ohs", 2 * 5 * NBLK),
                        ("ohr", 2 * 5 * CAP), ("cmp", XBLK * 32), ("exs", XBLK), ("bias", 36), ("wr", KC * 36)):
            rt[name] = part(r_mix, at, n)
            at += n
        assert at <= KC * TOK
        i8 = sb("i8", [P, 5, 8], U32)
        xg = part(r_c, 0, D)
        xT = part(r_c, 2048, KC, P)
        he = [part(r_c, 3072 + 512 * n, 512) for n in range(2)]
        h2 = [part(r_c, 4096 + 512 * n, 512) for n in range(2)]
        heT = [part(r_c, 5120 + 512 * n, 4, P) for n in range(2)]
        ys = [part(r_c, 6144 + 512 * n, 512) for n in range(2)]
        yg = [[part(b, at, D) for b, at in pair] for pair in
              (((r_c, 0), (r_c, D)), ((r_c, 2 * D), (r_c, 3 * D)), ((r_c, 4 * D), (r_c, 5 * D)),
               ((r_c, 6 * D), (r_c, 7 * D)), ((r_h, 0), (r_h, D)))]

        J = Banks(nc, psum, sem)
        x_in = [sem(f"x{i}_in") for i in range(5)]
        gain0_in, gain_in = sem("gain0_in"), sem("gain_in")
        const_in = sem("const_in")
        ident_in = sem("ident_in")
        w_in = [sem(f"wslot{n}_in") for n in range(2)]
        mem_in = sem("mem_in")
        s0_in = sem("s0_in")
        k_in = [sem(f"k{n}_in") for n in range(3)]
        v_in = sem("v_in")
        xk_in = [sem(f"xk{n}_in") for n in range(3)]
        xv_in = sem("xv_in")
        xr_in = sem("xr_in")
        rtw_in = sem("router_weights_in")
        rooted = sem("rooted")
        normed = sem("normed")
        exped = sem("exped")
        hgd, hga = sem("hg_exponents"), sem("hg_exps")
        zeroed = sem("zeroed")
        head_ready = sem("head_ready")
        o_gated, o_root, heads_done = sem("o_gated"), sem("o_root"), sem("heads_done")
        qkx_done = sem("qx_and_kdx_done")
        s_max, s_exp, s_share, s_prob = sem("s_max"), sem("s_exp"), sem("s_share"), sem("s_prob")
        qx_done = sem("qx_done")
        sc_full, sc_free = sem("sample_scores_full"), sem("sample_scores_free")
        ss_max, ss_exp, ss_prob = sem("ss_max"), sem("ss_exp"), sem("ss_prob")
        xs_max, xs_exp, xs_prob = sem("xs_max"), sem("xs_exp"), sem("xs_prob")
        xr_new = sem("xr_new")
        r_exp_in, r_exp = sem("router_exp_in"), sem("router_exp")
        onehots, routed = sem("onehots"), sem("routed")
        out_mk, out_mv, out_s, out_mem, out_s0 = (sem(f"out_{n}") for n in ("mk", "mv", "s", "mem", "s0"))
        rows_out = [sem(f"rows{n}_out") for n in range(2)]
        zeros_out = sem("zeros_out")
        a_step, v_step, p_step = sem("act_step"), sem("dve_step"), sem("pool_step")
        wm_in = [sem(f"moe_w{r}_in") for r in range(12)]
        wm_odd_in = [sem(f"moe_odd_w{r}_in") for r in range(4)]
        up_used, down_used = sem("moe_up_weights_used"), sem("moe_down_weights_used")
        xg_in = sem("xg_in")
        xt_full, xt_free = sem("xt_full"), sem("xt_free")
        up_exp, up_free = sem("up_exp"), sem("up_free")
        ht_full, ht_free = sem("ht_full"), sem("ht_free")
        y_free = sem("y_free")
        dve_moe = sem("dve_moe_steps")
        rows_in = [sem(f"out_rows{n}_in") for n in range(2)]
        moe_done, late_stored = sem("moe_done"), sem("late_stored")
        yg_in = [sem(f"yg{n}_in") for n in range(5)]
        fin_out = sem("fin_out")

        block = ctx.enter_context(nc.Block())
        CONSTS = [(ident, "c_ident"), (maskd, "c_maskd"), (masko, "c_masko"), (masks, "c_masks"),
                  (bsel, "c_bsel"), (scan, "c_scan"), (alibi, "c_alibi"), (sbias, "c_sbias"),
                  (before, "c_before"), (ones, "c_ones"), (iota, "c_iota"), (tokid, "c_tokid"),
                  (steps, "c_steps")]
        NCONST = 16 * (len(CONSTS) - 1 + 2)
        x_rows = a["x_prompt"].rearrange("b (i p) d -> p (b i) d", p=P)
        x_samp = a["x_sample"].rearrange("b t d -> (b t) d")
        y_rows = a["y_prompt"].rearrange("b (i p) d -> p (b i) d", p=P)
        y_samp = a["y_sample"].rearrange("b t d -> (b t) d")

        def rows(i):
            return P if i < NT else NS

        def tok(i):
            return slice(P * i, P * i + rows(i))

        last = {"hf": ("hf", 4), "hq": ("hq", 4), "mk": ("mk", 4), "mq": ("mq", 4), "mv": ("mv", 4),
                "hi": ("hi", 4), "hg": ("hg", 4)}
        for n in range(2):
            last[f"o{n}"] = ("x1", n, (NT, LAST_HALF[-1])[n])
            last[f"xk{n}"] = ("mem", n, 1)
            last[f"xv{n}"] = ("mem", 2 + n, 1)
            last[f"xq{n}"] = ("xq", n, 4)
            last[f"xo{n}"] = ("x2", n, (NT, LAST_HALF[-1])[n])

        w_moe = [a["w1"][0], a["w3"][0], a["w2"][0]]

        def moe_place(r, u):
            if u == 0 or r >= 4:
                return ring[:, r, :, :]
            return part(r_h if r < 2 else r_mix, 2 * D * (r % 2), 2, D)

        def moe_in(r, u):
            return wm_odd_in[r] if u and r < 4 else wm_in[r]

        def reused(j, c):
            return not isinstance(j, int) or 2 * j + c >= 2

        def moe_chunk(r, e):
            m, q = (r % 2, r // 2) if r < 8 else (2, r - 8)
            return w_moe[m][e][256 * q:256 * (q + 1), :].rearrange("(a p) n -> p a n", p=P)

        def load_pages(eng, pages, dst, pool_name, b, s):
            for j in range(NPG):
                src = a[pool_name][0][bass.ds(pages[b][j], 1)].rearrange("a r h d -> (a r) (h d)")
                eng.dma_start(dst[:, j, :], src).then_inc(s, 16)

        @block.sync
        def _(sp):
            for i in range(NT):
                sp.dma_start(xr[:, i, :], x_rows[:, i, :]).then_inc(x_in[i], 16)
                if i == 0:
                    sp.dma_start(gain[:, :], a["g_mix"].to_broadcast([P, D])).then_inc(gain0_in, 16)
            sp.dma_start(xr[0:NS, NT, :], x_samp).then_inc(x_in[NT], 16)
            def weights(tag):
                n = WPOS[tag]
                name, col, _ = WBLOCKS[n]
                if n >= 2:
                    J.wait_filled(sp, *last[WBLOCKS[n - 2][2]])
                src = a[name][0].rearrange("(k p) n -> p k n", p=P)[:, :, 512 * col:512 * (col + 1)]
                sp.dma_start(wslot[n % 2], src).then_inc(w_in[n % 2], 16)

            def value_pages(g):
                for b in range(4 * g, 4 * g + 4):
                    load_pages(sp, pages, vbuf[b % 4], "cache_moba_v", b, v_in)

            def mem_values(g):
                for b in range(4 * g, 4 * g + 4):
                    sp.dma_start(xvbuf[b % 4], a["cache_mem_v"][0][b].rearrange("(m p) h d -> p m (h d)", p=P))\
                        .then_inc(xv_in, 16)

            def key_pages(b):
                load_pages(sp, pages, kbuf[b % 3], "cache_moba_k", b, k_in[b % 3])

            for tag in ("mk", "hf", "hq", "mq", "mv", "hg", "hi", "xk0", "xk1"):
                weights(tag)
            pages = [[sp.value_load(a["page_table"][b:b + 1, j:j + 1], min_val=0, max_val=NPHYS - 1)
                      for j in range(NPG)] for b in range(NB)]
            J.wait_filled(sp, "OT", 3)
            value_pages(0)
            J.wait_emptied(sp, "Us", NB - 1)
            key_pages(0)
            key_pages(1)
            sp.wait_ge(qx_done, 1)
            key_pages(2)
            for tag in ("xv0", "xv1", "o0"):
                weights(tag)
            for b in range(3, 8):
                J.wait_filled(sp, "KT", b - 3, 3)
                key_pages(b)
            J.wait_filled(sp, "Os", 0)
            value_pages(1)
            weights("o1")
            J.wait_filled(sp, "Os", 1)
            mem_values(0)
            for tag in ("xq0", "xq1", "xo0", "xo1"):
                weights(tag)
            J.wait_filled(sp, "XOs", 0, 1)
            mem_values(1)
            J.wait_filled(sp, "XOs", 1, 1)
            for r in range(4, 12):
                sp.dma_start(moe_place(r, 0), moe_chunk(r, 0)).then_inc(wm_in[r], 16)
            for half in range(2):
                J.wait_filled(sp, *last[f"xo{half}"])
                slot = WPOS[f"xo{half}"] % 2
                for r in (2 * slot, 2 * slot + 1):
                    sp.dma_start(moe_place(r, 0), moe_chunk(r, 0)).then_inc(wm_in[r], 16)

            J.wait_filled(sp, "logit", LAST_HALF[-1])
            for r in range(2):
                sp.dma_start(moe_place(r, 1), moe_chunk(r, 1)).then_inc(moe_in(r, 1), 16)
            sp.wait_ge(xg_in, 16)
            for r in range(2, 4):
                sp.dma_start(moe_place(r, 1), moe_chunk(r, 1)).then_inc(moe_in(r, 1), 16)

            def first_weights(b, n, u, expert):
                for r in range(4):
                    sp.wait_ge(up_used, 8 * b + (8 * n + r - 15))
                    sp.dma_start(moe_place(r, u), moe_chunk(r, expert)).then_inc(moe_in(r, u), 16)

            def up_weights(b, n, expert):
                for r in range(4, 8):
                    sp.wait_ge(up_used, 8 * b + (8 * n + r - 7))
                    sp.dma_start(moe_place(r, 0), moe_chunk(r, expert)).then_inc(wm_in[r], 16)

            def down_weights(b, n, expert, parts=(8, 9, 10, 11)):
                for place, r in enumerate(parts):
                    if max(parts[:place + 1]) == r:
                        sp.wait_ge(down_used, 4 * b + (4 * n + r - 11))
                    sp.dma_start(moe_place(r, 0), moe_chunk(r, expert)).then_inc(wm_in[r], 16)

            first_weights(0, 2, 0, 2)
            up_weights(0, 1, 1)
            with sp.Fori(1, NE - 3, 2) as e:
                for n in range(2):
                    first_weights(e, n + 2, 1 - n, e + (n + 2))
                    up_weights(e, n + 1, e + (n + 1))
                    down_weights(e, n, e + n, (9, 8, 10, 11) if n else (8, 9, 10, 11))
            first_weights(0, NE - 1, 1, NE - 1)
            up_weights(0, NE - 2, NE - 2)
            down_weights(0, NE - 3, NE - 3)
            up_weights(0, NE - 1, NE - 1)
            down_weights(0, NE - 2, NE - 2)
            down_weights(0, NE - 1, NE - 1)
            n_ov = sp.value_load(ovi[0:1, 0:1], min_val=0, max_val=XBLK)
            with sp.If(n_ov > 0):
                with sp.Fori(0, XBLK // 2) as j:
                    with sp.If(2 * j < n_ov):
                        for u in range(2):
                            ex = sp.value_load(ovi[0:1, bass.ds(2 * j + (u + 1), 1)], min_val=0, max_val=NE - 1)
                            first_weights(2 * j, NE + u, u, ex)
                            up_weights(2 * j, NE + u, ex)
                            down_weights(2 * j, NE + u, ex)
            for i, r in TILES:
                sp.wait_ge(normed, 18 + i)
                sp.dma_start(y_rows[:, i, :] if i < NT else y_samp, yg[i][0][0:r, :]).then_inc(fin_out, 16)
            sp.wait_ge(fin_out, 80)

        @block.gpsimd
        def _(pool):
            for n, (buf, name) in enumerate(CONSTS):
                if n == 1:
                    pool.wait_ge(x_in[NT], 16)
                full = buf[:, :] if len(buf.shape) == 2 else buf[:, :, :].rearrange("p a b -> p (a b)")
                q = ident_in if name == "c_ident" else const_in
                pool.dma_start(full, a[name]).then_inc(q, 16)
            pool.dma_start(lbl[:, :, :], a["hg_lb"].rearrange("l (h k) -> k l h", k=HD),
                           allow_slow_non_contiguous=True).then_inc(const_in, 16)
            pool.dma_start(ghn[:, :], a["hg_norm"].to_broadcast([P, HD])).then_inc(const_in, 16)
            pool.memset(zeros[:, :], 0.0).then_inc(p_step, 1)
            pool.wait_ge(p_step, 1)
            n = XBLK * CAP * D // P // P
            pool.dma_start(out_rows[NE * CAP:, :].rearrange("(p r) (c d) -> p (r c) d", p=P, d=P),
                           zeros[:, :].unsqueeze(1).to_broadcast([P, n, P])).then_inc(zeros_out, 16)
            pool.wait_ge(normed, 5)
            pool.memset(part(r_x, 0, 2048), 0.0).then_inc(zeroed, 1)
            pool.memset(part(flat, KV + 7 * TOK + 3 * P, 3 * SEQ), 0.0).then_inc(zeroed, 1)
            pool.memset(atts[:, :], 0.0).then_inc(zeroed, 1)
            J.wait_filled(pool, "kds", HG - 1)
            pool.dma_start(memx, a["mem_prompt"].rearrange("b (i p) d -> p (b i) d", p=P)).then_inc(mem_in, 16)
            J.wait_filled(pool, "U", NCH - 1)
            pool.dma_start(s0, a["state_hgrn"][0].rearrange("b h k v -> k b h v")).then_inc(s0_in, 16)
            pool.dma_start(gain[:, :], a["g_mem"].to_broadcast([P, D])).then_inc(gain_in, 16)
            J.wait_emptied(pool, "Us", NB - 1)
            pool.dma_start(a["hg_sample"][0].rearrange("b h k v -> k b h v"), s0).then_inc(out_s0, 16)
            pool.wait_ge(normed, 7)
            pool.dma_start(gain[:, :], a["g_cross"].to_broadcast([P, D])).then_inc(gain_in, 16)
            J.wait_filled(pool, "KT", NB - 1, 3)
            pool.dma_start(xr[:, 0:NT, :], x_rows).then_inc(xr_in, 16)
            pool.dma_start(xr[0:NS, NT, :], x_samp).then_inc(xr_in, 16)
            J.wait_filled(pool, "mem", 3, 1)
            pool.wait_ge(out_mem, 32)
            for b in range(NB):
                if b == 2:
                    pool.wait_ge(normed, 12)
                    pool.dma_start(gain[:, :], a["g_ffn"].to_broadcast([P, D])).then_inc(gain_in, 16)
                    J.wait_filled(pool, "XOT", XH - 1, 1)
                if b >= 3:
                    J.wait_filled(pool, "XKT", b - 3, 3)
                pool.dma_start(xkbuf[b % 3], a["cache_mem_k"][0][b].rearrange("(m p) h d -> p m (h d)", p=P))\
                    .then_inc(xk_in[b % 3], 16)
            J.wait_filled(pool, "XOsT", 1, 1)
            wr = rt["wr"].rearrange("p (k n) -> p k n", k=KC)
            pool.dma_start(wr[:, :, 0:NG], a["w_grp"][0].rearrange("(k p) n -> p k n", p=P)).then_inc(rtw_in, 16)
            pool.dma_start(wr[:, :, NG:36], a["w_exp"][0].rearrange("(k p) n -> p k n", p=P)).then_inc(rtw_in, 16)
            pool.dma_start(rt["bias"][:, 0:NG], a["b_grp"].to_broadcast([P, NG])).then_inc(rtw_in, 16)
            pool.dma_start(rt["bias"][:, NG:36], a["b_exp"].to_broadcast([P, NE])).then_inc(rtw_in, 16)
            pool.wait_ge(normed, 17)
            pool.dma_start(gain[:, :], a["g_final"].to_broadcast([P, D])).then_inc(gain_in, 16)

            pool.wait_ge(routed, 1)
            pool.wait_ge(rows_out[0], 48)
            pool.wait_ge(rows_out[1], 32)

            def gather(c):
                if c:
                    pool.wait_ge(xt_full, c)
                pool.indirect_dma_start(xg, None, tok_rows, bass.IndirectOffsetOnAxis(ap=table[:, c:c + 1], axis=0))\
                    .then_inc(xg_in, 16)

            for c in range(NE // 2):
                gather(c)
            n_ov = pool.value_load(ovi[0:1, 0:1], min_val=0, max_val=XBLK)
            for c in range(NE // 2, NBLK // 2):
                with pool.If(n_ov > 2 * c - NE):
                    gather(c)
            pool.wait_ge(moe_done, 1)
            for n in range(2):
                pool.wait_ge(rows_in[n], 32 * NE // 2)
            for i, r in TILES:
                for k in range(2):
                    pool.indirect_dma_start(yg[i][k][0:r, :], None, out_rows,
                                            bass.IndirectOffsetOnAxis(ap=yidx[0:r, k, i:i + 1], axis=0))\
                        .then_inc(yg_in[i], 16)

        @block.scalar
        def _(act):
            st = Steps(a_step)

            def rstd_root(n, src, width, out_junk):
                r = src.shape[0]
                st.did(act.activation(out_junk, src, ACT.Square, accum_out=ss[0:r, n:n + 1]))
                st.settle(act)
                act.activation(y0[0:r, n:n + 1], ss[0:r, n:n + 1], ACT.Sqrt, scale=1.0 / width, bias=EPS)\
                    .then_inc(rooted, 1)

            def norm_root(n, src):
                r = src.shape[0]
                rstd_root(n, src, D, hn[n % 2][0:r, :])

            def evac(out, *name, view=None):
                J.wait_filled(act, *name)
                src = J.bank(*name)
                J.empties(act.activation(out, view(src) if view else src, ACT.Copy), *name)

            def sample_rows(*what):
                evac(srows[:, :], *what, "rows", view=lambda s: s[:, 0:P])

            def turned(what, i):
                evac(hT[:, 0:4, tok(i)], what, i, 0,
                     view=lambda s: s.rearrange("p (k t) -> p k t", k=4)[:, :, 0:rows(i)])

            def rows_evac(dst, what, i):
                if i < NT:
                    evac(dst, what, i)
                    return
                J.wait_filled(act, what, i)
                for n in range(4):
                    ins = act.activation(dst[0:NS, P * n:P * (n + 1)], J.bank(what, i)[NS * n:NS * (n + 1), 0:P], ACT.Copy)
                J.empties(ins, what, i)

            for i, r in TILES:
                act.wait_ge(x_in[i], 16)
                if i >= 2:
                    J.wait_filled(act, "hT", i - 2, 1)
                norm_root(i, xr[0:r, i, :])
                if i:
                    turned("hT", i - 1)
                if i >= 2:
                    rows_evac(mkn[:, i - 2, :], "mk", i - 2)
            turned("hT", NT)
            for i in (NT - 1, NT):
                rows_evac(mkn[:, i, :], "mk", i)
            J.wait_emptied(act, "mk", NT)
            act.dma_start(a["mk_prompt"][0, 0].rearrange("(i p) h d -> p i (h d)", p=P), mkn[:, 0:NT, :]).then_inc(out_mk, 16)
            act.dma_start(a["mk_sample"][0].rearrange("b t h d -> (b t) (h d)"), mkn[0:NS, NT, :]).then_inc(out_mk, 16)
            sample_rows("hf")
            for c in range(5):
                J.wait_filled(act, "hf", c)
                s = J.bank("hf", c)
                if c < 4:
                    J.empties(act.activation(fk[:, c, 0:SEQ], s, ACT.Exp, scale=-1.0), "hf", c)
                else:
                    J.empties(act.activation(fk[:, :, SEQ:TOK], s[:, 0:128].rearrange("p (c t) -> p c t", c=4),
                                             ACT.Exp, scale=-1.0), "hf", c)
            sample_rows("hq")
            for c in range(5):
                J.wait_filled(act, "hq", c)
                if c >= 2:
                    J.wait_emptied(act, "hq", c - 2)
                n = SEQ if c < 4 else 128
                act.activation(qtmp[c % 2][:, 0:n], J.bank("hq", c)[:, 0:n], ACT.Exp, scale=-1.0).then_inc(exped, 1)
            act.wait_ge(hgd, 1)
            act.activation(lb[:, :], lb[:, :], ACT.Exp).then_inc(hga, 1)

            def head_log(h):
                act.wait_ge(hgd, 2 * h + 2)
                act.activation(hgt["lf"], fk[:, h, :], ACT.Ln).then_inc(hga, 1)

            def head_exps(h):
                act.wait_ge(hgd, 2 * h + 3)
                b3 = hgt["b"][:, 0:SEQ].rearrange("p (c t) -> p c t", t=CH)
                bs = hgt["b"][:, SEQ:TOK].rearrange("p (c t) -> p c t", t=NQ)
                act.activation(hgt["tb"], hgt["ta"], ACT.Exp).then_inc(hga, 1)
                act.activation(hgt["bc"], hgt["ta"], ACT.Exp, scale=-1.0).then_inc(hga, 1)
                act.activation(hgt["qo"], hgt["qo"], ACT.Exp).then_inc(hga, 1)
                for j in range(3):
                    v = kb[j].rearrange("p (c t) -> p c t", t=CH)[:, :, 0:SUB * (j + 1)]
                    act.activation(v, v, ACT.Exp).then_inc(hga, 1)
                act.activation(hgt["dec"], hgt["dec"], ACT.Exp).then_inc(hga, 1)
                act.activation(dl[:, h, 0:NCH], b3[:, :, CH - 1], ACT.Exp).then_inc(hga, 1)
                act.activation(dl[:, h, NCH:NCH + NB], bs[:, :, NQ - 1], ACT.Exp).then_inc(hga, 1)
                act.activation(hgt["lf"], hgt["b"], ACT.Exp).then_inc(hga, 1)

            sample_rows("mq")
            for c in range(5):
                J.wait_filled(act, "mq", c)
                s = J.bank("mq", c)
                if c < 4:
                    ins = act.activation(mqT[:, c, 0:SEQ], s, ACT.Copy, scale=MD ** -0.5)
                else:
                    ins = act.activation(mqT[:, :, SEQ:TOK], s[:, 0:128].rearrange("p (c t) -> p c t", c=4),
                                         ACT.Copy, scale=MD ** -0.5)
                J.empties(ins, "mq", c)
                if c == 1:
                    head_log(0)
                if c == 2:
                    head_exps(0)
            for c in range(5):
                if c < 4:
                    evac(mkT[:, c, 0:SEQ], "mkT", c)
                else:
                    evac(mkT[:, :, SEQ:TOK], "mkT", c, view=lambda s: s[:, 0:128].rearrange("p (c t) -> p c t", c=4))
            for i, r in TILES:
                rows_evac(mv[:, i, :] if i < NT else mvs, "mv", i)
                if i == 0:
                    head_log(1)
                if i == 1:
                    head_exps(1)
            J.wait_emptied(act, "mv", NT)
            act.dma_start(a["mv_prompt"][0, 0].rearrange("(i p) h d -> p i (h d)", p=P), mv).then_inc(out_mv, 16)
            act.dma_start(a["mv_sample"][0].rearrange("b t h d -> (b t) (h d)"), mvs[:, :]).then_inc(out_mv, 16)
            for i, r in TILES:
                J.wait_filled(act, "hg", i)
                if i < NT:
                    ins = act.activation(gh[:, i, :], J.bank("hg", i), ACT.Exp, scale=-1.0)
                else:
                    for n in range(4):
                        ins = act.activation(gh[0:NS, i, P * n:P * (n + 1)], J.bank("hg", i)[NS * n:NS * (n + 1), 0:P],
                                             ACT.Exp, scale=-1.0)
                ins.then_inc(exped, 1)
                if i == 0:
                    head_log(2)
                if i == 1:
                    head_exps(2)
            for i, r in TILES:
                rows_evac(vh[:, i, :], "hi", i)
                if i == 0:
                    head_log(3)
                if i == 1:
                    head_exps(3)
            for h in range(HG):
                evac(kdn[:, :, h, :], "kdn", h, view=lambda s: s.rearrange("p (i k) -> p i k", i=NT))
            for h in range(HG):
                evac(kds[0:NS, HD * h:HD * (h + 1)], "kds", h, view=lambda s: s[0:NS, 0:HD])

            def head_squares(i):
                r = rows(i)
                J.wait_filled(act, "o", i)
                act.wait_ge(o_gated, i + 1)
                src = J.bank("o", i)
                for h in range(HG):
                    ins = act.activation(osq[0:r, HD * h:HD * (h + 1)], src[0:r, HD * h:HD * (h + 1)],
                                         ACT.Square, accum_out=hss[0:r, i, h:h + 1])
                    if h < HG - 1:
                        st.did(ins)
                J.empties(ins, "o", i)

            def turn_heads(i):
                evac(mixT[:, 0:HG, tok(i)], "hgT", i,
                     view=lambda s: s.rearrange("p (h t) -> p h t", h=HG)[:, :, 0:rows(i)])

            def probs(n):
                h, i = n // NT, n % NT
                act.wait_ge(s_share, n + 1)
                p = pb[h % 2][i][:, 0:P * (i + 1)]
                act.activation(p, p, ACT.Copy, scale=stat[:, 3, n % 8:n % 8 + 1]).then_inc(s_prob, 1)

            def moba_step(h):
                def turned_probs(k):
                    if h > 2:
                        J.wait_filled(act, "OT", (h - 3) // 2)
                    evac(pt[(h - 1) % 2][:, k, P * k:SEQ], "PT", h - 1, k, view=lambda s: s[:, 0:SEQ - P * k])

                if h < MB:
                    for i in range(NT):
                        n = NT * h + i
                        act.wait_ge(s_max, n + 1)
                        p = pb[h % 2][i][:, 0:P * (i + 1)]
                        act.activation(p, p, ACT.Exp, bias=stat[:, 1, n % 8:n % 8 + 1],
                                       accum_out=stat[:, 2, n % 8:n % 8 + 1]).then_inc(s_exp, 1)
                        if h and i < NT // 2:
                            turned_probs(2 * i)
                            turned_probs(2 * i + 1)
                        if i:
                            probs(n - 1)
                    probs(n)
                if h:
                    if h == MB:
                        for k in range(NT):
                            turned_probs(k)
                    if h % 2 == 0:
                        evac(mixT[:, 4 + h // 2 - 1, 0:SEQ], "OT", h // 2 - 1)

            act.wait_ge(out_mk, 32)
            J.wait_emptied(act, "hq", 4)
            for i in range(NT):
                moba_step(2 * i)
                head_squares(i)
                moba_step(2 * i + 1)
            J.wait_emptied(act, "U", NCH - 1)
            act.dma_start(a["hg_prompt"][0, 0].rearrange("h k v -> k h v"), state[:, NCH % 6, :, :]).then_inc(out_s, 16)
            moba_step(MB)
            for i0, i1, r in ((0, NT, P), (NT, NT + 1, NS)):
                if i0 == NT:
                    head_squares(NT)
                J.wait_emptied(act, "o", i1 - 1)
                act.activation(hy0[0:r, i0:i1, :], hss[0:r, i0:i1, :], ACT.Sqrt, scale=1.0 / HD, bias=EPS)\
                    .then_inc(o_root, 1)
            act.wait_ge(mem_in, 16)
            act.wait_ge(qkx_done, 1)
            for i in range(MT):
                norm_root(5 + i, memx[:, i, :])
            for i, _ in TILES:
                turn_heads(i)

            for i in range(MT):
                evac(memT[:, 0:4, P * i:P * (i + 1)], "memT", i, 0, view=lambda s: s.rearrange("p (k t) -> p k t", k=4))
            act.wait_ge(out_mv, 32)
            for n in range(4):
                dst = (memk, memv)[n // 2]
                evac(dst[:, 0, 512 * (n % 2):512 * (n % 2 + 1)], "mem", n, 0)
                if n == 1:
                    for c in (0, 2):
                        evac(memkT[:, 2 * c:2 * c + 2, :], "memKT", c, view=lambda s: s.rearrange("p (k t) -> p k t", k=2))
                if n % 2:
                    J.wait_emptied(act, "mem", n, 0)
                    J.wait_emptied(act, "mem", n, 1)
                    out = a[("xk_prompt", "xv_prompt")[n // 2]][0, 0].rearrange("(i p) h d -> p i (h d)", p=P)
                    act.dma_start(out, dst).then_inc(out_mem, 16)

            def keys_turned(b):
                if b >= 2:
                    act.wait_ge(sc_full, b // 2)
                else:
                    act.wait_ge(out_s0, 16)
                for c in (0, 2):
                    evac(kT[b % 2][:, c, :], "KT", b, c)

            def sample_exps(g):
                act.wait_ge(ss_max, g + 1)
                act.activation(sx, sx, ACT.Exp, bias=stat[:, 1, 0:1], accum_out=stat[:, 2, 0:1]).then_inc(ss_exp, 1)

            def sample_probs(g):
                if g:
                    J.wait_filled(act, "Os", g - 1)
                evac(ptS, "Pt", g, view=lambda s: s.rearrange("p (j n) -> p j n", j=NPG))

            def sample_out(g):
                if g:
                    J.wait_filled(act, "OsT", g - 1)
                evac(osb, "Os", g)

            for b in range(4):
                keys_turned(b)
            sample_exps(0)
            keys_turned(4)
            keys_turned(5)
            sample_probs(0)
            sample_out(0)
            keys_turned(6)
            keys_turned(7)
            sample_exps(1)
            sample_probs(1)
            sample_out(1)

            for n, i in enumerate(LAST_HALF):
                if n >= 2:
                    turned("h2T", LAST_HALF[n - 2])
                    J.wait_filled(act, "h2T", LAST_HALF[n - 2], 1)
                J.wait_emptied(act, "x1", 1, i)
                norm_root(7 + n, xr[0:rows(i), i, :])
            for i in LAST_HALF[3:]:
                turned("h2T", i)

            def scaled_q(half, c):
                J.wait_filled(act, "xq", half, c)
                s = J.bank("xq", half, c)
                if c < 4:
                    ins = act.activation(qT[:, 4 * half + c, 0:SEQ], s, ACT.Copy, scale=XD ** -0.5)
                else:
                    ins = act.activation(qT[:, 4 * half:4 * half + 4, SEQ:TOK],
                                         s[:, 0:128].rearrange("p (c t) -> p c t", c=4), ACT.Copy, scale=XD ** -0.5)
                J.empties(ins, "xq", half, c)

            for half in range(2):
                sample_rows("xq", half)
                for c in (0, 2, 4):
                    scaled_q(half, c)
            act.wait_ge(out_mem, 32)
            for h in range(XH + 1):
                if h < XH:
                    for i2 in range(2):
                        act.wait_ge(xs_max, 2 * h + i2 + 1)
                        s = J.bank("XS", h, i2)
                        for u in range(2):
                            n = (2 * i2 + u) + 4 * (h % 2)
                            ins = act.activation(xp[h % 2][:, 2 * i2 + u, :], s[:, MEM * u:MEM * (u + 1)], ACT.Exp,
                                                 bias=stat[:, 1, n:n + 1], accum_out=stat[:, 2, n:n + 1])
                            if u == 0:
                                st.did(ins)
                        J.empties(ins, "XS", h, i2)
                if h:
                    for c in range(2):
                        evac(oT[:, 2 * (h - 1) + c, 0:SEQ], "XOT", h - 1, c)

            def mem_keys_turned(b):
                if b >= 2:
                    act.wait_ge(sc_full, NB // 2 + b // 2)
                for c in (0, 2):
                    evac(xkT[b % 2][:, 2 * c:2 * c + 2, :], "XKT", b, c, view=lambda s: s.rearrange("p (k t) -> p k t", k=2))

            def mem_exps(g):
                act.wait_ge(xs_max, 2 * XH + g + 1)
                act.activation(xsx, psum[6][:, 0:MEM], ACT.Exp, bias=stat[:, 1, 0:1], accum_out=stat[:, 2, 0:1])\
                    .then_inc(xs_exp, 1)

            def mem_probs(g):
                if g:
                    J.wait_filled(act, "XOs", g - 1, 1)
                evac(xptS, "XPt", g, view=lambda s: s[:, 0:MT * P].rearrange("p (j n) -> p j n", j=MT))

            def mem_out(g):
                if g:
                    J.wait_filled(act, "XOsT", g - 1, 0)
                evac(xosb[:, 0, :], "XOs", g, 0)

            for b in range(4):
                mem_keys_turned(b)
            mem_exps(0)
            mem_keys_turned(4)
            mem_probs(0)
            mem_out(0)
            mem_keys_turned(5)
            mem_keys_turned(6)
            mem_keys_turned(7)
            mem_exps(1)
            mem_probs(1)
            mem_out(1)

            def stored_and_turned(n):
                i = LAST_HALF[n]
                act.wait_ge(normed, 13 + n)
                act.dma_start(tok_rows[P * i:P * i + rows(i), :], hn[n % 2][0:rows(i), :]).then_inc(rows_out[n % 2], 16)
                turned("h3T", i)

            for n, i in enumerate(LAST_HALF):
                if n >= 2:
                    stored_and_turned(n - 2)
                    J.wait_filled(act, "h3T", LAST_HALF[n - 2], 1)
                    act.wait_ge(rows_out[n % 2], 16 * (n // 2))
                J.wait_emptied(act, "x2", 1, i)
                norm_root(12 + n, xr[0:rows(i), i, :])
            for n in range(3, 5):
                stored_and_turned(n)
            act.wait_ge(r_exp_in, 1)
            act.activation(rt["ge"], rt["ge"], ACT.Exp).then_inc(r_exp, 1)
            act.wait_ge(r_exp_in, 2)
            act.activation(rt["ex"], rt["ex"], ACT.Exp).then_inc(r_exp, 1)

            def rows_turned(j):
                act.wait_ge(xt_full, j + 1)
                act.activation(xT[:, 4:8, :], psum[1].rearrange("p (k t) -> p k t", k=4), ACT.Copy).then_inc(xt_free, 1)

            def gate_exp(j, c):
                u = c % 2
                act.wait_ge(up_used, 16 * j + 8 * (c + 1))
                if reused(j, c):
                    act.wait_ge(up_free, 2 * j + (c - 1))
                act.activation(he[u], psum[2 + 2 * u], ACT.Exp, scale=-1.0).then_inc(up_exp, 1)

            def down(j, c):
                u = c % 2
                act.wait_ge(ht_full, 2 * j + (c + 1))
                act.activation(heT[u].rearrange("p c t -> p (c t)"), psum[6], ACT.Copy).then_inc(ht_free, 1)
                act.wait_ge(down_used, 8 * j + 4 * (c + 1))
                if reused(j, c):
                    act.wait_ge(rows_in[u], 32 * (j if c >= 0 else j - 1))
                act.activation(ys[u], psum[7], ACT.Copy).then_inc(y_free, 1)
                act.wait_ge(y_free, 2 * j + (c + 1))
                for half in range(2):
                    act.dma_start(out_rows[bass.ds(2 * CAP * j + CAP * c, CAP), 512 * half:512 * (half + 1)],
                                  ys[u][CAP * half:CAP * (half + 1), :]).then_inc(rows_in[u], 16)

            def pair(j):
                gate_exp(j, 0)
                down(j, -1)
                gate_exp(j, 1)
                rows_turned(j + 1)
                down(j, 0)

            rows_turned(0)
            gate_exp(0, 0)
            gate_exp(0, 1)
            rows_turned(1)
            down(0, 0)
            pair(1)
            with act.Fori(2, NE // 2 - 1) as j:
                pair(j)
            gate_exp(NE // 2 - 1, 0)
            down(NE // 2 - 1, -1)
            gate_exp(NE // 2 - 1, 1)
            down(NE // 2 - 1, 0)
            down(NE // 2 - 1, 1)
            act.wait_ge(zeros_out, 16)
            n_ov = act.value_load(ovi[0:1, 0:1], min_val=0, max_val=XBLK)
            with act.If(n_ov > 0):
                with act.Fori(NE // 2, NBLK // 2) as j:
                    with act.If(2 * j - NE < n_ov):
                        rows_turned(j)
                        for u in range(2):
                            gate_exp(j, u)
                            down(j, u)
                        for u in range(2):
                            act.wait_ge(rows_in[u], 32 * j + 32)
                        act.activation(nt[0:1, 3, bass.ds(j - NE // 2, 1)], ss[0:1, 0:1], ACT.Copy).then_inc(late_stored, 1)
            act.activation(nt[0:1, 3, 21:22], ss[0:1, 0:1], ACT.Copy).then_inc(moe_done, 1)
            act.activation(nt[0:1, 3, 20:21], ss[0:1, 0:1], ACT.Sqrt)
            for i, r in TILES:
                act.wait_ge(xr_new, i + 1)
                rstd_root(17 + i, xr[0:r, i, :], D, yg[i][0][0:r, :])
            act.wait_ge(out_mk, 32)
            act.wait_ge(out_mv, 32)
            act.wait_ge(out_s, 16)
            act.wait_ge(out_mem, 32)
            act.wait_ge(out_s0, 16)

        @block.vector
        def _(dve):
            st = Steps(v_step)

            def v(ins):
                st.did(ins)
                st.settle(dve)

            def evac(out, *name, view=None):
                J.wait_filled(dve, *name)
                src = J.bank(*name)
                J.empties(dve.tensor_copy(out, view(src) if view else src), *name)

            def refined(root, mean_src, width, tmp, cols):
                v(dve.reciprocal(root, root))
                v(dve.tensor_scalar(tmp[0], mean_src, 1.0 / width, EPS, ALU.mult, ALU.add))
                v(dve.tensor_tensor(tmp[1], tmp[0], root, ALU.mult))
                v(dve.tensor_tensor(tmp[1], tmp[1], root, ALU.mult))
                v(dve.tensor_scalar(tmp[1], tmp[1], -0.5, 1.5, ALU.mult, ALU.add))
                v(dve.tensor_tensor(tmp[2], tmp[1], root, ALU.mult))
                return tmp[2]

            def norm_scale(n, src, out):
                r = src.shape[0]
                dve.wait_ge(rooted, n + 1)
                y = refined(y0[0:r, n:n + 1], ss[0:r, n:n + 1], D, [nt[0:r, k, n:n + 1] for k in range(3)], 1)
                dve.scalar_tensor_tensor(out=out, in0=src, scalar=y, in1=gain[0:r, :], op0=ALU.mult, op1=ALU.mult)\
                    .then_inc(normed, 1)

            def turned(what, i):
                evac(hT[:, 4:8, tok(i)], what, i, 1,
                     view=lambda s: s.rearrange("p (k t) -> p k t", k=4)[:, :, 0:rows(i)])

            dve.wait_ge(gain0_in, 16)
            for i, r in TILES:
                norm_scale(i, xr[0:r, i, :], hn[i % 2][0:r, :])
                if i:
                    turned("hT", i - 1)
            turned("hT", NT)
            dve.wait_ge(const_in, NCONST)
            dve.tensor_tensor(lb[:, :], lbl[:, 1, :], lbl[:, 0, :], ALU.subtract).then_inc(hgd, 1)
            for c in range(5):
                dve.wait_ge(exped, c + 1)
                n = SEQ if c < 4 else 128
                t = qtmp[c % 2][:, 0:n]
                v(dve.tensor_scalar(t, t, 1.0, None, ALU.add))
                v(dve.reciprocal(t, t))
                s = J.bank("hq", c)
                if c < 4:
                    ins = dve.tensor_tensor(qh[:, c, 0:SEQ], s, t, ALU.mult)
                else:
                    ins = dve.tensor_tensor(qh[:, :, SEQ:TOK], s[:, 0:n].rearrange("p (c t) -> p c t", c=4),
                                            t.rearrange("p (c t) -> p c t", c=4), ALU.mult)
                J.empties(ins, "hq", c)
            dve.wait_ge(hga, 1)
            v(dve.tensor_scalar(lb[:, :], lb[:, :], 1.0, None, ALU.add))
            v(dve.reciprocal(lb[:, :], lb[:, :]))
            v(dve.tensor_scalar(omlb[:, :], lb[:, :], -1.0, 1.0, ALU.mult, ALU.add))
            J.wait_emptied(dve, "hf", 4)
            dve.wait_ge(zeroed, 3)
            t = hgt

            def cut(x, size, lo, hi):
                return x[:, lo:hi].rearrange("p (c t) -> p c t", t=size)

            def gate_share(h):
                v(dve.tensor_scalar(fk[:, h, :], fk[:, h, :], 1.0, None, ALU.add))
                v(dve.reciprocal(fk[:, h, :], fk[:, h, :]))

            def decayed(h):
                f = fk[:, h, :]
                dve.tensor_scalar(f, f, omlb[:, h:h + 1], lb[:, h:h + 1], ALU.mult, ALU.add).then_inc(hgd, 1)
                dve.wait_ge(hga, 11 * h + 2)
                st.did(dve.tensor_scalar(f, f, -1.0, 1.0, ALU.mult, ALU.add))
                st.did(dve.tensor_scalar(t["tb"], t["lf"], -21.0, None, ALU.max))
                v(dve.tensor_tensor_scan(t["b"], scan[:, :], t["lf"], 0.0, ALU.mult, ALU.add))
                v(dve.tensor_tensor_scan(t["bc"], scan[:, :], t["tb"], 0.0, ALU.mult, ALU.add))
                b8 = cut(t["bc"], SUB, 0, SEQ)
                st.did(dve.tensor_tensor(cut(t["ta"], SUB, 0, SEQ), b8,
                                         b8[:, :, 3:4].to_broadcast([P, SEQ // SUB, SUB]), ALU.subtract))
                b4 = cut(t["bc"], NQ, SEQ, TOK)
                st.did(dve.tensor_tensor(cut(t["ta"], NQ, SEQ, TOK), b4,
                                         b4[:, :, 1:2].to_broadcast([P, NB, NQ]), ALU.subtract))
                bj = t["b"][:, 0:SEQ].rearrange("p (c j u) -> p j c u", j=CH // SUB, u=SUB)
                qo = t["qo"].rearrange("p (j c u) -> p j c u", j=3, u=SUB)
                for j in range(3):
                    st.did(dve.tensor_tensor(qo[:, j], bj[:, j + 1],
                                             bj[:, j, :, SUB - 1:SUB].to_broadcast([P, NCH, SUB]), ALU.subtract))
                b32 = cut(t["b"], CH, 0, SEQ)
                for j in range(3):
                    n = SUB * (j + 1)
                    st.did(dve.tensor_tensor(kb[j].rearrange("p (c t) -> p c t", t=CH)[:, :, 0:n],
                                             b32[:, :, n - 1:n].to_broadcast([P, NCH, n]), b32[:, :, 0:n], ALU.subtract))
                st.did(dve.tensor_tensor(cut(t["dec"], CH, 0, SEQ), b32[:, :, CH - 1:CH].to_broadcast([P, NCH, CH]),
                                         b32, ALU.subtract))
                bs = cut(t["b"], NQ, SEQ, TOK)
                dve.tensor_tensor(cut(t["dec"], NQ, SEQ, TOK), bs[:, :, NQ - 1:NQ].to_broadcast([P, NB, NQ]),
                                  bs, ALU.subtract).then_inc(hgd, 1)
                if h == 2:
                    gated(0)
                q, k = qh[:, h, :], fk[:, h, :]
                dve.wait_ge(hga, 11 * h + 12)
                st.did(dve.tensor_tensor(t["qd"], q, t["tb"], ALU.mult))
                st.did(dve.tensor_tensor(t["kd"], k, t["bc"], ALU.mult))
                q3 = q[:, 0:SEQ].rearrange("p (c j u) -> p j c u", j=CH // SUB, u=SUB)
                k32 = cut(k, CH, 0, SEQ)
                for j in range(3):
                    st.did(dve.tensor_tensor(qo[:, j], qo[:, j], q3[:, j + 1], ALU.mult))
                    kv = kb[j].rearrange("p (c t) -> p c t", t=CH)[:, :, 0:SUB * (j + 1)]
                    st.did(dve.tensor_tensor(kv, kv, k32[:, :, 0:SUB * (j + 1)], ALU.mult))
                st.settle(dve)
                st.did(dve.tensor_tensor(k, t["dec"], k, ALU.mult))
                dve.tensor_tensor(q, q, t["lf"], ALU.mult).then_inc(head_ready, 1)

            def weights_inside(h):
                J.wait_filled(dve, "attd", h)
                J.empties(dve.copy_predicated(att[:, h, :], maskd[:, :].bitcast(U32), J.bank("attd", h)), "attd", h)
                J.wait_filled(dve, "atto", h)
                J.wait_emptied(dve, "attd", h)
                s = J.bank("atto", h)
                a4 = att[:, h, :].rearrange("p (c j u) -> p j c u", j=CH // SUB, u=SUB)
                for j in range(3):
                    st.did(dve.copy_predicated(a4[:, j + 1], masko[:, P * j:P * (j + 1)].bitcast(U32)
                                               .rearrange("p (c u) -> p c u", u=SUB),
                                               s[:, P * j:P * (j + 1)].rearrange("p (c u) -> p c u", u=SUB)))
                J.empties(dve.copy_predicated(atts[0:NS, NS * h:NS * (h + 1)],
                                              masks[:, 0:NS].bitcast(U32), s[0:NS, 3 * P:3 * P + NS]), "atto", h)

            def gated(i):
                r = rows(i)
                dve.wait_ge(exped, 6 + i)
                g = gh[0:r, i, :]
                v(dve.tensor_scalar(g, g, 1.0, None, ALU.add))
                v(dve.reciprocal(g, g))
                if i < NT:
                    ins = dve.tensor_tensor(g, J.bank("hg", i)[0:r, :], g, ALU.mult)
                else:
                    for n in range(4):
                        c = slice(P * n, P * (n + 1))
                        ins = dve.tensor_tensor(g[:, c], J.bank("hg", i)[NS * n:NS * (n + 1), 0:P], g[:, c], ALU.mult)
                J.empties(ins, "hg", i)
                J.wait_emptied(dve, "hg", i)
                g3 = g.rearrange("p (h v) -> p h v", h=HG)
                st.did(dve.tensor_tensor(g3, g3, ghn[0:r, :].unsqueeze(1).to_broadcast([r, HG, HD]), ALU.mult))

            gate_share(0)
            for h in range(HG):
                decayed(h)
                if h < HG - 1:
                    gate_share(h + 1)
                if h == 2:
                    gated(1)
                    gated(2)
                    gated(3)
                weights_inside(h)
                if h == 2:
                    gated(4)

            def new_state(n):
                J.wait_filled(dve, "U", n)
                if n >= 5:
                    J.wait_filled(dve, "o", (n - 5) // 4)
                if n:
                    J.wait_emptied(dve, "U", n - 1)
                for h in range(HG):
                    u = J.bank("U", n)[:, HD * h:HD * (h + 1)]
                    dst = state[:, (n + 1) % 6, h, :]
                    if n == 0:
                        ins = dve.tensor_copy(dst, u)
                    else:
                        ins = dve.scalar_tensor_tensor(out=dst, in0=state[:, n % 6, h, :], scalar=dl[:, h, n:n + 1],
                                                       in1=u, op0=ALU.mult, op1=ALU.add)
                J.empties(ins, "U", n)

            def gate_applied(i):
                r = rows(i)
                J.wait_filled(dve, "o", i)
                g = gh[0:r, i, :]
                dve.tensor_tensor(g, J.bank("o", i)[0:r, :], g, ALU.mult).then_inc(o_gated, 1)

            def heads_normed(i0, i1, r):
                dve.wait_ge(o_root, 1 if i0 == 0 else 2)
                y = refined(hy0[0:r, i0:i1, :], hss[0:r, i0:i1, :], HD, [hnt[0:r, k, i0:i1, :] for k in range(3)], HG)
                for i in range(i0, i1):
                    g = gh[0:r, i, :].rearrange("p (h v) -> p h v", h=HG)
                    dve.tensor_tensor(g, g, y[:, i - i0, :].unsqueeze(2).to_broadcast([r, HG, HD]), ALU.mult)\
                        .then_inc(heads_done, 1)

            def softmax_stats(src, col, sem_max, n=1):
                dve.tensor_reduce(stat[:, 1, col:col + n], src, AX, ALU.max, negate=True).then_inc(sem_max, 1)

            def probs(p, col, sem_exp, count, sem_prob):
                dve.wait_ge(sem_exp, count)
                v(dve.reciprocal(stat[:, 3, col:col + 1], stat[:, 2, col:col + 1]))
                dve.tensor_scalar(p, p, stat[:, 3, col:col + 1], None, ALU.mult).then_inc(sem_prob, 1)

            def share(n):
                dve.wait_ge(s_exp, n + 1)
                dve.reciprocal(stat[:, 3, n % 8:n % 8 + 1], stat[:, 2, n % 8:n % 8 + 1]).then_inc(s_share, 1)

            def moba_step(h):
                for i in range(NT):
                    n = NT * h + i
                    m = P * (i + 1)
                    J.wait_filled(dve, "S", h, i)
                    if h >= 2:
                        J.wait_filled(dve, "PT", h - 2, NT - 1)
                    p = pb[h % 2][i][:, 0:m]
                    J.empties(dve.scalar_tensor_tensor(out=p, in0=alibi[:, SEQ - P - P * i:SEQ - P - P * i + m],
                                                       scalar=2.0 ** -(h + 1), in1=J.bank("S", h, i)[:, 0:m],
                                                       op0=ALU.mult, op1=ALU.add), "S", h, i)
                    J.wait_emptied(dve, "S", h, i)
                    softmax_stats(p, n % 8, s_max)
                    if i:
                        share(n - 1)
                share(n)

            for i in range(NT):
                for c in range(P // CH):
                    new_state(i * (P // CH) + c)
                moba_step(2 * i)
                gate_applied(i)
                moba_step(2 * i + 1)
            J.wait_filled(dve, "o", NT - 1)
            dve.wait_ge(out_s, 16)
            v(dve.memset(qx, 0.0))
            for h in range(HG):
                q = qh[:, h, SEQ:TOK]
                dve.tensor_copy(qx[:, h, 0:252].rearrange("p (b m) -> p b m", m=36)[:, :, 0:NQ],
                                q[:, 0:NS - NQ].rearrange("p (b t) -> p b t", t=NQ))
                ins = dve.tensor_copy(qx[:, h, 252:256], q[:, NS - NQ:NS])
            ins.then_inc(qkx_done, 1)
            J.wait_emptied(dve, "kds", HG - 1)
            for b in range(NB):
                ins = dve.tensor_scalar(kdx[0:NS, b, :], kds[0:NS, :], bsel[:, b:b + 1], None, ALU.mult)
            ins.then_inc(qkx_done, 1)
            heads_normed(0, NT, P)
            gate_applied(NT)
            heads_normed(NT, NT + 1, NS)
            for b in range(NB):
                J.wait_filled(dve, "Us", b)
                for h in range(HG):
                    u = J.bank("Us", b)[:, HD * h:HD * (h + 1)]
                    ins = dve.scalar_tensor_tensor(out=s0[:, b, h, :], in0=s0[:, b, h, :],
                                                   scalar=dl[:, h, NCH + b:NCH + b + 1], in1=u,
                                                   op0=ALU.mult, op1=ALU.add)
                J.empties(ins, "Us", b)

            dve.wait_ge(gain_in, 16)
            for i in range(MT):
                norm_scale(5 + i, memx[:, i, :], hn[(5 + i) % 2])
            for i in range(MT):
                evac(memT[:, 4:8, P * i:P * (i + 1)], "memT", i, 1, view=lambda s: s.rearrange("p (k t) -> p k t", k=4))
            v(dve.memset(part(r_c, 4 * TOK, 4 * NB * 32), 0.0))
            for h in range(MB):
                par, c = h % 2, h // 2
                rr = slice(64 * par, 64 * par + 64)
                ins = dve.tensor_copy(qxm[rr, c, :, NQ * h:NQ * (h + 1)],
                                      mqT[rr, c, SEQ:TOK].rearrange("p (b t) -> p b t", t=NQ))
            ins.then_inc(qx_done, 1)
            dve.wait_ge(out_mv, 32)
            for n in range(4):
                evac((memk, memv)[n // 2][:, 1, 512 * (n % 2):512 * (n % 2 + 1)], "mem", n, 1)
                if n == 1:
                    for c in (1, 3):
                        evac(memkT[:, 2 * c:2 * c + 2, :], "memKT", c, view=lambda s: s.rearrange("p (k t) -> p k t", k=2))

            def keys_turned(b):
                if b < 2:
                    dve.wait_ge(out_s0, 16)
                else:
                    dve.wait_ge(sc_full, b // 2)
                for c in (1, 3):
                    evac(kT[b % 2][:, c, :], "KT", b, c)

            def sample_probs(g):
                dve.wait_ge(sc_full, 2 * g + 2)
                if g:
                    J.wait_filled(dve, "Ptn", g - 1)
                dve.tensor_tensor(sx[:, 0:PAST], sbias[:, 0:PAST], psum[6], ALU.add).then_inc(sc_free, 1)
                J.wait_filled(dve, "Sn", g)
                J.empties(dve.tensor_tensor(sx[:, PAST:], sbias[:, PAST + NS * g:PAST + NS * (g + 1)],
                                            J.bank("Sn", g)[:, 0:NS], ALU.add), "Sn", g)
                J.wait_emptied(dve, "Sn", g)
                dve.wait_ge(sc_free, g + 1)
                softmax_stats(sx, 0, ss_max)
                probs(sx, 0, ss_exp, g + 1, ss_prob)

            def new_probs_turned(g):
                if g:
                    J.wait_filled(dve, "Os", g - 1)
                evac(ptn[0:NS, :], "Ptn", g, view=lambda s: s[0:NS, 0:P])

            def out_turned(g):
                J.wait_filled(dve, "OsT", g)
                s = J.bank("OsT", g).rearrange("p (c b m) -> p c b m", c=4, b=4)
                for h in range(MB):
                    rr = slice(64 * (h % 2), 64 * (h % 2) + 64)
                    ins = dve.tensor_copy(mixT[rr, 4 + h // 2, SEQ + 16 * g:SEQ + 16 * (g + 1)]
                                          .rearrange("p (b t) -> p b t", b=4), s[rr, h // 2, :, NQ * h:NQ * (h + 1)])
                J.empties(ins, "OsT", g)

            for b in range(4):
                keys_turned(b)
            sample_probs(0)
            keys_turned(4)
            keys_turned(5)
            new_probs_turned(0)
            keys_turned(6)
            out_turned(0)
            keys_turned(7)
            sample_probs(1)
            new_probs_turned(1)

            def add_rows(tag, half, i):
                J.wait_filled(dve, tag, half, i)
                x = xr[0:rows(i), i, 512 * half:512 * (half + 1)]
                if i < NT:
                    ins = dve.tensor_tensor(x, x, J.bank(tag, half, i), ALU.add)
                else:
                    for n in range(4):
                        c = slice(P * n, P * (n + 1))
                        ins = dve.tensor_tensor(x[:, c], x[:, c], J.bank(tag, half, i)[NS * n:NS * (n + 1), 0:P], ALU.add)
                J.empties(ins, tag, half, i)

            def summed(what, turn, n0, meanwhile, logit=None):
                def norm(n):
                    i = LAST_HALF[n]
                    norm_scale(n0 + n, xr[0:rows(i), i, :], hn[(n0 + n) % 2][0:rows(i), :])

                for i, _ in TILES:
                    add_rows(what, 0, i)
                    if i == 0:
                        meanwhile()
                for n, i in enumerate(LAST_HALF):
                    add_rows(what, 1, i)
                    if n:
                        norm(n - 1)
                    if n >= 2:
                        turned(turn, LAST_HALF[n - 2])
                norm(NT)
                if logit:
                    logit(0)
                    logit(1)
                for n in (NT - 1, NT):
                    turned(turn, LAST_HALF[n])
                    if logit:
                        logit(n - 1)
                if logit:
                    logit(NT)

            dve.wait_ge(xr_in, 32)
            dve.wait_ge(gain_in, 32)
            summed("x1", "h2T", 7, lambda: out_turned(1))
            for half in range(2):
                for c in (1, 3):
                    J.wait_filled(dve, "xq", half, c)
                    J.empties(dve.tensor_scalar(qT[:, 4 * half + c, 0:SEQ], J.bank("xq", half, c), XD ** -0.5, None,
                                                ALU.mult), "xq", half, c)
            for h in range(XH + 1):
                if h < XH:
                    for i2 in range(2):
                        J.wait_filled(dve, "XS", h, i2)
                        if h >= 2:
                            J.wait_filled(dve, "XPT", h - 2, MT - 1)
                        softmax_stats(J.bank("XS", h, i2).rearrange("p (u m) -> p u m", u=2), 2 * i2 + 4 * (h % 2), xs_max, 2)
                if h:
                    for k in range(MT):
                        if h >= 3:
                            J.wait_filled(dve, "XOT", h - 3, 1)
                        if h == 1:
                            dve.wait_ge(out_mem, 32)
                        evac(xpt[(h - 1) % 2][:, k, :], "XPT", h - 1, k)
                if h < XH:
                    for i2 in range(2):
                        J.wait_emptied(dve, "XS", h, i2)
                        for u in range(2):
                            n = 2 * i2 + u + 4 * (h % 2)
                            v(dve.reciprocal(stat[:, 3, n:n + 1], stat[:, 2, n:n + 1]))
                            x = xp[h % 2][:, 2 * i2 + u, :]
                            dve.tensor_scalar(x, x, stat[:, 3, n:n + 1], None, ALU.mult).then_inc(xs_prob, 1)
            J.wait_filled(dve, "XPT", XH - 1, MT - 1)
            v(dve.memset(part(flat, TAIL + 6144, KC * NB * 32), 0.0))
            for h in range(XH):
                for c in (2 * h, 2 * h + 1):
                    ins = dve.tensor_copy(qxx[:, c, :, NQ * h:NQ * (h + 1)],
                                          qT[:, c, SEQ:TOK].rearrange("p (b t) -> p b t", t=NQ))
            ins.then_inc(qx_done, 1)

            def mem_keys_turned(b):
                if b >= 2:
                    dve.wait_ge(sc_full, NB // 2 + b // 2)
                for c in (1, 3):
                    evac(xkT[b % 2][:, 2 * c:2 * c + 2, :], "XKT", b, c, view=lambda s: s.rearrange("p (k t) -> p k t", k=2))

            def mem_probs(g):
                dve.wait_ge(sc_full, NB // 2 + 2 * g + 2)
                if g:
                    J.wait_filled(dve, "XPt", g - 1)
                softmax_stats(psum[6][:, 0:MEM], 0, xs_max)
                probs(xsx, 0, xs_exp, g + 1, xs_prob)

            def mem_out(g):
                if g:
                    J.wait_filled(dve, "XOsT", g - 1, 1)
                evac(xosb[:, 1, :], "XOs", g, 1)

            def mem_out_turned(g):
                for half in range(2):
                    J.wait_filled(dve, "XOsT", g, half)
                    s = J.bank("XOsT", g, half).rearrange("p (c b m) -> p c b m", c=4, b=4)
                    for h in (2 * half, 2 * half + 1):
                        for u in range(2):
                            ins = dve.tensor_copy(oT[:, 2 * h + u, SEQ + 16 * g:SEQ + 16 * (g + 1)]
                                                  .rearrange("p (b t) -> p b t", b=4),
                                                  s[:, 2 * (h % 2) + u, :, NQ * h:NQ * (h + 1)])
                    J.empties(ins, "XOsT", g, half)

            for b in range(4):
                mem_keys_turned(b)
            mem_probs(0)
            mem_keys_turned(4)
            mem_out(0)
            mem_keys_turned(5)
            mem_out_turned(0)
            mem_keys_turned(6)
            mem_keys_turned(7)
            mem_probs(1)
            mem_out(1)

            lg = rt["lg"].rearrange("p (i n) -> p i n", n=36)

            def logit(n):
                i = LAST_HALF[n]
                if n == 0:
                    dve.wait_ge(rtw_in, 64)
                    v(dve.memset(lg, 0.0))
                r = rows(i)
                J.wait_filled(dve, "logit", i)
                J.empties(dve.tensor_tensor(lg[0:r, i, :], rt["bias"][0:r, :], J.bank("logit", i)[0:r, 0:36], ALU.add),
                          "logit", i)

            dve.wait_ge(gain_in, 48)
            summed("x2", "h3T", 12, lambda: mem_out_turned(1), logit)

            R = rt
            iota3 = lambda n: iota[:, 0:n].unsqueeze(1).to_broadcast([P, 5, n])
            v(dve.memset(R["g8"], -3e38))
            J.wait_emptied(dve, "logit", NT)
            g8 = R["g8"].rearrange("p (i n) -> p i n", n=8)
            m8 = R["m8"].rearrange("p (i n) -> p i n", n=8)
            v(dve.tensor_copy(g8[:, :, 0:NG], lg[:, :, 0:NG]))
            for i in range(5):
                ins = dve.max(m8[:, i, :], g8[:, i, :])
            v(ins)
            for i in range(5):
                ins = dve.max_index(i8[:, i, :], m8[:, i, :], g8[:, i, :])
            v(ins)
            gi = R["i8f"]
            v(dve.tensor_copy(gi, i8[:, :, 0]))
            ge = R["ge"].rearrange("p (i n) -> p i n", n=NG)
            dve.tensor_tensor(ge, lg[:, :, 0:NG], m8[:, :, 0:1].to_broadcast([P, 5, NG]), ALU.subtract)\
                .then_inc(r_exp_in, 1)
            ohg = R["ohg"].rearrange("p (i n) -> p i n", n=NG)
            v(dve.tensor_tensor(ohg, iota3(NG), gi.unsqueeze(2).to_broadcast([P, 5, NG]), ALU.is_equal))
            pr = R["pr"].rearrange("p (i g e) -> p i g e", i=5, g=NG)
            for i in range(5):
                ins = dve.tensor_tensor(pr[:, i], lg[:, i, NG:36].rearrange("p (g e) -> p g e", g=NG),
                                        ohg[:, i, :].unsqueeze(2).to_broadcast([P, NG, EPG]), ALU.mult)
            v(ins)
            se = R["se"].rearrange("p (i n) -> p i n", n=8)
            for i in range(5):
                ins = dve.tensor_reduce(se[:, i, :], pr[:, i].rearrange("p g e -> p e g"), AX, ALU.add)
            v(ins)
            me = R["me"].rearrange("p (i n) -> p i n", n=8)
            for i in range(5):
                ins = dve.max(me[:, i, :], se[:, i, :])
            v(ins)
            for i in range(5):
                ins = dve.max_index(i8[:, i, :], me[:, i, :], se[:, i, :])
            v(ins)
            ek = R["ek"].rearrange("p (k i) -> p k i", k=2)
            for k in range(2):
                ins = dve.tensor_copy(ek[:, k, :], i8[:, :, k])
            dve.tensor_tensor(R["ex"], me[:, :, 1], me[:, :, 0], ALU.subtract).then_inc(r_exp_in, 1)
            dve.wait_ge(r_exp_in, 2)
            eid = R["eid"].rearrange("p (k i) -> p k i", k=2)
            for k in range(2):
                ins = dve.scalar_tensor_tensor(out=eid[:, k, :], in0=gi, scalar=float(EPG), in1=ek[:, k, :],
                                               op0=ALU.mult, op1=ALU.add)
            v(ins)
            m = R["m"].rearrange("p (k i n) -> p k i n", k=2, i=5)
            ms = R["ms"].rearrange("p (i n) -> p i n", i=5)
            for k in range(2):
                ins = dve.tensor_tensor(m[:, k], iota3(NE), eid[:, k, :].unsqueeze(2).to_broadcast([P, 5, NE]), ALU.is_equal)
            v(ins)
            dve.tensor_tensor(ms, m[:, 0], m[:, 1], ALU.add).then_inc(onehots, 1)
            dve.wait_ge(r_exp, 2)
            v(dve.tensor_reduce(R["gw"], ge, AX, ALU.add))
            v(dve.reciprocal(R["gw"], R["gw"]))
            v(dve.tensor_scalar(R["t1"][:, 0:5], R["ex"], 1.0, None, ALU.add))
            v(dve.reciprocal(R["t1"][:, 0:5], R["t1"][:, 0:5]))
            v(dve.tensor_tensor(gates[:, 0, :], R["gw"], R["t1"][:, 0:5], ALU.mult))
            v(dve.tensor_tensor(gates[:, 1, :], gates[:, 0, :], R["ex"], ALU.mult))
            J.wait_filled(dve, "rank")
            s = J.bank("rank")
            v(dve.tensor_copy(R["cnt"], s[:, 160:192]))
            tmp = R["tmp"].rearrange("p (k i n) -> p k i n", k=2, i=5)
            rk = R["rk"].rearrange("p (k i) -> p k i", k=2)
            J.empties(dve.tensor_tensor(tmp, m, s[:, 0:160].rearrange("p (i n) -> p i n", i=5).unsqueeze(1)
                                        .to_broadcast([P, 2, 5, NE]), ALU.mult), "rank")
            J.wait_emptied(dve, "rank")
            v(dve.tensor_reduce(rk, tmp, AX, ALU.add))
            big = R["big"].rearrange("p (e m) -> p e m", e=NE)
            v(dve.tensor_tensor(big, R["cnt"].unsqueeze(2).to_broadcast([P, NE, 8]),
                                steps[:, :].unsqueeze(1).to_broadcast([P, NE, 8]), ALU.is_gt))
            v(dve.tensor_reduce(R["ovn"], big, AX, ALU.add))
            v(dve.tensor_tensor_scan(R["ove"], ones[:, 0:NE], R["ovn"], 0.0, ALU.mult, ALU.add))
            v(dve.tensor_tensor(R["ovs"], R["ove"], R["ovn"], ALU.subtract))
            qk = R["qk"].rearrange("p (k i) -> p k i", k=2)
            b5 = R["big"][:, 0:80].rearrange("p (i m) -> p i m", m=8)
            v(dve.tensor_tensor(b5, R["rk"].unsqueeze(2).to_broadcast([P, 10, 8]),
                                steps[:, :].unsqueeze(1).to_broadcast([P, 10, 8]), ALU.is_ge))
            v(dve.tensor_reduce(R["qk"], b5, AX, ALU.add))
            v(dve.scalar_tensor_tensor(out=R["rr"], in0=R["qk"], scalar=-float(CAP), in1=R["rk"], op0=ALU.mult, op1=ALU.add))
            tmp = R["tmp"].rearrange("p (a n) -> p a n", a=10)
            v(dve.tensor_tensor(tmp, R["m"].rearrange("p (a n) -> p a n", a=10),
                                R["ovs"].unsqueeze(1).to_broadcast([P, 10, NE]), ALU.mult))
            v(dve.tensor_reduce(R["ovk"], tmp, AX, ALU.add))
            v(dve.tensor_tensor(R["t1"], R["ovk"], R["qk"], ALU.add))
            v(dve.scalar_tensor_tensor(out=R["t1"], in0=R["t1"], scalar=float(NE - 1), in1=R["eid"], op0=ALU.add, op1=ALU.subtract))
            v(dve.tensor_scalar(R["t2"], R["qk"], 0.0, None, ALU.is_gt))
            v(dve.tensor_tensor(R["t1"], R["t1"], R["t2"], ALU.mult))
            v(dve.tensor_tensor(R["sk"], R["eid"], R["t1"], ALU.add))
            v(dve.scalar_tensor_tensor(out=yidx[:, :, :].rearrange("p k i -> p (k i)"), in0=R["sk"], scalar=float(CAP),
                                       in1=R["rr"], op0=ALU.mult, op1=ALU.add))
            ohs = R["ohs"].rearrange("p (a n) -> p a n", n=NBLK)
            ohr = R["ohr"].rearrange("p (a n) -> p a n", n=CAP)
            v(dve.tensor_tensor(ohs, iota[:, 0:NBLK].unsqueeze(1).to_broadcast([P, 10, NBLK]),
                                R["sk"].unsqueeze(2).to_broadcast([P, 10, NBLK]), ALU.is_equal))
            for k in range(2):
                o5 = ohs[:, 5 * k:5 * k + 5, :]
                ins = dve.tensor_tensor(o5, o5, tokid[:, :].unsqueeze(2).to_broadcast([P, 5, NBLK]), ALU.mult)
            v(ins)
            dve.tensor_tensor(ohr, iota[:, 0:CAP].unsqueeze(1).to_broadcast([P, 10, CAP]),
                              R["rr"].unsqueeze(2).to_broadcast([P, 10, CAP]), ALU.is_equal).then_inc(onehots, 1)
            cmp = R["cmp"].rearrange("p (s e) -> p s e", s=XBLK)
            v(dve.tensor_tensor(cmp[0:1], R["ove"][0:1, :].unsqueeze(1).to_broadcast([1, XBLK, NE]),
                                iota[0:1, 0:XBLK].unsqueeze(2).to_broadcast([1, XBLK, NE]), ALU.is_le))
            v(dve.tensor_reduce(R["exs"][0:1], cmp[0:1], AX, ALU.add))
            dve.tensor_scalar(ovi[0:1, 1:1 + XBLK], R["exs"][0:1], float(NE - 1), None, ALU.min)
            v(dve.tensor_copy(ovi[0:1, 0:1], R["ove"][0:1, NE - 1:NE]))
            J.wait_filled(dve, "table")
            dve.tensor_copy(table[:, :], J.bank("table")[:, 0:NBLK // 2]).then_inc(routed, 1)

            def rows_turned(j):
                dve.wait_ge(xt_full, j + 1)
                dve.tensor_copy(xT[:, 0:4, :], psum[0].rearrange("p (k t) -> p k t", k=4)).then_inc(xt_free, 1)

            def gated_product(j, c):
                u = c % 2
                dve.wait_ge(up_exp, 2 * j + (c + 1))
                step = 6 * j + 3 * c
                dve.tensor_scalar(he[u], he[u], 1.0, None, ALU.add).then_inc(dve_moe, 1)
                dve.wait_ge(dve_moe, step + 1)
                dve.reciprocal(he[u], he[u]).then_inc(dve_moe, 1)
                dve.wait_ge(dve_moe, step + 2)
                dve.tensor_tensor(he[u], he[u], psum[2 + 2 * u], ALU.mult).then_inc(dve_moe, 1)
                dve.wait_ge(dve_moe, step + 3)
                if reused(j, c):
                    dve.wait_ge(ht_full, 2 * j + (c - 1))
                dve.tensor_tensor(h2[u], he[u], psum[3 + 2 * u], ALU.mult).then_inc(up_free, 1)

            def pair(j):
                gated_product(j, 0)
                gated_product(j, 1)
                rows_turned(j + 1)

            rows_turned(0)
            pair(0)
            with dve.Fori(1, NE // 2 - 1) as j:
                pair(j)
            gated_product(NE // 2 - 1, 0)
            gated_product(NE // 2 - 1, 1)
            n_ov = dve.value_load(ovi[0:1, 0:1], min_val=0, max_val=XBLK)
            with dve.If(n_ov > 0):
                with dve.Fori(NE // 2, NBLK // 2) as j:
                    with dve.If(2 * j - NE < n_ov):
                        rows_turned(j)
                        gated_product(j, 0)
                        gated_product(j, 1)
            dve.wait_ge(gain_in, 64)

            def expert_rows_added(i):
                r = rows(i)
                dve.wait_ge(yg_in[i], 32)
                x = xr[0:r, i, :]
                v(dve.scalar_tensor_tensor(out=x, in0=yg[i][0][0:r, :], scalar=gates[0:r, 0, i:i + 1], in1=x,
                                           op0=ALU.mult, op1=ALU.add))
                dve.scalar_tensor_tensor(out=x, in0=yg[i][1][0:r, :], scalar=gates[0:r, 1, i:i + 1], in1=x,
                                         op0=ALU.mult, op1=ALU.add).then_inc(xr_new, 1)

            expert_rows_added(0)
            for i, r in TILES:
                if i < NT:
                    expert_rows_added(i + 1)
                norm_scale(17 + i, xr[0:r, i, :], yg[i][0][0:r, :])

        @block.tensor
        def _(pe):
            def turn(what, i, n, ready):
                r = rows(i)
                pe.wait_ge(normed, ready)
                for half in range(2):
                    J.wait_free(pe, what, i, half)
                    s = J.bank(what, i, half)
                    for k in range(4):
                        ins = pe.transpose(s[:, P * k:P * k + r], hn[n % 2][0:r, P * (4 * half + k):P * (4 * half + k + 1)],
                                           ident[0:r, 0:r])
                    J.fills(ins, what, i, half)

            def weights(tag):
                n = WPOS[tag]
                pe.wait_ge(w_in[n % 2], 16 * (n // 2 + 1))
                return wslot[n % 2]

            def quarters(s, i, w, lhs):
                for k in range(KC):
                    for n in range(4):
                        ins = pe.matmul(s[NS * n:NS * (n + 1), 0:P], lhs[:, k, tok(i)], w[:, k, P * n:P * (n + 1)],
                                        start=(k == 0), stop=(k == KC - 1), skip_group_check=True)
                return ins

            def features_out(what, *key, chunks=range(5)):
                w = weights(what if not key else f"xq{key[0]}")
                for c in chunks:
                    if c == 0:
                        J.wait_free(pe, what, *key, "rows")
                        J.fills(quarters(J.bank(what, *key, "rows"), NT, w, hT), what, *key, "rows")
                    J.wait_free(pe, what, *key, c)
                    s = J.bank(what, *key, c)
                    if c < 4:
                        for k in range(KC):
                            ins = pe.matmul(s, w[:, k, P * c:P * (c + 1)], hT[:, k, 0:SEQ], start=(k == 0), stop=(k == KC - 1))
                    else:
                        J.wait_emptied(pe, what, *key, "rows")
                        ins = pe.transpose(s[:, 0:P], srows[:, :], ident[:, :])
                    J.fills(ins, what, *key, c)

            def rows_of(name, i, w, lhs):
                J.wait_free(pe, *name)
                if i == NT:
                    J.fills(quarters(J.bank(*name), i, w, lhs), *name)
                    return
                for k in range(KC):
                    ins = pe.matmul(J.bank(*name), lhs[:, k, tok(i)], w[:, k, :], start=(k == 0), stop=(k == KC - 1))
                J.fills(ins, *name)

            def weights_inside(h):
                pe.wait_ge(head_ready, h + 1)
                J.wait_free(pe, "attd", h)
                s = J.bank("attd", h)
                for i in range(NT):
                    ins = pe.matmul(s[:, tok(i)], hgt["kd"][:, tok(i)], hgt["qd"][:, tok(i)], start=True, stop=True)
                J.fills(ins, "attd", h)
                J.wait_free(pe, "atto", h)
                s = J.bank("atto", h)
                for j in range(3):
                    for i in range(NT):
                        c = slice(P * j + NS * i, P * j + NS * (i + 1))
                        pe.matmul(s[:, c], kb[j][:, tok(i)], hgt["qo"][:, c], start=True, stop=True)
                ins = pe.matmul(s[0:NS, 3 * P:3 * P + NS], hgt["kd"][:, SEQ:TOK], hgt["qd"][:, SEQ:TOK], start=True, stop=True)
                J.fills(ins, "atto", h)

            pe.wait_ge(ident_in, 16)
            w = wslot[WPOS["mk"] % 2]

            def key_rows(i):
                J.wait_emptied(pe, "hT", i, 0)
                J.wait_emptied(pe, "hT", i, 1)
                if i == 0:
                    weights("mk")
                rows_of(("mk", i), i, w, hT)

            for i, r in TILES:
                turn("hT", i, i, i + 1)
                if i:
                    key_rows(i - 1)
            key_rows(NT)
            features_out("hf")
            features_out("hq")
            features_out("mq")
            J.wait_emptied(pe, "mk", NT)
            for c in range(5):
                J.wait_free(pe, "mkT", c)
                s = J.bank("mkT", c)
                for n in range(4):
                    if c < 4:
                        ins = pe.transpose(s[:, P * n:P * (n + 1)], mkn[:, n, P * c:P * (c + 1)], ident[:, :])
                    else:
                        ins = pe.transpose(s[:, NS * n:NS * (n + 1)], mkn[0:NS, NT, P * n:P * (n + 1)], ident[0:NS, 0:NS])
                J.fills(ins, "mkT", c)
            weights_inside(0)
            w = weights("mv")
            for i, r in TILES:
                rows_of(("mv", i), i, w, hT)
            weights_inside(1)
            w = weights("hg")
            for i, r in TILES:
                if i == 4:
                    weights_inside(2)
                rows_of(("hg", i), i, w, hT)
            w = weights("hi")
            for i, r in TILES:
                rows_of(("hi", i), i, w, hT)
            weights_inside(3)
            for h in range(HG):
                J.wait_free(pe, "kdn", h)
                for i in range(NT):
                    ins = pe.transpose(J.bank("kdn", h)[:, tok(i)], fk[:, h, tok(i)], ident[:, :])
                J.fills(ins, "kdn", h)
            for h in range(HG):
                J.wait_free(pe, "kds", h)
                ins = pe.transpose(J.bank("kds", h)[0:NS, 0:P], fk[:, h, SEQ:TOK], ident[:, :])
                J.fills(ins, "kds", h)

            def turn_heads(i):
                r = rows(i)
                pe.wait_ge(heads_done, i + 1)
                J.wait_free(pe, "hgT", i)
                for h in range(HG):
                    ins = pe.transpose(J.bank("hgT", i)[:, P * h:P * h + r], gh[0:r, i, HD * h:HD * (h + 1)], ident[0:r, 0:r])
                J.fills(ins, "hgT", i)

            def moba_step(h):
                if h < MB:
                    rr = slice(64 * (h % 2), 64 * (h % 2) + 64)
                    for i in range(NT):
                        J.wait_free(pe, "S", h, i)
                        ins = pe.matmul(J.bank("S", h, i)[:, 0:P * (i + 1)], mqT[rr, h // 2, tok(i)],
                                        mkT[rr, h // 2, 0:P * (i + 1)], start=True, stop=True)
                        J.fills(ins, "S", h, i)
                if h:
                    g = h - 1
                    for k in range(NT):
                        J.wait_free(pe, "PT", g, k)
                        for i in range(k, NT):
                            pe.wait_ge(s_prob, NT * g + i + 1)
                            ins = pe.transpose(J.bank("PT", g, k)[:, P * (i - k):P * (i - k + 1)],
                                               pb[g % 2][i][:, P * k:P * (k + 1)], ident[:, :])
                        J.fills(ins, "PT", g, k)
                    if h % 2 == 0:
                        c = h // 2 - 1
                        J.wait_free(pe, "OT", c)
                        J.wait_emptied(pe, "PT", g, NT - 1)
                        for k in range(NT):
                            for par in range(2):
                                hh = 2 * c + par
                                ins = pe.matmul(J.bank("OT", c)[64 * par:64 * par + 64, P * k:SEQ],
                                                mv[:, k, MD * hh:MD * (hh + 1)], pt[par][:, k, P * k:SEQ],
                                                start=(k == 0), stop=(k == NT - 1), skip_group_check=True)
                        J.fills(ins, "OT", c)

            J.wait_emptied(pe, "kdn", HG - 1)
            J.wait_emptied(pe, "kds", HG - 1)
            J.wait_emptied(pe, "atto", HG - 1)
            for i in range(NT):
                for c in range(P // CH):
                    n = i * (P // CH) + c
                    J.wait_free(pe, "U", n)
                    q = slice(CH * c, CH * (c + 1))
                    for h in range(HG):
                        ins = pe.matmul(J.bank("U", n)[:, HD * h:HD * (h + 1)], kdn[q, i, h, :], vh[q, i, HD * h:HD * (h + 1)],
                                        start=True, stop=True, tile_position=(CH * c, 0))
                    J.fills(ins, "U", n)
                moba_step(2 * i)
                J.wait_free(pe, "o", i)
                J.wait_emptied(pe, "U", 4 * i + 2)
                for h in range(HG):
                    c0 = slice(HD * h, HD * (h + 1))
                    s = J.bank("o", i)
                    ins = pe.matmul(s[:, c0], att[:, h, tok(i)], vh[:, i, c0], start=True, stop=True)
                    for c in range(P // CH):
                        n = i * (P // CH) + c
                        if n:
                            ins = pe.matmul(s[CH * c:CH * (c + 1), c0], qh[:, h, CH * n:CH * (n + 1)], state[:, n % 6, h, :],
                                            start=False, stop=True, skip_group_check=True)
                J.fills(ins, "o", i)
                moba_step(2 * i + 1)
            moba_step(MB)
            J.wait_free(pe, "o", NT)
            pe.wait_ge(s0_in, 16)
            pe.wait_ge(qkx_done, 1)
            s = J.bank("o", NT)
            for h in range(HG):
                c0 = slice(HD * h, HD * (h + 1))
                pe.matmul(s[0:NS, c0], atts[0:NS, NS * h:NS * (h + 1)], vh[0:NS, NT, c0], start=True, stop=False)
                for b in range(NB):
                    ins = pe.matmul(s[0:NS, c0], qx[:, h, NS * b:NS * (b + 1)], s0[:, b, h, :], start=False, stop=(b == NB - 1))
            J.fills(ins, "o", NT)
            pe.wait_ge(qkx_done, 2)
            for b in range(NB):
                J.wait_free(pe, "Us", b)
                for h in range(HG):
                    c0 = slice(HD * h, HD * (h + 1))
                    ins = pe.matmul(J.bank("Us", b)[:, c0], kdx[0:NS, b, c0], vh[0:NS, NT, c0], start=True, stop=True)
                J.fills(ins, "Us", b)
            for i, _ in TILES:
                turn_heads(i)

            for i in range(MT):
                turn("memT", i, 5 + i, 6 + i)
            J.wait_emptied(pe, "memT", 1, 0)
            J.wait_emptied(pe, "memT", 1, 1)
            for n in range(4):
                w = weights(("xk0", "xk1", "xv0", "xv1")[n])
                for i in range(MT):
                    J.wait_free(pe, "mem", n, i)
                    for k in range(KC):
                        ins = pe.matmul(J.bank("mem", n, i), memT[:, k, P * i:P * (i + 1)], w[:, k, :], start=(k == 0), stop=(k == KC - 1))
                    J.fills(ins, "mem", n, i)
                if n == 1:
                    for c in range(4):
                        J.wait_free(pe, "memKT", c)
                        J.wait_emptied(pe, "mem", 1, 0)
                        J.wait_emptied(pe, "mem", 1, 1)
                        for m in range(4):
                            k, i = 2 * c + m // 2, m % 2
                            ins = pe.transpose(J.bank("memKT", c)[:, P * m:P * (m + 1)], memk[:, i, P * k:P * (k + 1)], ident[:, :])
                        J.fills(ins, "memKT", c)

            def keys_turned(b):
                pe.wait_ge(k_in[b % 3], 16 * NPG * (b // 3 + 1))
                for c in range(4):
                    J.wait_free(pe, "KT", b, c)
                    for j in range(NPG):
                        ins = pe.transpose(J.bank("KT", b, c)[:, P * j:P * (j + 1)], kbuf[b % 3][:, j, P * c:P * (c + 1)],
                                           ident[:, :])
                    J.fills(ins, "KT", b, c)

            def scores(b0):
                if b0 == 4:
                    pe.wait_ge(sc_free, 1)
                J.wait_emptied(pe, "KT", b0 + 1, 2)
                J.wait_emptied(pe, "KT", b0 + 1, 3)
                for c in range(4):
                    for b in (b0, b0 + 1):
                        ins = pe.matmul(psum[6][32 * (b % 4):32 * (b % 4) + 32, :], qxm[:, c, b, :], kT[b % 2][:, c, :],
                                        start=(c == 0), stop=(c == 3), skip_group_check=True)
                ins.then_inc(sc_full, 1)

            def new_scores(g):
                J.wait_free(pe, "Sn", g)
                for c in range(4):
                    for b in range(4 * g, 4 * g + 4):
                        q = slice(32 * (b % 4), 32 * (b % 4) + 32)
                        ins = pe.matmul(J.bank("Sn", g)[q, 0:NS], qxm[:, c, b, :], mkT[:, c, SEQ:TOK], start=(c == 0),
                                        stop=(c == 3), skip_group_check=True)
                J.fills(ins, "Sn", g)

            def probs_turned(g):
                pe.wait_ge(ss_prob, g + 1)
                J.wait_free(pe, "Pt", g)
                for j in range(NPG):
                    ins = pe.transpose(J.bank("Pt", g)[:, P * j:P * (j + 1)], sx[:, P * j:P * (j + 1)], ident[:, :])
                J.fills(ins, "Pt", g)
                J.wait_free(pe, "Ptn", g)
                ins = pe.transpose(J.bank("Ptn", g)[0:NS, 0:P], sx[:, PAST:], ident[:, :])
                J.fills(ins, "Ptn", g)

            def sample_out(g):
                J.wait_free(pe, "Os", g)
                J.wait_emptied(pe, "Pt", g)
                J.wait_emptied(pe, "Ptn", g)
                pe.wait_ge(v_in, 16 * NPG * 4 * (g + 1))
                s = J.bank("Os", g)
                ins = pe.matmul(s, ptn[0:NS, :], mvs[0:NS, :], start=True, stop=True, skip_group_check=True)
                for j in range(NPG):
                    for b in range(4):
                        ins = pe.matmul(s[32 * b:32 * b + 32, :], ptS[:, j, 32 * b:32 * b + 32], vbuf[b][:, j, :],
                                        start=False, stop=True, skip_group_check=True)
                J.fills(ins, "Os", g)

            def out_turned(g):
                J.wait_free(pe, "OsT", g)
                J.wait_emptied(pe, "Os", g)
                for c in range(4):
                    ins = pe.transpose(J.bank("OsT", g)[:, P * c:P * (c + 1)], osb[:, P * c:P * (c + 1)], ident[:, :])
                J.fills(ins, "OsT", g)

            keys_turned(0)
            keys_turned(1)
            keys_turned(2)
            pe.wait_ge(qx_done, 1)
            scores(0)
            keys_turned(3)
            scores(2)
            new_scores(0)
            keys_turned(4)
            keys_turned(5)
            probs_turned(0)
            sample_out(0)
            keys_turned(6)
            out_turned(0)
            scores(4)
            keys_turned(7)
            scores(6)
            new_scores(1)
            probs_turned(1)
            sample_out(1)

            def summed(what, wtag, lhs, turned, n0, meanwhile, samples, logit=None):
                for half in range(2):
                    w = weights(f"{wtag}{half}")
                    for n, i in enumerate(LAST_HALF if half else range(NT + 1)):
                        if i == NT and half == 0:
                            J.wait_emptied(pe, *samples)
                        rows_of((what, half, i), i, w, lhs)
                        if i == 0 and half == 0:
                            meanwhile()
                        if half and n >= 2:
                            turn(turned, LAST_HALF[n - 2], n0 + n - 2, n0 + n - 1)
                if logit:
                    logit(0)
                    logit(1)
                for n in (NT - 1, NT):
                    turn(turned, LAST_HALF[n], n0 + n, n0 + n + 1)
                    if logit:
                        logit(n - 1)
                if logit:
                    logit(NT)

            J.wait_emptied(pe, "OsT", 0)
            summed("x1", "o", mixT, "h2T", 7, lambda: out_turned(1), ("OsT", 1))
            J.wait_emptied(pe, "h2T", LAST_HALF[-1], 0)
            J.wait_emptied(pe, "h2T", LAST_HALF[-1], 1)
            for half in range(2):
                features_out("xq", half)
            for c in range(5):
                J.wait_emptied(pe, "xq", 1, c)
            J.wait_emptied(pe, "memKT", 2)
            J.wait_emptied(pe, "memKT", 3)
            for h in range(XH + 1):
                if h < XH:
                    for i2 in range(2):
                        J.wait_free(pe, "XS", h, i2)
                        for u in range(2):
                            for c in range(2):
                                ins = pe.matmul(J.bank("XS", h, i2)[:, MEM * u:MEM * (u + 1)], qT[:, 2 * h + c, tok(2 * i2 + u)],
                                                memkT[:, 2 * h + c, :], start=(c == 0), stop=(c == 1))
                        J.fills(ins, "XS", h, i2)
                if h:
                    g = h - 1
                    for k in range(MT):
                        J.wait_free(pe, "XPT", g, k)
                        pe.wait_ge(xs_prob, NT * (g + 1))
                        for i in range(NT):
                            ins = pe.transpose(J.bank("XPT", g, k)[:, tok(i)], xp[g % 2][:, i, P * k:P * (k + 1)], ident[:, :])
                        J.fills(ins, "XPT", g, k)
                    J.wait_emptied(pe, "XPT", g, 1)
                    for c in range(2):
                        J.wait_free(pe, "XOT", g, c)
                        for k in range(MT):
                            ins = pe.matmul(J.bank("XOT", g, c), memv[:, k, P * (2 * g + c):P * (2 * g + c + 1)], xpt[g % 2][:, k, :],
                                            start=(k == 0), stop=(k == MT - 1))
                        J.fills(ins, "XOT", g, c)

            def mem_keys_turned(b):
                pe.wait_ge(xk_in[b % 3], 16 * (b // 3 + 1))
                for c in range(4):
                    J.wait_free(pe, "XKT", b, c)
                    for n in range(4):
                        k, i = 2 * c + n // 2, n % 2
                        ins = pe.transpose(J.bank("XKT", b, c)[:, P * n:P * (n + 1)], xkbuf[b % 3][:, i, P * k:P * (k + 1)], ident[:, :])
                    J.fills(ins, "XKT", b, c)

            def mem_scores(b0):
                if b0 == 0:
                    pe.wait_ge(sc_free, 2)
                if b0 == 4:
                    pe.wait_ge(xs_exp, 1)
                J.wait_emptied(pe, "XKT", b0 + 1, 2)
                J.wait_emptied(pe, "XKT", b0 + 1, 3)
                for c in range(KC):
                    for b in (b0, b0 + 1):
                        ins = pe.matmul(psum[6][32 * (b % 4):32 * (b % 4) + 32, 0:MEM], qxx[:, c, b, :], xkT[b % 2][:, c, :],
                                        start=(c == 0), stop=(c == KC - 1), skip_group_check=True)
                ins.then_inc(sc_full, 1)

            def mem_probs_turned(g):
                pe.wait_ge(xs_prob, NT * XH + g + 1)
                J.wait_free(pe, "XPt", g)
                for j in range(MT):
                    ins = pe.transpose(J.bank("XPt", g)[:, P * j:P * (j + 1)], xsx[:, P * j:P * (j + 1)], ident[:, :])
                J.fills(ins, "XPt", g)

            def mem_out(g):
                J.wait_emptied(pe, "XPt", g)
                pe.wait_ge(xv_in, 16 * 4 * (g + 1))
                for half in range(2):
                    J.wait_free(pe, "XOs", g, half)
                    for j in range(MT):
                        for b in range(4):
                            ins = pe.matmul(J.bank("XOs", g, half)[32 * b:32 * b + 32, :], xptS[:, j, 32 * b:32 * b + 32],
                                            xvbuf[b][:, j, 512 * half:512 * (half + 1)], start=(j == 0), stop=(j == MT - 1),
                                            skip_group_check=True)
                    J.fills(ins, "XOs", g, half)

            def mem_out_turned(g):
                for half in range(2):
                    J.wait_free(pe, "XOsT", g, half)
                    J.wait_emptied(pe, "XOs", g, half)
                    for c in range(4):
                        ins = pe.transpose(J.bank("XOsT", g, half)[:, P * c:P * (c + 1)], xosb[:, half, P * c:P * (c + 1)],
                                           ident[:, :])
                    J.fills(ins, "XOsT", g, half)

            mem_keys_turned(0)
            mem_keys_turned(1)
            mem_keys_turned(2)
            pe.wait_ge(qx_done, 2)
            mem_scores(0)
            mem_keys_turned(3)
            mem_scores(2)
            mem_keys_turned(4)
            mem_probs_turned(0)
            mem_out(0)
            mem_keys_turned(5)
            mem_out_turned(0)
            mem_keys_turned(6)
            mem_scores(4)
            mem_keys_turned(7)
            mem_scores(6)
            mem_probs_turned(1)
            mem_out(1)

            wr = rt["wr"].rearrange("p (k n) -> p k n", k=KC)

            def logit(n):
                i = LAST_HALF[n]
                if n == 0:
                    pe.wait_ge(rtw_in, 64)
                J.wait_free(pe, "logit", i)
                J.wait_emptied(pe, "h3T", i, 0)
                J.wait_emptied(pe, "h3T", i, 1)
                for k in range(KC):
                    ins = pe.matmul(J.bank("logit", i)[0:rows(i), 0:36], hT[:, k, tok(i)], wr[:, k, :], start=(k == 0), stop=(k == KC - 1))
                J.fills(ins, "logit", i)

            summed("x2", "xo", oT, "h3T", 12, lambda: mem_out_turned(1), ("XOsT", 1, 1), logit)
            J.wait_free(pe, "rank")
            pe.wait_ge(onehots, 1)
            ms = rt["ms"].rearrange("p (i n) -> p i n", i=5)
            s = J.bank("rank")
            pe.matmul(s[:, 0:NE * NT], before[:, :], ms[:, 0:NT, :], start=True, stop=True, skip_group_check=True)
            pe.matmul(s[:, NE * NT:NE * (NT + 1)], before[0:NS, :], ms[0:NS, NT, :], start=False, stop=True,
                      skip_group_check=True)
            for k, rr in TILES:
                ins = pe.matmul(s[:, NE * (k + 1):NE * (NT + 2)].rearrange("p (i n) -> p i n", n=NE), ones[0:rr, :],
                                ms[0:rr, k, :].unsqueeze(1).to_broadcast([rr, NT + 1 - k, NE]), start=False, stop=True,
                                skip_group_check=True)
            J.fills(ins, "rank")
            J.wait_free(pe, "table")
            pe.wait_ge(onehots, 2)
            ohs = rt["ohs"].rearrange("p (a n) -> p a n", n=NBLK)
            ohr = rt["ohr"].rearrange("p (a n) -> p a n", n=CAP)
            for k in range(2):
                for i, r in TILES:
                    for u in range(2):
                        ins = pe.matmul(J.bank("table")[CAP * u:CAP * (u + 1), 0:NBLK // 2], ohr[0:r, 5 * k + i, :],
                                        ohs[0:r, 5 * k + i, :].rearrange("p (c u) -> p u c", u=2)[:, u, :],
                                        start=(k == 0 and i == 0), stop=(k == 1 and i == NT), skip_group_check=True)
            J.fills(ins, "table")

            pe.wait_ge(routed, 1)

            def rows_turned(j):
                pe.wait_ge(xg_in, 16 * j + 16)
                for k in range(KC):
                    ins = pe.transpose(psum[k // 4][:, P * (k % 4):P * (k % 4 + 1)], xg[:, P * k:P * (k + 1)], ident[:, :])
                ins.then_inc(xt_full, 1)

            def up(j, c):
                u = c % 2
                if c == 0:
                    pe.wait_ge(xt_free, 2 * j + 2)
                if reused(j, c):
                    pe.wait_ge(up_free, 2 * j + (c - 1))
                for q in range(4):
                    for m in range(2):
                        if 2 * q + m < 4:
                            pe.wait_ge(moe_in(2 * q + m, u), 16 * j + 16)
                        else:
                            pe.wait_ge(wm_in[2 * q + m], 32 * j + 16 * (c + 1))
                        for kk in range(2):
                            k = 2 * q + kk
                            for half in range(2):
                                ins = pe.matmul(psum[2 + 2 * u + m][CAP * half:CAP * (half + 1), :],
                                                xT[:, k, CAP * u:CAP * (u + 1)],
                                                moe_place(2 * q + m, u)[:, kk, 512 * half:512 * (half + 1)],
                                                start=(k == 0), stop=(k == KC - 1), skip_group_check=True)
                        ins.then_inc(up_used, 1)

            def down(j, c):
                u = c % 2
                first = isinstance(j, int) and 2 * j + c == 0
                pe.wait_ge(up_free, 2 * j + (c + 1))
                if not first:
                    pe.wait_ge(ht_free, 2 * j + c)
                for n in range(4):
                    ins = pe.transpose(psum[6][:, P * n:P * (n + 1)], h2[u][:, P * n:P * (n + 1)], ident[:, :])
                ins.then_inc(ht_full, 1)
                pe.wait_ge(ht_free, 2 * j + (c + 1))
                if not first:
                    pe.wait_ge(y_free, 2 * j + c)
                for q in range(4):
                    pe.wait_ge(wm_in[8 + q], 32 * j + 16 * (c + 1))
                    for kk in range(2):
                        k = 2 * q + kk
                        for half in range(2):
                            ins = pe.matmul(psum[7][CAP * half:CAP * (half + 1), :],
                                            heT[u][:, k % 4, CAP * (k // 4):CAP * (k // 4 + 1)],
                                            ring[:, 8 + q, kk, 512 * half:512 * (half + 1)],
                                            start=(k == 0), stop=(k == KC - 1), skip_group_check=True)
                    ins.then_inc(down_used, 1)

            def pair(j):
                up(j, 0)
                down(j, -1)
                up(j, 1)
                rows_turned(j + 1)
                down(j, 0)

            rows_turned(0)
            up(0, 0)
            up(0, 1)
            rows_turned(1)
            down(0, 0)
            with pe.Fori(1, NE // 2 - 1) as j:
                pair(j)
            up(NE // 2 - 1, 0)
            down(NE // 2 - 1, -1)
            up(NE // 2 - 1, 1)
            down(NE // 2 - 1, 0)
            down(NE // 2 - 1, 1)
            n_ov = pe.value_load(ovi[0:1, 0:1], min_val=0, max_val=XBLK)
            with pe.If(n_ov > 0):
                with pe.Fori(NE // 2, NBLK // 2) as j:
                    with pe.If(2 * j - NE < n_ov):
                        rows_turned(j)
                        for u in range(2):
                            up(j, u)
                            down(j, u)


INS = ["x_prompt", "x_sample", "state_hgrn", "cache_moba_k", "cache_moba_v", "cache_mem_k", "cache_mem_v", "page_table",
       "mem_prompt", "g_mix", "w_in", "hg_lb", "hg_norm", "w_out", "g_cross", "g_mem", "w_xq", "w_xk", "w_xv", "w_xo",
       "g_ffn", "w_grp", "b_grp", "w_exp", "b_exp", "w1", "w3", "w2", "g_final"]


def kernel(**inputs):
    import concourse.bacc as bacc
    from concourse.bass_utils import run_bass_kernel_spmd

    nc = bacc.Bacc("TRN2", target_bir_lowering=False, num_devices=1)
    arrays = {name: np.ascontiguousarray(inputs[name]) for name in INS}
    arrays["g_final"] = arrays["g_final"].reshape(1, D)
    arrays.update(constants())
    aps = {name: nc.dram_tensor(name, x.shape, mybir.dt.from_np(x.dtype), kind="ExternalInput").ap()
           for name, x in arrays.items()}
    for name, shape in OUTS:
        aps[name] = nc.dram_tensor(name, shape, F32, kind="ExternalOutput").ap()
    step_kernel(nc, aps)
    r = run_bass_kernel_spmd(nc, [arrays], core_ids=[0])
    return tuple(r.results[0][name] for name, _ in OUTS)
```
